# Optimizing a Trainium2 kernel written in Bass

```python
import jax, jax.numpy as jnp
from jax import lax
import numpy as np

D_MODEL = 1024
BATCH = 1
SEQ = 256
DEPTH = 2

CTX_LEN = 256
GRID_W = 64
EPS = 1e-6
NA_HEADS = 8
NA_HEAD_DIM = 64
NA_WIDTH = NA_HEADS * NA_HEAD_DIM
NA_WIN_ROWS = 8
NA_WIN_COLS = 16
ROPE_THETA = 10000.0
ROT_HALF = NA_HEAD_DIM // 2
HG_HEADS = 4
HG_KEY_DIM = 128
HG_VAL_DIM = 128
HG_KEY_WIDTH = HG_HEADS * HG_KEY_DIM
HG_VAL_WIDTH = HG_HEADS * HG_VAL_DIM
HG_CHUNK = 64
GATE_FLOOR = 1e-30
IN_WIDTH = 3 * NA_WIDTH + 3 * HG_KEY_WIDTH + 2 * HG_VAL_WIDTH + 2 * D_MODEL
N_EXPERTS = 16
N_GROUPS = 4
EXPERTS_PER_GROUP = N_EXPERTS // N_GROUPS
TOP_K = 2
EXPERT_FF = 512
MASK_VALUE = -1e9

kernel_name = "hybrid_na_hgrn2_grouped_moe_dit"

def rms_norm(x, g):
    xf = x.astype(jnp.float32)
    y = xf * lax.rsqrt(jnp.mean(xf * xf, axis=-1, keepdims=True) + EPS)
    return (y * g.astype(jnp.float32)).astype(x.dtype)

def modulate(h, shift, scale):
    return h * (1 + scale) + shift

def to_heads(t, n):
    B, L, _ = t.shape
    return t.reshape(B, L, n, -1).transpose(0, 2, 1, 3)

def from_heads(t):
    B, H, L, d = t.shape
    return t.transpose(0, 2, 1, 3).reshape(B, L, H * d)

def split_columns(p):
    widths = (NA_WIDTH,) * 3 + (HG_KEY_WIDTH,) * 3 + (HG_VAL_WIDTH,) * 2 + (D_MODEL,) * 2
    offs = np.cumsum(widths)[:-1].tolist()
    return jnp.split(p, offs, axis=-1)

def axial_rope(L):
    t = jnp.arange(L, dtype=jnp.int32)
    row = (t // GRID_W).astype(jnp.float32)
    col = (t % GRID_W).astype(jnp.float32)
    inv = ROPE_THETA ** (-jnp.arange(0, ROT_HALF, 2, dtype=jnp.float32) / ROT_HALF)
    ang = jnp.concatenate([row[:, None] * inv, col[:, None] * inv], axis=-1)
    return jnp.cos(ang), jnp.sin(ang)

def apply_rope(x, cos, sin):
    xp = x.astype(jnp.float32).reshape(*x.shape[:-1], NA_HEAD_DIM // 2, 2)
    x1, x2 = xp[..., 0], xp[..., 1]
    out = jnp.stack([x1 * cos - x2 * sin, x1 * sin + x2 * cos], axis=-1)
    return out.reshape(x.shape).astype(x.dtype)

def na_indices(rows):
    wr = min(NA_WIN_ROWS, rows)
    L = rows * GRID_W
    t = jnp.arange(L, dtype=jnp.int32)
    r, col = t // GRID_W, t % GRID_W
    rs = jnp.clip(r - wr // 2, 0, rows - wr)
    cs = jnp.clip(col - NA_WIN_COLS // 2, 0, GRID_W - NA_WIN_COLS)
    kr = rs[:, None, None] + jnp.arange(wr, dtype=jnp.int32)[None, :, None]
    kc = cs[:, None, None] + jnp.arange(NA_WIN_COLS, dtype=jnp.int32)[None, None, :]
    full = (L, wr, NA_WIN_COLS)
    shape = (rows, GRID_W, wr * NA_WIN_COLS)
    idx = jnp.broadcast_to(kr * GRID_W + kc, full).reshape(shape)
    dr = jnp.broadcast_to(kr - r[:, None, None] + NA_WIN_ROWS - 1, full).reshape(shape)
    dc = jnp.broadcast_to(kc - col[:, None, None] + NA_WIN_COLS - 1, full).reshape(shape)
    return idx, dr, dc

def neighbourhood_attention(q_l, k_l, v_l, k_c, v_c, rel_bias, rows):
    B, H, L, dh = q_l.shape
    idx, dr, dc = na_indices(rows)
    scale = dh ** -0.5
    q_blocks = jnp.moveaxis(q_l.reshape(B, H, rows, GRID_W, dh), 2, 0)

    def block(args):
        q_b, idx_b, dr_b, dc_b = args
        k_g = k_l[:, :, idx_b]
        v_g = v_l[:, :, idx_b]
        s_win = jnp.einsum('bhqd,bhqkd->bhqk', q_b, k_g).astype(jnp.float32) * scale \
            + rel_bias[:, dr_b, dc_b].astype(jnp.float32)[None]
        s_ctx = jnp.einsum('bhqd,bhkd->bhqk', q_b, k_c).astype(jnp.float32) * scale
        p = jax.nn.softmax(jnp.concatenate([s_win, s_ctx], axis=-1), axis=-1).astype(v_l.dtype)
        nk = idx_b.shape[-1]
        return jnp.einsum('bhqk,bhqkd->bhqd', p[..., :nk], v_g) + jnp.einsum('bhqk,bhkd->bhqd', p[..., nk:], v_c)

    o = lax.map(block, (q_blocks, idx, dr, dc))
    return jnp.moveaxis(o, 0, 2).reshape(B, H, L, dh)

def context_attention(q_c, k_c, v_c):
    s = jnp.einsum('bhqd,bhkd->bhqk', q_c, k_c).astype(jnp.float32) * (q_c.shape[-1] ** -0.5)
    p = jax.nn.softmax(s, axis=-1).astype(v_c.dtype)
    return jnp.einsum('bhqk,bhkd->bhqd', p, v_c)

def layer_lower_bounds(raw):
    p = jax.nn.softmax(raw.astype(jnp.float32), axis=0)
    return jnp.cumsum(p, axis=0) - p[0:1]

def hgrn2_gates(f, lb):
    lb = lb.astype(jnp.float32).reshape(HG_HEADS, 1, HG_KEY_DIM)
    f = f.astype(jnp.float32)
    g = lb + (1 - lb) * jax.nn.sigmoid(f)
    log_g = jnp.log(jnp.maximum(g, GATE_FLOOR))
    k = (1 - lb) * jax.nn.sigmoid(-f)
    return k, log_g

def gla_chunked(q, k, v, log_g, s0):
    B, H, L, dk = q.shape
    n = L // HG_CHUNK
    out_dtype = v.dtype

    def chunks(t):
        return jnp.moveaxis(t.astype(jnp.float32).reshape(B, H, n, HG_CHUNK, t.shape[-1]), 2, 0)

    incl = jnp.tril(jnp.ones((HG_CHUNK, HG_CHUNK), dtype=bool))[..., None]

    def step(S, xs):
        qc, kc, vc, gc = xs
        b = jnp.cumsum(gc, axis=2)
        diff = b[:, :, :, None, :] - b[:, :, None, :, :]
        decay = jnp.where(incl, jnp.exp(jnp.where(incl, diff, 0.0)), 0.0)
        A = jnp.einsum('bhtsk,bhsk->bhts', decay * qc[:, :, :, None, :], kc)
        o = jnp.einsum('bhts,bhsv->bhtv', A, vc) + jnp.einsum('bhtk,bhkv->bhtv', qc * jnp.exp(b), S)
        b_last = b[:, :, -1:, :]
        S_new = jnp.exp(b_last[:, :, 0, :])[..., None] * S \
            + jnp.einsum('bhsk,bhsv->bhkv', kc * jnp.exp(b_last - b), vc)
        return S_new, o

    s_fin, o = lax.scan(step, s0, (chunks(q), chunks(k), chunks(v), chunks(log_g)))
    o = jnp.moveaxis(o, 0, 2).reshape(B, H, L, v.shape[-1])
    return o.astype(out_dtype), s_fin

def hgrn2_bidirectional(q_l, i_l, q_c, i_c, dirs):
    B = q_l.shape[0]
    o_lat, o_ctx = [], []
    for f_l, f_c, lb, flip in dirs:
        rev = (lambda t: t[:, :, ::-1]) if flip else (lambda t: t)
        k_c, lg_c = hgrn2_gates(f_c, lb)
        k_l, lg_l = hgrn2_gates(f_l, lb)
        s0 = jnp.zeros((B, HG_HEADS, HG_KEY_DIM, HG_VAL_DIM), jnp.float32)
        oc, s_ctx = gla_chunked(rev(q_c), rev(k_c), rev(i_c), rev(lg_c), s0)
        ol, _ = gla_chunked(rev(q_l), rev(k_l), rev(i_l), rev(lg_l), s_ctx)
        o_lat.append(rev(ol))
        o_ctx.append(rev(oc))
    return o_lat[0] + o_lat[1], o_ctx[0] + o_ctx[1]

def gated_head_norm(o, gate, gain):
    return from_heads(rms_norm(o, gain)) * jax.nn.silu(gate)

def merge_branches(o_na, o_hg, hg_gate, gate_na, gate_hg, hg_gain, w_na_o, w_hg_o, w_out):
    y_na = from_heads(o_na) @ w_na_o
    y_hg = gated_head_norm(o_hg, hg_gate, hg_gain) @ w_hg_o
    return (jax.nn.sigmoid(gate_na) * y_na + jax.nn.sigmoid(gate_hg) * y_hg) @ w_out

def parallel_mixer(h_lat, h_ctx, w_in, rel_bias, lb_f, lb_b, hg_gain, w_na_o, w_hg_o, w_out, with_ctx_out):
    B, L, _ = h_lat.shape
    rows = L // GRID_W
    (na_q_l, na_k_l, na_v_l, hq_l, hf_l, hb_l, hi_l, hg_l, ga_l, gh_l) = split_columns(h_lat @ w_in)
    (na_q_c, na_k_c, na_v_c, hq_c, hf_c, hb_c, hi_c, hg_c, ga_c, gh_c) = split_columns(h_ctx @ w_in)
    cos, sin = axial_rope(L)
    q_l = apply_rope(to_heads(na_q_l, NA_HEADS), cos, sin)
    k_l = apply_rope(to_heads(na_k_l, NA_HEADS), cos, sin)
    v_l = to_heads(na_v_l, NA_HEADS)
    k_c = to_heads(na_k_c, NA_HEADS)
    v_c = to_heads(na_v_c, NA_HEADS)
    o_na_l = neighbourhood_attention(q_l, k_l, v_l, k_c, v_c, rel_bias, rows)
    dirs = ((to_heads(hf_l, HG_HEADS), to_heads(hf_c, HG_HEADS), lb_f, False),
            (to_heads(hb_l, HG_HEADS), to_heads(hb_c, HG_HEADS), lb_b, True))
    o_hg_l, o_hg_c = hgrn2_bidirectional(to_heads(jax.nn.silu(hq_l), HG_HEADS), to_heads(hi_l, HG_HEADS),
                                         to_heads(jax.nn.silu(hq_c), HG_HEADS), to_heads(hi_c, HG_HEADS), dirs)
    y_l = merge_branches(o_na_l, o_hg_l, hg_l, ga_l, gh_l, hg_gain, w_na_o, w_hg_o, w_out)
    if not with_ctx_out:
        return y_l, None
    o_na_c = context_attention(to_heads(na_q_c, NA_HEADS), k_c, v_c)
    y_c = merge_branches(o_na_c, o_hg_c, hg_c, ga_c, gh_c, hg_gain, w_na_o, w_hg_o, w_out)
    return y_l, y_c

def grouped_moe(h, w_router, router_bias, w_gate, w_up, w_down):
    shp = h.shape
    t = h.reshape(-1, shp[-1])
    scores = jax.nn.sigmoid((t @ w_router).astype(jnp.float32))
    grouped = (scores + router_bias.astype(jnp.float32)).reshape(-1, N_GROUPS, EXPERTS_PER_GROUP)
    group_score = lax.top_k(grouped, TOP_K)[0].sum(-1)
    g_sel = jnp.argmax(group_score, axis=-1)
    in_group = (jnp.arange(N_GROUPS) == g_sel[:, None])[..., None]
    cand = jnp.where(in_group, grouped, MASK_VALUE).reshape(-1, N_EXPERTS)
    _, e_idx = lax.top_k(cand, TOP_K)
    w = jnp.take_along_axis(scores, e_idx, axis=-1)
    w = w / jnp.sum(w, axis=-1, keepdims=True)
    combine = jnp.sum(jax.nn.one_hot(e_idx, N_EXPERTS, dtype=jnp.float32) * w[..., None], axis=1).astype(t.dtype)
    out = jnp.zeros_like(t)
    for e in range(N_EXPERTS):
        h_e = jax.nn.silu(t @ w_gate[e]) * (t @ w_up[e])
        out = out + combine[:, e:e + 1] * (h_e @ w_down[e])
    return out.reshape(shp)

def setup_inputs(seed: int = 0) -> dict:
    key = jax.random.key(seed)
    ks = jax.random.split(key, 24)
    D = D_MODEL

    def nrm(k, shape, scale):
        return jax.random.normal(k, shape, jnp.float32) * scale

    return {
        'x': nrm(ks[0], (BATCH, SEQ, D), 1.0),
        'c': nrm(ks[1], (BATCH, D), 1.0),
        'ctx': nrm(ks[2], (BATCH, CTX_LEN, D), 1.0),
        'c_ctx': nrm(ks[3], (D,), 1.0),
        'w_ada': nrm(ks[4], (DEPTH, D, 6 * D), 0.5 * D ** -0.5),
        'b_ada': nrm(ks[5], (DEPTH, 6 * D), 0.02),
        'norm1_g': 1.0 + nrm(ks[6], (DEPTH, D), 0.02),
        'w_in': nrm(ks[7], (DEPTH, D, IN_WIDTH), D ** -0.5),
        'na_rel_bias': nrm(ks[8], (DEPTH, NA_HEADS, 2 * NA_WIN_ROWS - 1, 2 * NA_WIN_COLS - 1), 0.1),
        'hg_lower_fwd': nrm(ks[9], (DEPTH, HG_KEY_WIDTH), 0.1),
        'hg_lower_bwd': nrm(ks[10], (DEPTH, HG_KEY_WIDTH), 0.1),
        'hg_norm_g': 1.0 + nrm(ks[11], (DEPTH, HG_VAL_DIM), 0.02),
        'w_na_o': nrm(ks[12], (DEPTH, NA_WIDTH, D), NA_WIDTH ** -0.5),
        'w_hg_o': nrm(ks[13], (DEPTH, HG_VAL_WIDTH, D), HG_VAL_WIDTH ** -0.5),
        'w_out': nrm(ks[14], (DEPTH, D, D), D ** -0.5),
        'norm2_g': 1.0 + nrm(ks[15], (DEPTH, D), 0.02),
        'w_router': nrm(ks[16], (D, N_EXPERTS), D ** -0.5),
        'router_bias': nrm(ks[17], (N_EXPERTS,), 0.01),
        'w_gate': nrm(ks[18], (DEPTH, N_EXPERTS, D, EXPERT_FF), D ** -0.5),
        'w_up': nrm(ks[19], (DEPTH, N_EXPERTS, D, EXPERT_FF), D ** -0.5),
        'w_down': nrm(ks[20], (DEPTH, N_EXPERTS, EXPERT_FF, D), EXPERT_FF ** -0.5),
        'final_g': 1.0 + nrm(ks[21], (D,), 0.02),
    }

def reference(x, c, ctx, c_ctx, w_ada, b_ada, norm1_g, w_in, na_rel_bias, hg_lower_fwd, hg_lower_bwd,
              hg_norm_g, w_na_o, w_hg_o, w_out, norm2_g, w_router, router_bias, w_gate, w_up, w_down, final_g):
    n_ctx = ctx.shape[1]
    lb_f = layer_lower_bounds(hg_lower_fwd)
    lb_b = layer_lower_bounds(hg_lower_bwd)
    for l in range(DEPTH):
        last = l == DEPTH - 1
        sh1, sc1, g1, sh2, sc2, g2 = [m[:, None, :] for m in jnp.split(jax.nn.silu(c) @ w_ada[l] + b_ada[l], 6, axis=-1)]
        csh1, csc1, cg1, csh2, csc2, cg2 = jnp.split(jax.nn.silu(c_ctx) @ w_ada[l] + b_ada[l], 6, axis=-1)
        h_lat = modulate(rms_norm(x, norm1_g[l]), sh1, sc1)
        h_ctx = modulate(rms_norm(ctx, norm1_g[l]), csh1, csc1)
        y_lat, y_ctx = parallel_mixer(h_lat, h_ctx, w_in[l], na_rel_bias[l], lb_f[l], lb_b[l], hg_norm_g[l],
                                      w_na_o[l], w_hg_o[l], w_out[l], with_ctx_out=not last)
        x = x + g1 * y_lat
        h2_lat = modulate(rms_norm(x, norm2_g[l]), sh2, sc2)
        if last:
            x = x + g2 * grouped_moe(h2_lat, w_router, router_bias, w_gate[l], w_up[l], w_down[l])
        else:
            ctx = ctx + cg1 * y_ctx
            h2_ctx = modulate(rms_norm(ctx, norm2_g[l]), csh2, csc2)
            f = grouped_moe(jnp.concatenate([h2_ctx, h2_lat], axis=1), w_router, router_bias,
                            w_gate[l], w_up[l], w_down[l])
            ctx = ctx + cg2 * f[:, :n_ctx]
            x = x + g2 * f[:, n_ctx:]
    return rms_norm(x, final_g)


_drawn_inputs = setup_inputs


def setup_inputs(seed=0):
    import zlib

    import numpy as np

    out = dict(_drawn_inputs(seed))
    spreads = {}
    factors = {'norm1_g': 3.862,
     'na_rel_bias': 6.673,
     'hg_lower_fwd': 5.843,
     'hg_lower_bwd': 8.0,
     'hg_norm_g': 4.19,
     'final_g': 7.61,
     'norm2_g': 3.032}
    for name, (base, spread) in spreads.items():
        noise = np.random.default_rng([zlib.crc32(name.encode()), seed]).standard_normal(out[name].shape)
        drawn = base * np.exp(spread * noise) if base else spread * noise
        out[name] = __import__('jax').numpy.asarray(drawn.astype(out[name].dtype))
    for name, factor in factors.items():
        out[name] = (out[name] * factor).astype(out[name].dtype)
    return out
```

```python
import numpy as np
import concourse.bass as bass
from concourse import mybir
from contextlib import ExitStack

D = 1024
SEG = 256
TOK = 2 * SEG
DEPTH = 2
P = 128
KT = D // P
GRID_W = 64
WIN_COLS = 16
NA_HEADS = 8
NA_DIM = 64
HG_HEADS = 4
EPS = 1e-6
N_EXPERTS = 16
N_GROUPS = 4
PER_GROUP = N_EXPERTS // N_GROUPS
FF = 512
SLOTS = 4
SLOT = 4096
LEVELS = 7
GATE_FLOOR = 1e-30
MASKED = -1e30

VEC_BADA = 0
VEC_N1 = VEC_BADA + DEPTH * 48
VEC_N2 = VEC_N1 + DEPTH * KT
VEC_FINAL = VEC_N2 + DEPTH * KT
VEC_LOWER = VEC_FINAL + KT
VEC_HGAIN = VEC_LOWER + 2 * DEPTH * HG_HEADS
VEC_COND = VEC_HGAIN + DEPTH
VEC_RBIAS = VEC_COND + 2 * KT
VEC_GIDX = VEC_RBIAS + N_EXPERTS
VEC_N = VEC_GIDX + 4
C_IDENT, C_ONES, C_ROT, C_COS, C_SIN, C_WMUL, C_WNEG = 0, 128, 256, 384, 640, 896, 960
C_N = 1024


def build(nc, A, out, stop=99):
    f32, u8 = mybir.dt.float32, mybir.dt.uint8
    ALU, ACT, AX = mybir.AluOpType, mybir.ActivationFunctionType, mybir.AxisListType
    V, S, G, T = nc.vector, nc.scalar, nc.gpsimd, nc.tensor

    at = [(nc.sbuf_base + 31) // 32 * 32]

    def fixed(name, shape, dtype=f32, offset=None):
        size = int(np.prod(shape[1:])) * (1 if dtype == u8 else 4)
        where = at[0] if offset is None else offset
        if offset is None:
            at[0] += (size + 31) // 32 * 32
        return nc.alloc_sbuf_tensor_at(name, shape, dtype, offset=where)

    xT = fixed("xT", [P, KT, TOK])
    hT = fixed("hT", [P, KT, TOK])
    ring = fixed("ring", [P, SLOTS, SLOT])
    const = fixed("const", [P, C_N])
    levmask = fixed("levmask", [P, 2 * LEVELS, P], u8)
    vec = fixed("vec", [P, VEC_N])
    router = fixed("router", [P, KT, N_EXPERTS])
    cond = fixed("cond", [P, KT, 2])
    mod = fixed("mod", [P, DEPTH, 48, 2])
    gain1 = fixed("gain1", [P, DEPTH, KT, 2])
    gain2 = fixed("gain2", [P, DEPTH, KT, 2])
    lower = fixed("lower", [P, 2, DEPTH, HG_HEADS])
    upper = fixed("upper", [P, 2, DEPTH, HG_HEADS])
    lowtmp = fixed("lowtmp", [P, 8, 2, HG_HEADS])
    credit = fixed("credit", [P, 2 * DEPTH])
    epsv = fixed("epsv", [P, 1])
    adarow = fixed("adarow", [2, 2, 512])
    square = fixed("square", [P, 2, TOK])
    rstd = fixed("rstd", [P, TOK])
    normed = fixed("normed", [P, 2, TOK])
    narow = fixed("narow", [P, 3, 4])
    ident = const[:, C_IDENT:C_IDENT + P]
    ones = const[:, C_ONES:C_ONES + P]
    rot = const[:, C_ROT:C_ROT + P]
    cos = const[:, C_COS:C_COS + SEG]
    sin = const[:, C_SIN:C_SIN + SEG]
    wmul = const[:, C_WMUL:C_WMUL + GRID_W]
    wneg = const[:, C_WNEG:C_WNEG + GRID_W]

    A0 = at[0]
    KB = 1024
    qh = fixed("qh", [P, 8, SEG], offset=A0)
    kf = fixed("kf", [P, 8, SEG], offset=A0 + 8 * KB)
    kb = fixed("kb", [P, 8, SEG], offset=A0 + 16 * KB)
    pf = fixed("pf", [P, 8, SEG + 1], offset=A0 + 24 * KB)
    pb = fixed("pb", [P, 8, SEG + 1], offset=A0 + 24 * KB + 8224)
    vh = fixed("vh", [P, 4, 512], offset=A0 + 24 * KB + 2 * 8224)
    B0 = A0 + 32 * KB + 2 * 8224
    att = fixed("att", [P, HG_HEADS, 2, 2, SEG], offset=B0)
    attx = fixed("attx", [P, HG_HEADS, 2, SEG], offset=B0 + 16 * KB)
    dec = [fixed(f"dec{i}", [P, 4, SEG], offset=B0 + 24 * KB + i * 4 * KB) for i in range(2)]
    fac = [fixed(f"fac{i}", [P, 4, SEG], offset=B0 + 32 * KB + i * 4 * KB) for i in range(2)]
    C0 = B0 + 40 * KB
    naq = fixed("naq", [P, 4, TOK], offset=C0)
    nak = fixed("nak", [P, 4, TOK], offset=C0 + 8 * KB)
    roped = fixed("roped", [P, 2, SEG], offset=A0 + 24 * KB + 2 * 8224)
    END = C0 + 16 * KB
    assert END <= nc.sbuf_usable_end, (END, nc.sbuf_usable_end)
    sig = fixed("sig", [P, 8 * SEG], offset=B0 + 24 * KB)
    small = fixed("small", [P, 8 * SEG], offset=B0 + 32 * KB)
    logs = fixed("logs", [P, 8 * SEG], offset=B0)
    onescan = fixed("onescan", [P, SEG], offset=B0 + 8 * KB)
    oh = fixed("oh", [P, HG_HEADS, TOK], offset=A0 + 8 * KB)
    hgate = fixed("hgate", [P, HG_HEADS, TOK], offset=A0 + 16 * KB)
    navv = fixed("navv", [P, 4, 512], offset=A0)
    ona = fixed("ona", [P, 4, TOK], offset=A0 + 24 * KB)
    pt = [fixed(f"pt{i}", [P, 4, SEG], offset=A0 + 32 * KB + 4 * KB * i) for i in range(2)]
    bias = fixed("bias", [P, NA_HEADS, 2, 4 * GRID_W], offset=B0 + 24 * KB)
    levmask_f = fixed("levmask_f", [P, 2 * LEVELS, P], offset=A0)
    bias_skew = fixed("bias_skew", [P, NA_HEADS, 2, 4 * GRID_W], offset=B0)
    probs = [fixed(f"probs{i}", [P, TOK], offset=B0 + 16 * KB + 2 * KB * i) for i in range(3)]
    osq = fixed("osq", [P, 2, TOK], offset=C0)
    ors = fixed("ors", [P, 2, TOK], offset=C0 + 4 * KB)
    merged = fixed("merged", [P, KT, TOK], offset=B0)
    gsig = fixed("gsig", [P, 2, TOK], offset=C0 + 8 * KB)
    gmul = fixed("gmul", [P, 2, TOK], offset=C0 + 12 * KB)
    combb = fixed("combb", [P, N_EXPERTS, TOK], offset=A0)
    acts = fixed("acts", [P, 2, 4, TOK], offset=A0 + 32 * KB)
    silu = fixed("silu", [P, 4, TOK], offset=A0 + 48 * KB)
    R0 = A0 + 56 * KB
    rt = [fixed(f"rt{i}", [P, 4, N_GROUPS, PER_GROUP], offset=R0 + 256 * i) for i in range(12)]
    combw = fixed("combw", [P, 4, N_EXPERTS, P], offset=R0 + 4 * KB)
    assert R0 + 36 * KB + 256 <= END + 4 * KB

    names = """const_loaded vec_loaded x_loaded bias_loaded out_stored psum_ready cond_ready ada_row ada_mod
        epsv_ready gains_ready lower_ready square_ready square_used norm_std rstd_ready normed_ready h_ready q_ready
        sig_ready k_sig gates_ready log_in log_out v_ready naqk_ready rope_done decay_in decay_out fac_ready
        att_block oh_ready osq_ready hg_std og_ready hgate_ready nav_ready bias_ready na_z na_max na_p na_pn
        na_pt na_o silu_scaled gate_sig merged_ready x_updated route_done comb_col comb_bcast silu_ready act_ready
        down_done dve_chain act_chain pool_chain pool_ready""".split()
    with ExitStack() as ctx:
        sem = {n: ctx.enter_context(nc.semaphore(n)) for n in names}
        slot_full = [ctx.enter_context(nc.semaphore(f"slot_full{i}")) for i in range(SLOTS)]
        bank = [ctx.enter_context(nc.psum_tensor(f"bank{i}", [P, 512], f32)) for i in range(8)]
        block = ctx.enter_context(nc.Block())

        loads = []

        def slot_of(key):
            return loads.index(key)

        for l in range(DEPTH):
            loads += [("ada", l, s) for s in range(12)]
        for l in range(DEPTH):
            loads += [("in", l, s) for s in (3, 4, 5, 6, 0, 1, 2, 7)]
            loads += [("nao", l), ("in", l, 8), ("in", l, 9), ("hgo", l), ("in", l, 10), ("in", l, 11)]
            loads += [("out", l, 0), ("out", l, 1)]
            assert len(loads) % SLOTS == 0
            loads += [("moe", l, e, k) for e in range(N_EXPERTS) for k in range(3)]

        def slot(key):
            return ring[:, slot_of(key) % SLOTS, :]

        def full(key):
            n = slot_of(key)
            return slot_full[n % SLOTS], 16 * (n // SLOTS + 1)

        ready, reader, last_use, spent = {}, {}, {}, {}
        in_bank = [None] * 8
        counts = {}
        slot_spent = {}
        jobs = [0]

        def read_by(key):
            return sem[reader[key][0]], reader[key][1]

        def is_ready(key):
            return sem["psum_ready"], ready[key][1]

        def result(key):
            return bank[ready[key][0]]

        segs_of = {0: (0, 1), 1: (1,)}

        def expert_spent(m):
            return 16 * (m // 3) + (7, 8, 16)[m % 3]

        def moe_down0(l):
            return 8 * (N_EXPERTS + 1) * l + 8

        def acts0(l):
            return 4 * (N_EXPERTS + 1) * l + 4


        @block.tensor
        def _(pe):
            def open_bank(key, who):
                b = jobs[0] % 8
                jobs[0] += 1
                if in_bank[b] is not None:
                    pe.wait_ge(*read_by(in_bank[b]))
                in_bank[b] = key
                counts[who] = counts.get(who, 0) + 1
                ready[key] = (b, jobs[0])
                reader[key] = (who, counts[who])
                return bank[b]

            pe.wait_ge(sem["const_loaded"], 16)
            pe.wait_ge(sem["cond_ready"], 1)

            def ada_rows(l, s):
                pe.wait_ge(*full(("ada", l, s)))
                w = slot(("ada", l, s)).rearrange("p (k n) -> p k n", k=KT)
                o = open_bank(("ada", l, s), "ada_row")
                for k in range(KT):
                    mm = T.matmul(o[0:2, :], cond[:, k, :], w[:, k, :], start=(k == 0), stop=(k == KT - 1))
                mm.then_inc(sem["psum_ready"], 1)
                slot_spent[slot_of(("ada", l, s))] = jobs[0]

            def ada_turn(l, s):
                o = open_bank(("adaT", l, s), "ada_mod")
                pe.wait_ge(*read_by(("ada", l, s)))
                n = (l * 12 + s) % 2
                for j in range(4):
                    mm = T.transpose(o[:, 2 * j:2 * j + 2], adarow[:, n, j * P:(j + 1) * P], ident[0:2, 0:2])
                mm.then_inc(sem["psum_ready"], 1)

            for n in range(DEPTH * 12 + 1):
                if n < DEPTH * 12:
                    ada_rows(n // 12, n % 12)
                if n:
                    ada_turn((n - 1) // 12, (n - 1) % 12)

            def mean_square(key, count, lo):
                o = open_bank(key, "norm_std")
                for k in range(KT):
                    pe.wait_ge(sem["square_ready"], count * KT + k + 1)
                    mm = T.matmul(o[:, lo:TOK], ones, square[:, k % 2, lo:TOK], start=(k == 0), stop=(k == KT - 1))
                    if k < KT - 1:
                        mm.then_inc(sem["square_used"], 1)
                mm.then_inc(sem["psum_ready"], 1)

            def project(l, s, c, who, lo):
                w = slot(("in", l, s)).rearrange("p (k n) -> p k n", k=KT)
                o = open_bank(("in", l, s, c), who)
                for k in range(KT):
                    mm = T.matmul(o[:, lo:TOK], w[:, k, c * P:(c + 1) * P], hT[:, k, lo:TOK],
                                  start=(k == 0), stop=(k == KT - 1))
                mm.then_inc(sem["psum_ready"], 1)
                if c == 3:
                    slot_spent[slot_of(("in", l, s))] = jobs[0]

            def project_rows(l, s, t, who):
                w = slot(("in", l, s)).rearrange("p (k n) -> p k n", k=KT)
                o = open_bank(("in", l, s, t), who)
                for k in range(KT):
                    mm = T.matmul(o[:, :], hT[:, k, t * P:(t + 1) * P], w[:, k, :], start=(k == 0), stop=(k == KT - 1))
                mm.then_inc(sem["psum_ready"], 1)
                if t == 3:
                    slot_spent[slot_of(("in", l, s))] = jobs[0]

            units_before = [0]
            rounds = {"norm": 0, "square_used": 0}
            for l in range(DEPTH):
                if stop <= 10 * l + 1:
                    break
                lo = 0 if l == 0 else SEG
                segs = segs_of[l]
                mean_square(("ms", l, 0), 2 * l, 0)
                pe.wait_ge(sem["h_ready"], KT * (2 * l + 1))
                for s, who in ((3, "q_ready"), (4, "k_sig"), (5, "k_sig")):
                    pe.wait_ge(*full(("in", l, s)))
                    for c in range(4):
                        project(l, s, c, who, lo if s == 3 else 0)
                pe.wait_ge(*full(("in", l, 6)))
                for t in range(4):
                    project_rows(l, 6, t, "v_ready")
                if stop <= 10 * l + 2:
                    break

                extra = [(s, c) for s in (0, 1) for c in range(4)]

                def between():
                    if not extra:
                        return
                    s, c = extra.pop(0)
                    if c == 0:
                        pe.wait_ge(*full(("in", l, s)))
                    project(l, s, c, "naqk_ready", lo if s == 0 else 0)

                u = 38 * l
                for hp in range(2):
                    for unit in range(19):
                        pe.wait_ge(sem["fac_ready"], u + 1)
                        f = fac[u % 2]
                        lev, way = (unit - 1) // 2, (unit - 1) % 2
                        if lev < LEVELS:
                            for h in range(2):
                                o = open_bank(("lev", l, u, h), "att_block")
                                for i, sg in enumerate(segs):
                                    for b in range(2):
                                        left = f[:, h * len(segs) + i, b * P:(b + 1) * P]
                                        right = qh[:, 2 * (2 * hp + h) + sg, b * P:(b + 1) * P] if unit == 0 else left
                                        mm = T.matmul(o[:, (2 * i + b) * P:(2 * i + b + 1) * P], left, right,
                                                      start=True, stop=True)
                                mm.then_inc(sem["psum_ready"], 1)
                        elif lev == LEVELS:
                            o = open_bank(("lev", l, u, 0), "att_block")
                            for h in range(2):
                                for i in range(len(segs)):
                                    j = h * len(segs) + i
                                    halves = f[:, j, 0:P], f[:, j, P:SEG]
                                    mm = T.matmul(o[:, j * P:(j + 1) * P], halves[way], halves[1 - way],
                                                  start=True, stop=True)
                            mm.then_inc(sem["psum_ready"], 1)
                        elif way == 1:
                            g = fac[(u - 1) % 2]
                            for h in range(2):
                                o = open_bank(("cross", l, hp, h), "att_block")
                                for sb in range(2):
                                    for n, x in enumerate((g, f)):
                                        mm = T.matmul(o[:, sb * SEG:(sb + 1) * SEG], x[:, 2 * h, sb * P:(sb + 1) * P],
                                                      x[:, 2 * h + 1, :], start=(n == 0), stop=(n == 1))
                                mm.then_inc(sem["psum_ready"], 1)
                        spent[u] = jobs[0]
                        if lev > LEVELS and way == 1:
                            spent[u - 1] = jobs[0]
                        u += 1
                        if unit % 4 == 3:
                            between()
                while extra:
                    between()

                pe.wait_ge(*read_by(("cross", l, 1, 1)))
                for h in range(HG_HEADS):
                    o = open_bank(("o", l, h), "oh_ready")
                    for sg in segs:
                        terms = [(2 * sg + sb, att[:, h, sg, sb, :]) for sb in range(2)]
                        if sg == 1:
                            terms = [(sb, attx[:, h, sb, :]) for sb in range(2)] + terms
                        for n, (t, a) in enumerate(terms):
                            mm = T.matmul(o[:, sg * SEG:(sg + 1) * SEG], vh[:, t, h * P:(h + 1) * P], a,
                                          start=(n == 0), stop=(n == len(terms) - 1))
                    mm.then_inc(sem["psum_ready"], 1)
                if stop <= 10 * l + 3:
                    break

                pe.wait_ge(*full(("in", l, 2)))
                for t in range(4):
                    project_rows(l, 2, t, "nav_ready")
                for n in range(8):
                    buf = (naq, nak)[n // 4]
                    o = open_bank(("rot", l, n), "rope_done")
                    pe.wait_ge(sem["naqk_ready"], 8 * l + n + 1)
                    T.matmul(o[:, 0:SEG], rot, buf[:, n % 4, SEG:TOK], start=True, stop=True)\
                        .then_inc(sem["psum_ready"], 1)
                pe.wait_ge(*full(("in", l, 7)))
                for c in range(4):
                    project(l, 7, c, "hgate_ready", lo)
                pe.wait_ge(sem["rope_done"], 8 * (l + 1))

                tiles = [(h, q) for h in range(NA_HEADS) for sg in segs for q in (2 * sg, 2 * sg + 1)]
                per = len(tiles)
                before = 0 if l == 0 else NA_HEADS * 4
                for n in range(per + 4):
                    if n < per:
                        h, q = tiles[n]
                        r = 64 * (h % 2)
                        nk = SEG if q < 2 else TOK
                        o = open_bank(("S", l, n), "na_z")
                        T.matmul(o[:, 0:nk], naq[r:r + 64, h // 2, q * P:(q + 1) * P], nak[r:r + 64, h // 2, 0:nk],
                                 start=True, stop=True).then_inc(sem["psum_ready"], 1)
                    m = n - 2
                    if 0 <= m < per:
                        h, q = tiles[m]
                        o = open_bank(("TR", l, m), "na_pt")
                        pe.wait_ge(sem["na_pn"], before + m + 1)
                        for k in range(2 if q < 2 else 4):
                            mm = T.transpose(o[:, k * P:(k + 1) * P], probs[(before + m) % 3][:, k * P:(k + 1) * P], ident)
                        mm.then_inc(sem["psum_ready"], 1)
                    m = n - 4
                    if m >= 0 and m % 2 == 1:
                        h, q = tiles[m]
                        r = 64 * (h % 2)
                        o = open_bank(("PV", l, m // 2), "na_o")
                        pe.wait_ge(*read_by(("TR", l, m)))
                        nk = 2 if q < 2 else 4
                        for k in range(nk):
                            mm = T.matmul(o[r:r + 64, 0:SEG], navv[:, k, h * 64:(h + 1) * 64],
                                          pt[(m // 2) % 2][:, k, :], start=(k == 0), stop=(k == nk - 1))
                        mm.then_inc(sem["psum_ready"], 1)
                h, q = tiles[per - 1]
                if stop <= 10 * l + 4:
                    break

                for h in range(HG_HEADS):
                    o = open_bank(("oms", l, h), "hg_std")
                    pe.wait_ge(sem["osq_ready"], 4 * l + h + 1)
                    T.matmul(o[:, lo:TOK], ones, osq[:, h % 2, lo:TOK], start=True, stop=True)\
                        .then_inc(sem["psum_ready"], 1)

                for br, (first, wo, src) in enumerate(((8, "nao", ona), (10, "hgo", oh))):
                    pe.wait_ge(*full((wo, l)))
                    if br == 0:
                        pe.wait_ge(*read_by(("PV", l, per // 2 - 1)))
                    else:
                        pe.wait_ge(sem["og_ready"], 4 * (l + 1))
                    w = slot((wo, l)).rearrange("p (k n) -> p k n", k=4)
                    for d in range(KT):
                        if d % 4 == 0:
                            pe.wait_ge(*full(("in", l, first + d // 4)))
                        project(l, first + d // 4, d % 4, "gate_sig", lo)
                        o = open_bank(("y", l, br, d), "merged_ready")
                        for k in range(4):
                            mm = T.matmul(o[:, lo:TOK], w[:, k, d * P:(d + 1) * P], src[:, k, lo:TOK],
                                          start=(k == 0), stop=(k == 3))
                        mm.then_inc(sem["psum_ready"], 1)
                    slot_spent[slot_of((wo, l))] = jobs[0]
                pe.wait_ge(sem["merged_ready"], 16 * (l + 1))
                for d in range(KT):
                    key = ("out", l, d // 4)
                    if d % 4 == 0:
                        pe.wait_ge(*full(key))
                    w = slot(key).rearrange("p (k n) -> p k n", k=KT)
                    o = open_bank(("out", l, d), "x_updated")
                    for k in range(KT):
                        mm = T.matmul(o[:, lo:TOK], w[:, k, (d % 4) * P:(d % 4 + 1) * P], merged[:, k, lo:TOK],
                                      start=(k == 0), stop=(k == KT - 1))
                    mm.then_inc(sem["psum_ready"], 1)
                    if d % 4 == 3:
                        slot_spent[slot_of(key)] = jobs[0]
                if stop <= 10 * l + 5:
                    break

                mean_square(("ms", l, 1), 2 * l + 1, lo)
                pe.wait_ge(sem["h_ready"], KT * (2 * l + 2))
                o = open_bank(("route", l), "route_done")
                for t in range(2 * (l > 0), 4):
                    for k in range(KT):
                        mm = T.matmul(o[:, t * N_EXPERTS:(t + 1) * N_EXPERTS], hT[:, k, t * P:(t + 1) * P],
                                      router[:, k, :], start=(k == 0), stop=(k == KT - 1))
                mm.then_inc(sem["psum_ready"], 1)
                pe.wait_ge(sem["comb_col"], l + 1)
                for e in range(N_EXPERTS):
                    o = open_bank(("cb", l, e), "comb_bcast")
                    for t in range(2 * (l > 0), 4):
                        mm = T.matmul(o[:, t * P:(t + 1) * P], combw[:, t, e, :], ident, start=True, stop=True)
                    mm.then_inc(sem["psum_ready"], 1)
                for b in range(8):
                    pe.wait_ge(*read_by(in_bank[b]))
                first = jobs[0]
                base = slot_of(("moe", l, 0, 0))
                ready["moe", l] = first
                with pe.Fori(0, N_EXPERTS // 4) as i:
                    for e in range(4):
                        for f in range(4):
                            for g in range(2):
                                s = (base + 3 * e + g) % SLOTS
                                if f == 0:
                                    pe.wait_ge(slot_full[s], i * 48 + 16 * ((base + 3 * e + g) // SLOTS + 1))
                                pe.wait_ge(sem["down_done"], i * 32 + (moe_down0(l) + 8 * e - 8 + 2 * f + g + 1))
                                w = ring[:, s, :].rearrange("p (k n) -> p k n", k=KT)
                                for k in range(KT):
                                    mm = T.matmul(bank[2 * f + g][:, lo:TOK], w[:, k, f * P:(f + 1) * P],
                                                  hT[:, k, lo:TOK], start=(k == 0), stop=(k == KT - 1))
                                mm.then_inc(sem["psum_ready"], 1)
                        s = (base + 3 * e + 2) % SLOTS
                        pe.wait_ge(slot_full[s], i * 48 + 16 * ((base + 3 * e + 2) // SLOTS + 1))
                        pe.wait_ge(sem["act_ready"], i * 16 + (acts0(l) + 4 * e + 4))
                        w = ring[:, s, :].rearrange("p (k n) -> p k n", k=4)
                        for d in range(KT):
                            for k in range(4):
                                mm = T.matmul(bank[d][:, lo:TOK], w[:, k, d * P:(d + 1) * P],
                                              acts[:, e % 2, k, lo:TOK], start=(k == 0), stop=(k == 3))
                            mm.then_inc(sem["psum_ready"], 1)
                jobs[0] += 16 * N_EXPERTS
                for m in range(3 * N_EXPERTS):
                    slot_spent[base + m] = first + expert_spent(m)
                for b in range(8):
                    in_bank[b] = ("down", l, b)
                    reader["down", l, b] = ("down_done", moe_down0(l) + 8 * N_EXPERTS - 7 + b)
            if stop > 30:
                mean_square(("ms", 2, 0), 4, SEG)

        @block.sync
        def _(sp):
            sp.dma_start(vec[:], A["vec"]).then_inc(sem["vec_loaded"], 16)
            sp.dma_start(const[:], A["const"]).then_inc(sem["const_loaded"], 16)

            def source(key):
                if key[0] == "ada":
                    return A["w_ada"][key[1], :, key[2] * 512:(key[2] + 1) * 512].rearrange("(k p) n -> p k n", p=P), KT
                if key[0] == "in":
                    return A["w_in"][key[1], :, key[2] * 512:(key[2] + 1) * 512].rearrange("(k p) n -> p k n", p=P), KT
                if key[0] == "out":
                    return A["w_out"][key[1], :, key[2] * 512:(key[2] + 1) * 512].rearrange("(k p) n -> p k n", p=P), KT
                return A["w_na_o" if key[0] == "nao" else "w_hg_o"][key[1]].rearrange("(k p) n -> p k n", p=P), 4

            def fill(n):
                src, k = source(loads[n])
                sp.dma_start(ring[:, n % SLOTS, :].rearrange("p (k n) -> p k n", k=k), src)\
                    .then_inc(slot_full[n % SLOTS], 16)

            for n in range(SLOTS):
                fill(n)
            sp.dma_start(xT[:], A["xT"].rearrange("(k p) n -> p k n", p=P)).then_inc(sem["x_loaded"], 16)
            sp.dma_start(levmask_f[:], A["levmask"]).then_inc(sem["x_loaded"], 16)
            sp.dma_start(router[:], A["w_router"].rearrange("(k p) n -> p k n", p=P)).then_inc(sem["x_loaded"], 16)
            n = SLOTS
            for l in range(DEPTH):
                base = slot_of(("moe", l, 0, 0))
                while n < base:
                    if n - SLOTS not in slot_spent:
                        break
                    sp.wait_ge(sem["psum_ready"], slot_spent[n - SLOTS])
                    fill(n)
                    n += 1
                if n < base or ("moe", l) not in ready:
                    break
                first = ready["moe", l]
                w = (A["w_gate"], A["w_up"], A["w_down"])

                def fill_expert(m, src, k):
                    s = (base + m) % SLOTS
                    sp.dma_start(ring[:, s, :].rearrange("p (k n) -> p k n", k=k), src)\
                        .then_inc(slot_full[s], 16)

                for m in range(SLOTS):
                    sp.wait_ge(sem["psum_ready"], slot_spent[base + m - SLOTS])
                    fill_expert(m, w[m % 3][l, m // 3].rearrange("(k p) n -> p k n", p=P), (KT, KT, 4)[m % 3])
                flat = [x.rearrange("l e (k p) n -> (l e) p k n", p=P) for x in w]
                with sp.Fori(0, N_EXPERTS // 4 - 1) as i:
                    for m in range(SLOTS, SLOTS + 12):
                        sp.wait_ge(sem["psum_ready"], i * 64 + (first + expert_spent(m - SLOTS)))
                        fill_expert(m, flat[m % 3][i * 4 + (l * N_EXPERTS + m // 3), :, :, :], (KT, KT, 4)[m % 3])
                for m in range(SLOTS + 36, 48):
                    sp.wait_ge(sem["psum_ready"], first + 48 * 4 + expert_spent(m - SLOTS - 36))
                    fill_expert(m, w[m % 3][l, m // 3].rearrange("(k p) n -> p k n", p=P), (KT, KT, 4)[m % 3])
                n = base + 48
            if stop <= 30:
                for i in range(SLOTS):
                    sp.wait_ge(slot_full[i], 16 * sum(1 for m in range(n) if m % SLOTS == i))
                sp.wait_ge(sem["x_loaded"], 48)
            if stop > 30:
                for k in range(KT):
                    sp.wait_ge(sem["h_ready"], KT * 4 + k + 1)
                    sp.dma_start(out[k * P:(k + 1) * P, :], hT[:, k, SEG:TOK]).then_inc(sem["out_stored"], 16)
                sp.wait_ge(sem["out_stored"], 16 * KT)

        @block.scalar
        def _(act):
            chained = [0]

            def link(ins):
                chained[0] += 1
                ins.then_inc(sem["act_chain"], 1)
                act.wait_ge(sem["act_chain"], chained[0])

            act.wait_ge(sem["vec_loaded"], 16)
            S.activation(cond[:].rearrange("p k c -> p (k c)"), vec[:, VEC_COND:VEC_COND + 2 * KT], ACT.Silu)\
                .then_inc(sem["cond_ready"], 1)
            act.wait_ge(sem["lower_ready"], 1)
            S.activation(lowtmp[:, 1:3].rearrange("p l d h -> p (l d h)"),
                         lowtmp[:, 1:3].rearrange("p l d h -> p (l d h)"), ACT.Exp).then_inc(sem["lower_ready"], 1)
            for n in range(DEPTH * 12):
                l, s = n // 12, n % 12
                act.wait_ge(*is_ready(("ada", l, s)))
                if n >= 2:
                    act.wait_ge(*is_ready(("adaT", (n - 2) // 12, (n - 2) % 12)))
                S.activation(adarow[:, n % 2, :], result(("ada", l, s))[0:2, :], ACT.Copy).then_inc(sem["ada_row"], 1)

            def norm(key, count, lo, tail):
                for k in range(KT):
                    if k >= 2:
                        act.wait_ge(sem["square_used"], (KT - 1) * count + k - 1)
                    elif count:
                        act.wait_ge(*is_ready(prev_ms(key)))
                    if count == 0:
                        act.wait_ge(sem["x_loaded"], 48)
                    else:
                        act.wait_ge(*tail(k))
                    S.activation(square[:, k % 2, lo:TOK], xT[:, k, lo:TOK], ACT.Square)\
                        .then_inc(sem["square_ready"], 1)
                act.wait_ge(*is_ready(key))
                act.wait_ge(sem["epsv_ready"], 1)
                if count:
                    act.wait_ge(sem["normed_ready"], KT * count)
                S.activation(rstd[:, lo:TOK], result(key)[:, lo:TOK], ACT.Sqrt, scale=1.0 / D, bias=epsv[:, 0:1])\
                    .then_inc(sem["norm_std"], 1)

            def head_std(l, h, lo):
                act.wait_ge(*is_ready(("oms", l, h)))
                if h >= 2:
                    act.wait_ge(sem["og_ready"], 4 * l + h - 1)
                S.activation(ors[:, h % 2, lo:TOK], result(("oms", l, h))[:, lo:TOK], ACT.Sqrt, scale=1.0 / P,
                             bias=epsv[:, 0:1]).then_inc(sem["hg_std"], 1)

            def prev_ms(key):
                return {("ms", 0, 1): ("ms", 0, 0), ("ms", 1, 0): ("ms", 0, 1), ("ms", 1, 1): ("ms", 1, 0),
                        ("ms", 2, 0): ("ms", 1, 1)}[key]

            for l in range(DEPTH):
                if stop <= 10 * l + 1:
                    break
                lo = 0 if l == 0 else SEG
                segs = segs_of[l]
                norm(("ms", l, 0), 2 * l, 0, lambda k: (sem["down_done"], moe_down0(l - 1) + 8 * (N_EXPERTS - 1) + k + 1))
                for c in range(4):
                    act.wait_ge(*is_ready(("in", l, 3, c)))
                    S.activation(qh[:, 2 * c + segs[0]:2 * c + 2, :].rearrange("p s t -> p (s t)"),
                                 result(("in", l, 3, c))[:, lo:TOK], ACT.Silu).then_inc(sem["q_ready"], 1)
                for way, k_to in enumerate((kf, kb)):
                    if way == 1:
                        act.wait_ge(sem["log_out"], 2 * l + 1)
                    for c in range(4):
                        key = ("in", l, 4 + way, c)
                        act.wait_ge(*is_ready(key))
                        S.activation(sig[:, c * TOK:(c + 1) * TOK], result(key)[:, :], ACT.Sigmoid)\
                            .then_inc(sem["sig_ready"], 1)
                        S.activation(k_to[:, 2 * c:2 * c + 2, :].rearrange("p s t -> p (s t)"), result(key)[:, :],
                                     ACT.Sigmoid, scale=-1.0).then_inc(sem["k_sig"], 1)
                    act.wait_ge(sem["log_in"], 2 * l + way + 1)
                    S.activation(logs[:], sig[:], ACT.Ln).then_inc(sem["log_out"], 1)
                for t in range(4):
                    act.wait_ge(*is_ready(("in", l, 6, t)))
                    S.activation(vh[:, t, :], result(("in", l, 6, t))[:, :], ACT.Copy).then_inc(sem["v_ready"], 1)
                if stop <= 10 * l + 2:
                    break
                extra = [(s, c) for s in (0, 1) for c in range(4)]

                def between():
                    s, c = extra.pop(0)
                    a = lo if s == 0 else 0
                    act.wait_ge(*is_ready(("in", l, s, c)))
                    S.activation((naq, nak)[s][:, c, a:TOK], result(("in", l, s, c))[:, a:TOK], ACT.Copy)\
                        .then_inc(sem["naqk_ready"], 1)

                d = 36 * l
                u = 38 * l
                for hp in range(2):
                    for unit in range(19):
                        if unit:
                            act.wait_ge(sem["decay_in"], d + 1)
                            na = 4 if (unit - 1) // 2 > LEVELS or l == 0 else 2
                            e = dec[d % 2][:, 0:na, :]
                            S.activation(e, e, ACT.Exp).then_inc(sem["decay_out"], 1)
                            d += 1
                        if unit % 4 == 0 and unit and extra:
                            between()
                        u += 1
                while extra:
                    between()
                for h in range(HG_HEADS):
                    act.wait_ge(*is_ready(("o", l, h)))
                    S.activation(oh[:, h, lo:TOK], result(("o", l, h))[:, lo:TOK], ACT.Copy)\
                        .then_inc(sem["oh_ready"], 1)
                if stop <= 10 * l + 3:
                    break
                for r in range(4):
                    src = A["rel_bias_reversed"]
                    for h in range(NA_HEADS):
                        skew = bass.AP(src.tensor, ((l * NA_HEADS + h) * 15 + 7 - r) * 31 + 15 + 1 - GRID_W,
                                       [[1, GRID_W], [31, 4], [1, GRID_W]])
                        act.dma_start(bias_skew[64 * (r % 2):64 * (r % 2) + 64, h, r // 2, :]
                                      .rearrange("p (a c) -> p a c", a=4), skew).then_inc(sem["bias_loaded"], 16)
                for t in range(4):
                    act.wait_ge(*is_ready(("in", l, 2, t)))
                    S.activation(navv[:, t, :], result(("in", l, 2, t))[:, :], ACT.Copy).then_inc(sem["nav_ready"], 1)
                for c in range(4):
                    act.wait_ge(*is_ready(("in", l, 7, c)))
                    S.activation(hgate[:, c, lo:TOK], result(("in", l, 7, c))[:, lo:TOK], ACT.Silu)\
                        .then_inc(sem["hgate_ready"], 1)
                tiles = [(h, q) for h in range(NA_HEADS) for sg in segs for q in (2 * sg, 2 * sg + 1)]
                per = len(tiles)
                before = 0 if l == 0 else NA_HEADS * 4
                for n in range(per + 2):
                    if n < per:
                        h, q = tiles[n]
                        nk = SEG if q < 2 else TOK
                        act.wait_ge(sem["na_max"], before + n + 1)
                        x = probs[(before + n) % 3]
                        S.activation(x[:, 0:nk], x[:, 0:nk], ACT.Exp, bias=narow[:, (before + n) % 3, 0:1],
                                     accum_out=narow[:, (before + n) % 3, 1:2]).then_inc(sem["na_p"], 1)
                    m = n - 2
                    if m >= 0:
                        h, q = tiles[m]
                        nk = 2 if q < 2 else 4
                        act.wait_ge(*is_ready(("TR", l, m)))
                        if m // 2 >= 2 and m % 2 == 0:
                            act.wait_ge(*is_ready(("PV", l, m // 2 - 2)))
                        S.activation(pt[(m // 2) % 2][:, 0:nk, (q % 2) * P:(q % 2 + 1) * P],
                                     result(("TR", l, m))[:, 0:nk * P].rearrange("p (k q) -> p k q", k=nk), ACT.Copy)\
                            .then_inc(sem["na_pt"], 1)
                if stop <= 10 * l + 4:
                    break
                for h in range(HG_HEADS):
                    if h < 2:
                        act.wait_ge(*is_ready(("PV", l, per // 2 - 1)))
                        act.wait_ge(sem["oh_ready"], 4 * (l + 1))
                    else:
                        act.wait_ge(*is_ready(("oms", l, h - 2)))
                    S.activation(osq[:, h % 2, lo:TOK], oh[:, h, lo:TOK], ACT.Square).then_inc(sem["osq_ready"], 1)
                    if h >= 1:
                        head_std(l, h - 1, lo)
                head_std(l, HG_HEADS - 1, lo)
                for n in range(16):
                    br, d = n // 8, n % 8
                    key = ("in", l, (8, 10)[br] + d // 4, d % 4)
                    act.wait_ge(*is_ready(key))
                    if n >= 2:
                        act.wait_ge(sem["merged_ready"], 16 * l + n - 1)
                    S.activation(gsig[:, n % 2, lo:TOK], result(key)[:, lo:TOK], ACT.Sigmoid)\
                        .then_inc(sem["gate_sig"], 1)
                if stop <= 10 * l + 5:
                    break
                norm(("ms", l, 1), 2 * l + 1, lo, lambda k: (sem["x_updated"], 8 * l + k + 1))
                act.wait_ge(*is_ready(("route", l)))
                S.activation(rt[0][:, 2 * l:4].rearrange("p t g e -> p (t g e)"),
                             result(("route", l))[:, 2 * l * N_EXPERTS:4 * N_EXPERTS], ACT.Sigmoid)\
                    .then_inc(sem["route_done"], 1)
                first = ready["moe", l]
                with act.Fori(0, N_EXPERTS // 4) as i:
                    for e in range(4):
                        for f in range(4):
                            act.wait_ge(sem["psum_ready"], i * 64 + (first + 16 * e + 2 * f + 1))
                            act.wait_ge(sem["act_ready"], i * 16 + (acts0(l) + 4 * e + f - 3))
                            S.activation(silu[:, f, lo:TOK], bank[2 * f][:, lo:TOK], ACT.Silu)\
                                .then_inc(sem["silu_ready"], 1)
            if stop > 30:
                norm(("ms", 2, 0), 4, SEG, lambda k: (sem["down_done"], moe_down0(1) + 8 * (N_EXPERTS - 1) + k + 1))

        @block.gpsimd
        def _(pool):
            for l in range(DEPTH):
                if stop <= 10 * l + 3:
                    break
                pool.wait_ge(sem["const_loaded"], 16)
                pool.wait_ge(sem["bias_loaded"], 16 * 32 * (l + 1))
                for h in range(NA_HEADS):
                    b = bias[:, h].rearrange("p q (r c) -> p (q r) c", c=GRID_W)
                    x = bias_skew[:, h].rearrange("p q (r c) -> p (q r) c", c=GRID_W)
                    back = bass.AP(x.tensor, x.offset + GRID_W - 1, [x.ap[0], [GRID_W, 8], [-1, GRID_W]])
                    wide = [P, 8, GRID_W]
                    G.tensor_tensor(b, back, wmul.unsqueeze(1).to_broadcast(wide), ALU.mult).then_inc(sem["pool_chain"], 1)
                    pool.wait_ge(sem["pool_chain"], 8 * l + h + 1)
                    G.tensor_tensor(b, b, wneg.unsqueeze(1).to_broadcast(wide), ALU.add).then_inc(sem["bias_ready"], 1)

        @block.vector
        def _(dve):
            chained = [0]

            def link(ins):
                chained[0] += 1
                ins.then_inc(sem["dve_chain"], 1)
                dve.wait_ge(sem["dve_chain"], chained[0])

            V.memset(epsv[:], EPS).then_inc(sem["epsv_ready"], 1)
            dve.wait_ge(sem["vec_loaded"], 16)
            raw = vec[:, VEC_LOWER:VEC_LOWER + 2 * DEPTH * HG_HEADS].rearrange("p (l d h) -> p l d h", l=DEPTH, d=2)
            link(V.tensor_tensor(lowtmp[:, 0], raw[:, 0], raw[:, 1], ALU.max))
            V.tensor_tensor(lowtmp[:, 1], raw[:, 0], lowtmp[:, 0], ALU.subtract)
            V.tensor_tensor(lowtmp[:, 2], raw[:, 1], lowtmp[:, 0], ALU.subtract).then_inc(sem["lower_ready"], 1)
            dve.wait_ge(sem["lower_ready"], 2)
            link(V.tensor_tensor(lowtmp[:, 3], lowtmp[:, 1], lowtmp[:, 2], ALU.add))
            link(V.reciprocal(lowtmp[:, 3], lowtmp[:, 3]))
            V.tensor_tensor(lowtmp[:, 4], lowtmp[:, 1], lowtmp[:, 3], ALU.mult)
            link(V.tensor_tensor(lowtmp[:, 5], lowtmp[:, 2], lowtmp[:, 3], ALU.mult))
            V.tensor_tensor(lower[:, :, 0], lowtmp[:, 4], lowtmp[:, 4], ALU.subtract)
            link(V.tensor_tensor(lowtmp[:, 6], lowtmp[:, 4], lowtmp[:, 5], ALU.add))
            link(V.tensor_tensor(lower[:, :, 1], lowtmp[:, 6], lowtmp[:, 4], ALU.subtract))
            link(V.tensor_scalar(upper[:], lower[:], -1.0, 1.0, ALU.mult, ALU.add))

            dve.wait_ge(sem["x_loaded"], 48)
            link(V.tensor_copy(levmask[:], levmask_f[:]))

            for n in range(DEPTH * 12):
                l, s = n // 12, n % 12
                dve.wait_ge(*is_ready(("adaT", l, s)))
                b = vec[:, VEC_BADA + 48 * l + 4 * s:VEC_BADA + 48 * l + 4 * s + 4].unsqueeze(2).to_broadcast([P, 4, 2])
                V.tensor_tensor(mod[:, l, 4 * s:4 * s + 4, :], result(("adaT", l, s))[:, 0:8]
                                .rearrange("p (j c) -> p j c", c=2), b, ALU.add).then_inc(sem["ada_mod"], 1)
            dve.wait_ge(sem["ada_mod"], DEPTH * 12)
            for l in range(DEPTH):
                for gain, at_scale, at_g in ((gain1, KT, VEC_N1), (gain2, 4 * KT, VEC_N2)):
                    g = vec[:, at_g + KT * l:at_g + KT * (l + 1)].unsqueeze(2).to_broadcast([P, KT, 2])
                    link(V.scalar_tensor_tensor(gain[:, l], mod[:, l, at_scale:at_scale + KT, :], 1.0, g,
                                                ALU.add, ALU.mult))

            def norm(count, lo, gain, shift):
                dve.wait_ge(sem["norm_std"], count + 1)
                link(V.reciprocal(rstd[:, lo:TOK], rstd[:, lo:TOK]))
                for k in range(KT):
                    V.tensor_tensor(normed[:, k % 2, lo:TOK], xT[:, k, lo:TOK], rstd[:, lo:TOK], ALU.mult)\
                     .then_inc(sem["normed_ready"], 1)
                    dve.wait_ge(sem["normed_ready"], KT * count + k + 1)
                    for sg in range(1 if lo else 0, 2):
                        a = slice(sg * SEG, (sg + 1) * SEG)
                        if shift is None:
                            op = V.tensor_scalar(hT[:, k, a], normed[:, k % 2, a], gain[:, k:k + 1], None, ALU.mult)
                        else:
                            op = V.tensor_scalar(hT[:, k, a], normed[:, k % 2, a], gain[:, k, 1 - sg:2 - sg],
                                                 shift[:, k, 1 - sg:2 - sg], ALU.mult, ALU.add)
                    op.then_inc(sem["h_ready"], 1)

            def add_scaled(key_bank, l, d, at_gate, lo):
                for sg in range(1 if lo else 0, 2):
                    a = slice(sg * SEG, (sg + 1) * SEG)
                    op = V.scalar_tensor_tensor(xT[:, d, a], key_bank[:, a], mod[:, l, at_gate + d, 1 - sg:2 - sg],
                                                xT[:, d, a], ALU.mult, ALU.add)
                return op

            for l in range(DEPTH):
                if stop <= 10 * l + 1:
                    break
                lo = 0 if l == 0 else SEG
                segs = segs_of[l]
                norm(2 * l, 0, gain1[:, l], mod[:, l, 0:KT, :])
                V.memset(onescan[:], 1.0)
                V.memset(pf[:, :, 0:1], 0.0)
                link(V.memset(pb[:, :, 0:1], 0.0))
                for way, (k_to, p_to) in enumerate(((kf, pf), (kb, pb))):
                    for h in range(HG_HEADS):
                        dve.wait_ge(sem["sig_ready"], 8 * l + 4 * way + h + 1)
                        dve.wait_ge(sem["k_sig"], 8 * l + 4 * way + h + 1)
                        up, low = upper[:, way, l, h:h + 1], lower[:, way, l, h:h + 1]
                        kh = k_to[:, 2 * h:2 * h + 2, :].rearrange("p s t -> p (s t)")
                        V.tensor_scalar(kh, kh, up, None, ALU.mult)
                        gh = sig[:, h * TOK:(h + 1) * TOK]
                        last = V.tensor_scalar(gh, gh, up, low, ALU.mult, ALU.add)
                    link(last)
                    V.tensor_scalar(small[:], sig[:], 2.0 ** -40, 2.0 ** 60, ALU.is_lt, ALU.mult)
                    link(V.tensor_scalar(sig[:], sig[:], GATE_FLOOR, None, ALU.max))
                    V.scalar_tensor_tensor(sig[:], small[:], 1.0, sig[:], ALU.add, ALU.mult).then_inc(sem["log_in"], 1)
                    dve.wait_ge(sem["log_out"], 2 * l + way + 1)
                    link(V.scalar_tensor_tensor(logs[:], small[:], -60.0 * float(np.log(2.0)) / 2.0 ** 60, logs[:],
                                                ALU.mult, ALU.add))
                    for hs in range(8):
                        last = V.tensor_tensor_scan(p_to[:, hs, 1:SEG + 1], onescan[:], logs[:, hs * SEG:(hs + 1) * SEG],
                                                    0.0, ALU.mult, ALU.add)
                    link(last)
                if stop <= 10 * l + 2:
                    break

                def rows(hp, all_segs):
                    return slice(4 * hp, 4 * hp + 4) if all_segs else slice(4 * hp + 1, 4 * hp + 4, 2)

                def halves(x, h):
                    y = x.rearrange("p a (n two h) -> p a n two h", two=2, h=h)
                    return y[:, :, :, 0, :], y[:, :, :, 1, :]

                def decays(hp, unit, u, d):
                    if u >= 2:
                        dve.wait_ge(sem["fac_ready"], u - 1)
                    lev, way = (unit - 1) // 2, (unit - 1) % 2
                    p, off = ((pf, 1), (pb, 0))[way]
                    x = dec[d % 2]
                    if lev <= LEVELS:
                        h = 1 << lev
                        r = rows(hp, l == 0)
                        na = 2 * len(segs)
                        left, right = halves(p[:, r, off:off + SEG], h)
                        to_left, to_right = halves(x[:, 0:na, :], h)
                        shape = [P, na, SEG // (2 * h), h]
                        mid = p[:, r, h:SEG:2 * h].unsqueeze(3).to_broadcast(shape)
                        V.tensor_tensor(to_left, mid, left, ALU.subtract)
                        V.tensor_tensor(to_right, right, mid, ALU.subtract).then_inc(sem["decay_in"], 1)
                    else:
                        for sg in range(2):
                            q = p[:, 4 * hp + sg:4 * hp + 4:2, off:off + SEG]
                            to = x[:, sg:4:2, :]
                            if sg == way:
                                end = p[:, 4 * hp + sg:4 * hp + 4:2, SEG:SEG + 1].to_broadcast([P, 2, SEG])
                                op = V.tensor_tensor(to, end, q, ALU.subtract)
                            else:
                                op = V.tensor_copy(to, q)
                        op.then_inc(sem["decay_in"], 1)

                def factors(hp, unit, u, d):
                    lev, way = (unit - 1) // 2, (unit - 1) % 2
                    if u - 2 in spent:
                        dve.wait_ge(sem["psum_ready"], spent[u - 2])
                    y = fac[u % 2]
                    r = rows(hp, l == 0)
                    na = 2 * len(segs)
                    if unit == 0:
                        V.tensor_tensor(y[:, 0:na, :], kf[:, r, :], kb[:, r, :], ALU.add).then_inc(sem["fac_ready"], 1)
                        return
                    dve.wait_ge(sem["decay_out"], d + 1)
                    k = (kf, kb)[way]
                    if lev <= LEVELS:
                        h = 1 << lev
                        e, to = halves(dec[d % 2][:, 0:na, :], h), halves(y[:, 0:na, :], h)
                        src = (halves(k[:, r, :], h)[way], halves(qh[:, r, :], h)[1 - way])
                        V.tensor_tensor(to[way], e[way], src[0], ALU.mult)
                        V.tensor_tensor(to[1 - way], e[1 - way], src[1], ALU.mult).then_inc(sem["fac_ready"], 1)
                    else:
                        x = dec[d % 2]
                        V.tensor_tensor(y[:, 0:4:2, :], x[:, 0:4:2, :], k[:, 4 * hp:4 * hp + 4:2, :], ALU.mult)
                        V.tensor_tensor(y[:, 1:4:2, :], x[:, 1:4:2, :], qh[:, 4 * hp + 1:4 * hp + 4:2, :], ALU.mult)\
                         .then_inc(sem["fac_ready"], 1)

                def diagonal(head):
                    x = att[:, head, segs[0], :, :]
                    dims = [x.ap[0]] + ([[2 * SEG, 2]] if l == 0 else []) + [[SEG + P, 2], [1, P]]
                    return bass.AP(x.tensor, x.offset, dims)

                def collect(hp, unit, u):
                    lev, way = (unit - 1) // 2, (unit - 1) % 2
                    if lev < LEVELS:
                        for h in range(2):
                            dve.wait_ge(*is_ready(("lev", l, u, h)))
                            got = result(("lev", l, u, h))[:, 0:2 * P * len(segs)]
                            if l == 0:
                                got = got.rearrange("p (s b t) -> p s b t", s=2, b=2)
                                shape = [P, 2, 2, P]
                            else:
                                got = got.rearrange("p (b t) -> p b t", b=2)
                                shape = [P, 2, P]
                            if unit == 0:
                                V.tensor_copy(diagonal(2 * hp + h), got).then_inc(sem["att_block"], 1)
                            else:
                                mask = levmask[:, way * LEVELS + lev, :]
                                for _ in range(len(shape) - 2):
                                    mask = mask.unsqueeze(1)
                                dve.wait_ge(*read_by(("lev", l, u - 1, h)))
                                V.copy_predicated(diagonal(2 * hp + h), mask.to_broadcast(shape), got)\
                                 .then_inc(sem["att_block"], 1)
                    elif lev == LEVELS:
                        dve.wait_ge(*is_ready(("lev", l, u, 0)))
                        got = result(("lev", l, u, 0))[:, 0:2 * P * len(segs)]
                        t0 = P * (1 - way)
                        if l == 0:
                            V.tensor_copy(att[:, 2 * hp:2 * hp + 2, :, way, t0:t0 + P],
                                          got.rearrange("p (h s t) -> p h s t", h=2, s=2)).then_inc(sem["att_block"], 1)
                        else:
                            V.tensor_copy(att[:, 2 * hp:2 * hp + 2, 1, way, t0:t0 + P],
                                          got.rearrange("p (h t) -> p h t", h=2)).then_inc(sem["att_block"], 1)
                    elif way == 1:
                        for h in range(2):
                            dve.wait_ge(*is_ready(("cross", l, hp, h)))
                            V.tensor_copy(attx[:, 2 * hp + h].rearrange("p b t -> p (b t)"),
                                          result(("cross", l, hp, h))[:, :]).then_inc(sem["att_block"], 1)

                units = [(hp, unit) for hp in range(2) for unit in range(19)]
                d_in = d_out = 36 * l
                for n in range(-1, len(units) + 1):
                    if n + 1 < len(units) and units[n + 1][1]:
                        decays(*units[n + 1], 38 * l + n + 1, d_in)
                        d_in += 1
                    if 0 <= n < len(units):
                        factors(*units[n], 38 * l + n, d_out)
                        d_out += units[n][1] > 0
                    if n >= 1:
                        collect(*units[n - 1], 38 * l + n - 1)
                if stop <= 10 * l + 3:
                    break

                for n in range(8):
                    dve.wait_ge(*is_ready(("rot", l, n)))
                    if n:
                        dve.wait_ge(sem["rope_done"], 8 * l + n)
                    x = (naq, nak)[n // 4][:, n % 4, SEG:TOK]
                    V.tensor_tensor(roped[:, 0], x, cos, ALU.mult)
                    link(V.tensor_tensor(roped[:, 1], result(("rot", l, n))[:, 0:SEG], sin, ALU.mult))
                    V.tensor_tensor(x, roped[:, 0], roped[:, 1], ALU.add).then_inc(sem["rope_done"], 1)

                tiles = [(h, q) for h in range(NA_HEADS) for sg in segs for q in (2 * sg, 2 * sg + 1)]
                per = len(tiles)
                before = 0 if l == 0 else NA_HEADS * 4
                scale = NA_DIM ** -0.5
                for n in range(per + 5):
                    if n < per:
                        h, q = tiles[n]
                        x = probs[(before + n) % 3]
                        dve.wait_ge(*is_ready(("S", l, n)))
                        if n >= 3:
                            dve.wait_ge(*is_ready(("TR", l, n - 3)))
                        got = result(("S", l, n))
                        op = V.tensor_scalar(x[:, 0:SEG], got[:, 0:SEG], scale, None, ALU.mult)
                        if q >= 2:
                            dve.wait_ge(sem["bias_ready"], 8 * l + h + 1)
                            op = V.scalar_tensor_tensor(x[:, SEG:TOK], got[:, SEG:TOK], scale, bias[:, h, q - 2, :],
                                                        ALU.mult, ALU.add)
                        op.then_inc(sem["na_z"], 1)
                        dve.wait_ge(*read_by(("S", l, n)))
                        V.tensor_reduce(narow[:, (before + n) % 3, 0:1], x[:, 0:SEG if q < 2 else TOK], AX.X, ALU.max,
                                        negate=True).then_inc(sem["na_max"], 1)
                    m = n - 1
                    if 0 <= m < per:
                        h, q = tiles[m]
                        nk = SEG if q < 2 else TOK
                        i = (before + m) % 3
                        dve.wait_ge(sem["na_p"], before + m + 1)
                        link(V.reciprocal(narow[:, i, 2:3], narow[:, i, 1:2]))
                        V.tensor_scalar(probs[i][:, 0:nk], probs[i][:, 0:nk], narow[:, i, 2:3], None, ALU.mult)\
                         .then_inc(sem["na_pn"], 1)
                    m = n - 5
                    if m >= 0 and m % 2 == 1:
                        h, q = tiles[m]
                        r = 64 * (h % 2)
                        sg = q // 2
                        dve.wait_ge(*is_ready(("PV", l, m // 2)))
                        V.tensor_copy(ona[r:r + 64, h // 2, sg * SEG:(sg + 1) * SEG],
                                      result(("PV", l, m // 2))[r:r + 64, 0:SEG]).then_inc(sem["na_o"], 1)
                if stop <= 10 * l + 4:
                    break

                for h in range(HG_HEADS):
                    dve.wait_ge(sem["hg_std"], 4 * l + h + 1)
                    dve.wait_ge(sem["hgate_ready"], 4 * l + h + 1)
                    x, y = oh[:, h, lo:TOK], ors[:, h % 2, lo:TOK]
                    link(V.reciprocal(y, y))
                    link(V.tensor_tensor(x, x, y, ALU.mult))
                    V.scalar_tensor_tensor(x, x, vec[:, VEC_HGAIN + l:VEC_HGAIN + l + 1], hgate[:, h, lo:TOK],
                                           ALU.mult, ALU.mult).then_inc(sem["og_ready"], 1)

                for n in range(16):
                    br, d = n // 8, n % 8
                    dve.wait_ge(sem["gate_sig"], 16 * l + n + 1)
                    dve.wait_ge(*is_ready(("y", l, br, d)))
                    got, gate, to = result(("y", l, br, d))[:, lo:TOK], gsig[:, n % 2, lo:TOK], merged[:, d, lo:TOK]
                    if br == 0:
                        V.tensor_tensor(to, gate, got, ALU.mult).then_inc(sem["merged_ready"], 1)
                    else:
                        link(V.tensor_tensor(gmul[:, n % 2, lo:TOK], gate, got, ALU.mult))
                        V.tensor_tensor(to, to, gmul[:, n % 2, lo:TOK], ALU.add).then_inc(sem["merged_ready"], 1)
                for d in range(KT):
                    dve.wait_ge(*is_ready(("out", l, d)))
                    add_scaled(result(("out", l, d)), l, d, 2 * KT, lo).then_inc(sem["x_updated"], 1)
                if stop <= 10 * l + 5:
                    break
                norm(2 * l + 1, lo, gain2[:, l], mod[:, l, 3 * KT:4 * KT, :])

                t0 = 2 * l
                nt = 4 - t0
                shape = [P, 4 * nt, PER_GROUP]
                idx = vec[:, VEC_GIDX:VEC_GIDX + 4].unsqueeze(1)
                flat = [x[:, t0:4].rearrange("p t g e -> p (t g) e") for x in rt]
                scores, biased, eq, cand, oh1, oh2, sel, m1, m2, mn, gs, ing = flat

                def first_max(x, hot, mx, n):
                    shape = [P, n, 4]
                    link(V.tensor_reduce(mx, x, AX.X, ALU.max))
                    link(V.tensor_tensor(eq[:, 0:n, :], x, mx.to_broadcast(shape), ALU.is_equal))
                    link(V.scalar_tensor_tensor(cand[:, 0:n, :], eq[:, 0:n, :], -8.0, idx.to_broadcast(shape),
                                                ALU.mult, ALU.add))
                    link(V.tensor_reduce(mn[:, 0:n, 0:1], cand[:, 0:n, :], AX.X, ALU.min))
                    link(V.tensor_tensor(hot, cand[:, 0:n, :], mn[:, 0:n, 0:1].to_broadcast(shape), ALU.is_equal))

                dve.wait_ge(sem["route_done"], l + 1)
                rb = vec[:, VEC_RBIAS:VEC_RBIAS + N_EXPERTS].unsqueeze(1).to_broadcast([P, nt, N_EXPERTS])
                link(V.tensor_tensor(biased.rearrange("p (t g) e -> p t (g e)", g=4),
                                     scores.rearrange("p (t g) e -> p t (g e)", g=4), rb, ALU.add))
                first_max(biased, oh1, m1[:, :, 0:1], 4 * nt)
                link(V.scalar_tensor_tensor(biased, oh1, -1e9, biased, ALU.mult, ALU.add))
                first_max(biased, oh2, m2[:, :, 0:1], 4 * nt)
                g4 = gs[:, 0:nt, :]
                link(V.tensor_tensor(g4, m1[:, :, 0].rearrange("p (t g) -> p t g", g=4),
                                     m2[:, :, 0].rearrange("p (t g) -> p t g", g=4), ALU.add))
                first_max(g4, ing[:, 0:nt, :], m1[:, 0:nt, 1:2], nt)
                link(V.tensor_tensor(sel, oh1, oh2, ALU.add))
                link(V.tensor_tensor(sel, sel, ing[:, 0:nt, :].rearrange("p t g -> p (t g)").unsqueeze(2)
                                     .to_broadcast(shape), ALU.mult))
                link(V.tensor_tensor(sel, sel, scores, ALU.mult))
                link(V.tensor_reduce(m2[:, 0:nt, 1:2], sel.rearrange("p (t g) e -> p t (g e)", g=4), AX.X, ALU.add))
                link(V.reciprocal(m2[:, 0:nt, 2:3], m2[:, 0:nt, 1:2]))
                link(V.tensor_tensor(sel.rearrange("p (t g) e -> p t (g e)", g=4), sel.rearrange("p (t g) e -> p t (g e)", g=4),
                                     m2[:, 0:nt, 2:3].to_broadcast([P, nt, N_EXPERTS]), ALU.mult))
                for t in range(nt):
                    op = V.tensor_copy(combw[:, t0 + t], sel[:, 4 * t:4 * t + 4, :].rearrange("p g e -> p (g e)")
                                       .unsqueeze(2).to_broadcast([P, N_EXPERTS, P]))
                op.then_inc(sem["comb_col"], 1)
                V.memset(credit[:, 2 * l:2 * l + 1], 0.0).then_inc(sem["down_done"], 8)
                V.memset(credit[:, 2 * l + 1:2 * l + 2], 0.0).then_inc(sem["act_ready"], 4)
                for e in range(N_EXPERTS):
                    dve.wait_ge(*is_ready(("cb", l, e)))
                    V.tensor_copy(combb[:, e, lo:TOK], result(("cb", l, e))[:, lo:TOK]).then_inc(sem["comb_bcast"], 1)
                dve.wait_ge(sem["comb_bcast"], N_EXPERTS * (l + 1))

                first = ready["moe", l]
                down0, a0 = moe_down0(l), acts0(l)
                scaled0 = 64 * l
                with dve.Fori(0, N_EXPERTS // 4) as i:
                    for e in range(4):
                        for f in range(4):
                            dve.wait_ge(sem["silu_ready"], i * 16 + (64 * l + 4 * e + f + 1))
                            V.tensor_tensor(silu[:, f, lo:TOK], silu[:, f, lo:TOK], combb[:, i * 4 + e, lo:TOK], ALU.mult)\
                             .then_inc(sem["silu_scaled"], 1)
                            dve.wait_ge(sem["silu_scaled"], i * 16 + (scaled0 + 4 * e + f + 1))
                            dve.wait_ge(sem["psum_ready"], i * 64 + (first + 16 * e + 2 * f + 2))
                            V.tensor_tensor(acts[:, e % 2, f, lo:TOK], silu[:, f, lo:TOK], bank[2 * f + 1][:, lo:TOK],
                                            ALU.mult).then_inc(sem["act_ready"], 1)
                        for d in range(KT):
                            dve.wait_ge(sem["psum_ready"], i * 64 + (first + 16 * e + 8 + d + 1))
                            dve.wait_ge(sem["down_done"], i * 32 + (down0 + 8 * e - 8 + d + 1))
                            add_scaled(bank[d], l, d, 5 * KT, lo).then_inc(sem["down_done"], 1)
            if stop > 30:
                norm(4, SEG, vec[:, VEC_FINAL:VEC_FINAL + KT], None)


def constants():
    c = np.zeros((P, C_N), np.float32)
    c[:, C_IDENT:C_IDENT + P] = np.eye(P)
    c[:, C_ONES:C_ONES + P] = 1.0
    for i in range(0, P, 2):
        c[i + 1, C_ROT + i] = -1.0
        c[i, C_ROT + i + 1] = 1.0
    t = np.arange(SEG)
    row, col = (t // GRID_W).astype(np.float32), (t % GRID_W).astype(np.float32)
    inv = np.float32(10000.0) ** (-np.arange(0, 32, 2, dtype=np.float32) / np.float32(32))
    ang = np.concatenate([row[:, None] * inv, col[:, None] * inv], axis=-1)
    c[:, C_COS:C_COS + SEG] = np.repeat(np.tile(np.cos(ang).T, (2, 1)), 2, axis=0)
    c[:, C_SIN:C_SIN + SEG] = np.repeat(np.tile(np.sin(ang).T, (2, 1)), 2, axis=0)
    col = np.arange(P)[:, None] % GRID_W
    kc = np.arange(GRID_W)[None, :]
    start = np.clip(col - WIN_COLS // 2, 0, GRID_W - WIN_COLS)
    inside = (kc >= start) & (kc < start + WIN_COLS)
    c[:, C_WMUL:C_WMUL + GRID_W] = inside
    c[:, C_WNEG:C_WNEG + GRID_W] = np.where(inside, 0.0, MASKED)
    m = np.zeros((P, 2 * LEVELS, P), np.float32)
    s, t = np.arange(P)[:, None], np.arange(P)[None, :]
    for lev in range(LEVELS):
        h = 1 << lev
        same = s // (2 * h) == t // (2 * h)
        m[:, lev] = same & (s % (2 * h) < h) & (t % (2 * h) >= h)
        m[:, LEVELS + lev] = same & (s % (2 * h) >= h) & (t % (2 * h) < h)
    return c, m


def kernel(**inputs):
    import numpy as _np
    import concourse.bacc as _bacc
    from concourse import mybir as _mybir
    from concourse.bass_utils import run_bass_kernel_spmd as _run

    a = {k: _np.asarray(v) for k, v in inputs.items()}

    def cols(x):
        x = x.reshape(*x.shape[:-1], -1, P)
        return _np.moveaxis(x, -1, 0).reshape(P, -1)

    lower = _np.stack([a["hg_lower_fwd"], a["hg_lower_bwd"]], axis=1)
    cond = _np.stack([a["c"][0], a["c_ctx"]], axis=0)
    vec = _np.concatenate([
        cols(a["b_ada"]), cols(a["norm1_g"]), cols(a["norm2_g"]), cols(a["final_g"]), cols(lower),
        _np.ascontiguousarray(a["hg_norm_g"].T),
        _np.moveaxis(cond.reshape(2, KT, P), 2, 0).transpose(0, 2, 1).reshape(P, 2 * KT),
        _np.broadcast_to(a["router_bias"], (P, N_EXPERTS)),
        _np.broadcast_to(_np.arange(4, dtype=_np.float32), (P, 4)),
    ], axis=1)
    assert vec.shape == (P, VEC_N), vec.shape
    const, levmask = constants()
    arrays = {
        "xT": _np.concatenate([a["ctx"][0], a["x"][0]], axis=0).T, "vec": vec, "const": const, "levmask": levmask,
        "rel_bias_reversed": a["na_rel_bias"][..., ::-1],
    }
    for n in ("w_ada", "w_in", "w_na_o", "w_hg_o", "w_out", "w_router", "w_gate", "w_up", "w_down"):
        arrays[n] = a[n]
    arrays = {n: _np.ascontiguousarray(x) for n, x in arrays.items()}
    nc = _bacc.Bacc("TRN2", target_bir_lowering=False, num_devices=1, dynamic_dma_scratch_size=1024)
    aps = {n: nc.dram_tensor(f"in_{n}", x.shape, _mybir.dt.from_np(x.dtype), kind="ExternalInput").ap()
           for n, x in arrays.items()}
    out = nc.dram_tensor("out_yT", (D, SEG), _mybir.dt.float32, kind="ExternalOutput").ap()
    build(nc, aps, out)
    r = _run(nc, [{f"in_{n}": x for n, x in arrays.items()}], core_ids=[0])
    return r.results[0]["out_yT"].T[None]
```

```python
import numpy as np
import concourse.bass as bass
from concourse import mybir
from contextlib import ExitStack

D = 1024
SEG = 256
TOK = 2 * SEG
DEPTH = 2
P = 128
KT = D // P
GRID_W = 64
WIN_COLS = 16
NA_HEADS = 8
NA_DIM = 64
HG_HEADS = 4
EPS = 1e-6
N_EXPERTS = 16
N_GROUPS = 4
PER_GROUP = N_EXPERTS // N_GROUPS
FF = 512
SLOTS = 4
SLOT = 4096
LEVELS = 7
GATE_FLOOR = 1e-30
MASKED = -1e30
CAPACITY = 128

VEC_BADA = 0
VEC_N1 = VEC_BADA + DEPTH * 48
VEC_N2 = VEC_N1 + DEPTH * KT
VEC_FINAL = VEC_N2 + DEPTH * KT
VEC_LOWER = VEC_FINAL + KT
VEC_HGAIN = VEC_LOWER + 2 * DEPTH * HG_HEADS
VEC_COND = VEC_HGAIN + DEPTH
VEC_RBIAS = VEC_COND + 2 * KT
VEC_GIDX = VEC_RBIAS + N_EXPERTS
VEC_N = VEC_GIDX + 4
C_IDENT, C_ONES, C_ROT, C_COS, C_SIN, C_WMUL, C_WNEG, C_IOTA, C_BEFORE = 0, 128, 256, 384, 640, 896, 960, 1024, 1152
C_N = 1280


def build(nc, A, out, stop=99):
    f32, f32r, u8, i32 = mybir.dt.float32, mybir.dt.float32r, mybir.dt.uint8, mybir.dt.int32
    ALU, ACT, AX = mybir.AluOpType, mybir.ActivationFunctionType, mybir.AxisListType
    V, S, G, T = nc.vector, nc.scalar, nc.gpsimd, nc.tensor

    at = [(nc.sbuf_base + 31) // 32 * 32]

    def fixed(name, shape, dtype=f32, offset=None):
        size = int(np.prod(shape[1:])) * (1 if dtype == u8 else 4)
        where = at[0] if offset is None else offset
        if offset is None:
            at[0] += (size + 31) // 32 * 32
        return nc.alloc_sbuf_tensor_at(name, shape, dtype, offset=where)

    xT = fixed("xT", [P, KT, TOK])
    hT = fixed("hT", [P, KT, TOK])
    ring = fixed("ring", [P, SLOTS, SLOT])
    const = fixed("const", [P, C_N])
    levmask = fixed("levmask", [P, 2 * LEVELS, P], u8)
    vec = fixed("vec", [P, VEC_N])
    router = fixed("router", [P, KT, N_EXPERTS])
    cond = fixed("cond", [P, KT, 2])
    mod = fixed("mod", [P, DEPTH, 48, 2])
    gain1 = fixed("gain1", [P, DEPTH, KT, 2])
    gain2 = fixed("gain2", [P, DEPTH, KT, 2])
    lower = fixed("lower", [P, 2, DEPTH, HG_HEADS])
    upper = fixed("upper", [P, 2, DEPTH, HG_HEADS])
    lowtmp = fixed("lowtmp", [P, 8, 2, HG_HEADS])
    over_at = N_EXPERTS + 1
    place = fixed("place", [P, 4, over_at + 3 * N_EXPERTS + 1])
    weight = fixed("weight", [P, 4, over_at + 3 * N_EXPERTS + 1])
    crowd = fixed("crowd", [P, 1])
    crowd_int = fixed("crowd_int", [P, 1], mybir.dt.int32)
    chosen = fixed("chosen", [P, 4, N_EXPERTS])
    slot_weight = fixed("slot_weight", [P, 2])
    epsv = fixed("epsv", [P, 1])
    adarow = fixed("adarow", [2, 2, 512])
    rstd = fixed("rstd", [P, TOK])
    narow = fixed("narow", [P, 3, 4])
    ident = const[:, C_IDENT:C_IDENT + P]
    ones = const[:, C_ONES:C_ONES + P]
    rot = const[:, C_ROT:C_ROT + P]
    cos = const[:, C_COS:C_COS + SEG]
    sin = const[:, C_SIN:C_SIN + SEG]
    wmul = const[:, C_WMUL:C_WMUL + GRID_W]
    iota = const[:, C_IOTA:C_IOTA + P]
    later = const[:, C_BEFORE:C_BEFORE + P]
    wneg = const[:, C_WNEG:C_WNEG + GRID_W]

    A0 = at[0]
    KB = 1024
    qh = fixed("qh", [P, 8, SEG], offset=A0)
    kf = fixed("kf", [P, 8, SEG], offset=A0 + 8 * KB)
    kb = fixed("kb", [P, 8, SEG], offset=A0 + 16 * KB)
    pf = fixed("pf", [P, 8, SEG + 1], offset=A0 + 24 * KB)
    pb = fixed("pb", [P, 8, SEG + 1], offset=A0 + 24 * KB + 8224)
    vh = fixed("vh", [P, 4, 512], offset=A0 + 24 * KB + 2 * 8224)
    B0 = A0 + 32 * KB + 2 * 8224
    att = fixed("att", [P, HG_HEADS, 2, 2, SEG], offset=B0)
    attx = fixed("attx", [P, HG_HEADS, 2, SEG], offset=B0 + 16 * KB)
    dec = [fixed(f"dec{i}", [P, 4, SEG], offset=B0 + 24 * KB + i * 4 * KB) for i in range(2)]
    fac = [fixed(f"fac{i}", [P, 4, SEG], offset=B0 + 32 * KB + i * 4 * KB) for i in range(2)]
    C0 = B0 + 40 * KB
    naq = fixed("naq", [P, 4, TOK], offset=C0)
    nak = fixed("nak", [P, 4, TOK], offset=C0 + 8 * KB)
    roped = fixed("roped", [P, 2, SEG], offset=A0 + 24 * KB + 2 * 8224)
    END = C0 + 16 * KB
    assert END <= nc.sbuf_usable_end, (END, nc.sbuf_usable_end)
    sig = fixed("sig", [P, 8 * SEG], offset=B0 + 24 * KB)
    small = fixed("small", [P, 8 * SEG], offset=B0 + 32 * KB)
    logs = fixed("logs", [P, 8 * SEG], offset=B0)
    onescan = fixed("onescan", [P, SEG], offset=B0 + 8 * KB)
    oh = fixed("oh", [P, HG_HEADS, TOK], offset=A0 + 8 * KB)
    hgate = fixed("hgate", [P, HG_HEADS, TOK], offset=A0 + 16 * KB)
    navv = fixed("navv", [P, 4, 512], offset=A0)
    ona = fixed("ona", [P, 4, TOK], offset=A0 + 24 * KB)
    pt = [fixed(f"pt{i}", [P, 4, SEG], offset=A0 + 32 * KB + 4 * KB * i) for i in range(2)]
    bias = fixed("bias", [P, NA_HEADS, 2, 4 * GRID_W], offset=B0 + 24 * KB)
    levmask_f = fixed("levmask_f", [P, 2 * LEVELS, P], offset=A0)
    bias_skew = fixed("bias_skew", [P, NA_HEADS, 2, 4 * GRID_W], offset=B0)
    probs = [fixed(f"probs{i}", [P, TOK], offset=B0 + 16 * KB + 2 * KB * i) for i in range(3)]
    square = fixed("square", [P, 2, TOK], offset=C0 + 8 * KB)
    normed = fixed("normed", [P, 2, TOK], offset=C0 + 12 * KB)
    osq = fixed("osq", [P, 2, TOK], offset=C0)
    ors = fixed("ors", [P, 2, TOK], offset=C0 + 4 * KB)
    merged = fixed("merged", [P, KT, TOK], offset=B0)
    gsig = fixed("gsig", [P, 2, TOK], offset=C0 + 8 * KB)
    gmul = fixed("gmul", [P, 2, TOK], offset=C0 + 12 * KB)
    hrow_hi = fixed("hrow_hi", [P, 4, D], f32r, offset=A0)
    hrow_lo = fixed("hrow_lo", [P, 4, D], f32r, offset=A0 + 16 * KB)
    y_hi = fixed("y_hi", [P, 4, D], f32r, offset=A0 + 32 * KB)
    y_lo = fixed("y_lo", [P, 4, D], f32r, offset=A0 + 48 * KB)
    spread = fixed("spread", [P, 4, TOK], f32r, offset=A0 + 64 * KB)
    picked = fixed("picked", [P, KT, P], offset=A0 + 72 * KB)
    pick = fixed("pick", [P, 2, 4, P], f32r, offset=A0 + 76 * KB)
    pickw = fixed("pickw", [P, 2, 4, P], offset=A0 + 80 * KB)
    silu = fixed("silu", [P, FF], offset=A0 + 84 * KB)
    acts = fixed("acts", [P, FF], offset=A0 + 86 * KB)
    acts_t = fixed("acts_t", [P, 4, P], offset=A0 + 88 * KB)
    unused = fixed("unused", [P, TOK], offset=A0 + 90 * KB)
    R0 = A0 + 92 * KB
    rt = [fixed(f"rt{i}", [P, 4, N_GROUPS, PER_GROUP], offset=R0 + 256 * i) for i in range(12)]
    assert R0 + 3 * KB <= END

    names = """const_loaded vec_loaded x_loaded bias_loaded out_stored psum_ready cond_ready ada_row ada_mod
        epsv_ready gains_ready lower_ready square_ready square_used norm_std rstd_ready normed_ready h_ready q_ready
        sig_ready k_sig gates_ready log_in log_out v_ready naqk_ready rope_done decay_in decay_out fac_ready
        att_block oh_ready osq_ready hg_std og_ready hgate_ready nav_ready bias_ready na_z na_max na_p na_pn
        na_pt na_o gate_sig merged_ready x_updated route_done chosen_ready place_ready crowd_ready over_ready
        hrow_hi_ready hrow_ready gathered pickw_turned gate_done up_done act_turned y_done scattered
        pick_ready spread_ready act_ready y_lo_ready x_added pick_bare picked_ready slot_weight_ready silu_ready
        acts_t_ready y_hi_ready dve_chain act_chain pool_chain pool_ready""".split()
    with ExitStack() as ctx:
        sem = {n: ctx.enter_context(nc.semaphore(n)) for n in names}
        slot_full = [ctx.enter_context(nc.semaphore(f"slot_full{i}")) for i in range(SLOTS)]
        bank = [ctx.enter_context(nc.psum_tensor(f"bank{i}", [P, 512], f32)) for i in range(8)]
        block = ctx.enter_context(nc.Block())

        loads = []

        def slot_of(key):
            return loads.index(key)

        for l in range(DEPTH):
            loads += [("ada", l, s) for s in range(12)]
        for l in range(DEPTH):
            loads += [("in", l, s) for s in (3, 4, 5, 6, 0, 1, 2, 7)]
            loads += [("nao", l), ("in", l, 8), ("in", l, 9), ("hgo", l), ("in", l, 10), ("in", l, 11)]
            loads += [("out", l, 0), ("out", l, 1)]
            assert len(loads) % SLOTS == 0
            for ph, n in ((2 * l, N_EXPERTS), (2 * l + 1, 3 * N_EXPERTS if l == 0 else N_EXPERTS)):
                loads += [("moe", ph, e, k) for e in range(n) for k in range(3)]

        def slot(key):
            return ring[:, slot_of(key) % SLOTS, :]

        def full(key):
            n = slot_of(key)
            return slot_full[n % SLOTS], 16 * (n // SLOTS + 1)

        ready, reader, last_use, spent = {}, {}, {}, {}
        in_bank = [None] * 8
        counts = {}
        slot_spent = {}
        jobs = [0]

        def read_by(key):
            return sem[reader[key][0]], reader[key][1]

        def is_ready(key):
            return sem["psum_ready"], ready[key][1]

        def result(key):
            return bank[ready[key][0]]

        scatter_bank = (0, 1, 5, 6, 7, 0, 1, 5)
        segs_of = {0: (0, 1), 1: (1,)}

        phases = []
        for l in range(DEPTH):
            rounds_left = (len(segs_of[l]) * SEG + CAPACITY - 1) // CAPACITY - 1
            phases += [(0, N_EXPERTS), (over_at, N_EXPERTS * rounds_left)]
        signals = {"gathered": (2, 1), "pickw_turned": (1, 1), "gate_done": (1, 0), "up_done": (1, 0),
                   "act_turned": (1, 0), "y_done": (2, 0), "scattered": (2, 0),
                   "pick_bare": (1, 1), "pick_ready": (1, 1), "spread_ready": (1, 0), "act_ready": (1, 0),
                   "y_lo_ready": (2, 0), "x_added": (2, 0),
                   "picked_ready": (2, 1), "slot_weight_ready": (1, 1), "silu_ready": (1, 0),
                   "acts_t_ready": (1, 0), "y_hi_ready": (2, 0)}
        signalled_by = {
            "pe": ("gathered", "pickw_turned", "gate_done", "up_done", "act_turned", "y_done", "scattered"),
            "dve": ("pick_bare", "pick_ready", "spread_ready", "act_ready", "y_lo_ready", "x_added"),
            "act": ("picked_ready", "slot_weight_ready", "silu_ready", "acts_t_ready", "y_hi_ready")}

        def worth(ph, name):
            per, more = signals[name]
            return per * (phases[ph][1] + more + 4)

        def total(ph, i, name, e, k):
            per = signals[name][0]
            static = sum(worth(p, name) for p in range(ph)) + 4 * per + per * e + k
            return sem[name], (static if i is None else i * (4 * per) + static)

        def open_phase(engine, who):
            for name in signalled_by[who]:
                engine.sem_inc(sem[name], 4 * signals[name][0])

        def close_phase(engine, who, ph):
            for name in signalled_by[who]:
                per, more = signals[name]
                engine.wait_ge(*total(ph, None, name, phases[ph][1] + more - 1, per))

        def skip_phase(engine, who, ph):
            for name in signalled_by[who]:
                engine.sem_inc(sem[name], worth(ph, name))

        @block.tensor
        def _(pe):
            def open_bank(key, who):
                b = jobs[0] % 8
                jobs[0] += 1
                if in_bank[b] is not None:
                    pe.wait_ge(*read_by(in_bank[b]))
                in_bank[b] = key
                counts[who] = counts.get(who, 0) + 1
                ready[key] = (b, jobs[0])
                reader[key] = (who, counts[who])
                return bank[b]

            pe.wait_ge(sem["const_loaded"], 16)
            pe.wait_ge(sem["cond_ready"], 1)

            def ada_rows(l, s):
                pe.wait_ge(*full(("ada", l, s)))
                w = slot(("ada", l, s)).rearrange("p (k n) -> p k n", k=KT)
                o = open_bank(("ada", l, s), "ada_row")
                for k in range(KT):
                    mm = T.matmul(o[0:2, :], cond[:, k, :], w[:, k, :], start=(k == 0), stop=(k == KT - 1))
                mm.then_inc(sem["psum_ready"], 1)
                slot_spent[slot_of(("ada", l, s))] = (sem["psum_ready"], jobs[0])

            def ada_turn(l, s):
                o = open_bank(("adaT", l, s), "ada_mod")
                pe.wait_ge(*read_by(("ada", l, s)))
                n = (l * 12 + s) % 2
                for j in range(4):
                    mm = T.transpose(o[:, 2 * j:2 * j + 2], adarow[:, n, j * P:(j + 1) * P], ident[0:2, 0:2])
                mm.then_inc(sem["psum_ready"], 1)

            for n in range(DEPTH * 12 + 1):
                if n < DEPTH * 12:
                    ada_rows(n // 12, n % 12)
                if n:
                    ada_turn((n - 1) // 12, (n - 1) % 12)

            def mean_square(key, count, lo):
                o = open_bank(key, "norm_std")
                for k in range(KT):
                    pe.wait_ge(sem["square_ready"], count * KT + k + 1)
                    mm = T.matmul(o[:, lo:TOK], ones, square[:, k % 2, lo:TOK], start=(k == 0), stop=(k == KT - 1))
                    if k < KT - 1:
                        mm.then_inc(sem["square_used"], 1)
                mm.then_inc(sem["psum_ready"], 1)

            def project(l, s, c, who, lo):
                w = slot(("in", l, s)).rearrange("p (k n) -> p k n", k=KT)
                o = open_bank(("in", l, s, c), who)
                for k in range(KT):
                    mm = T.matmul(o[:, lo:TOK], w[:, k, c * P:(c + 1) * P], hT[:, k, lo:TOK],
                                  start=(k == 0), stop=(k == KT - 1))
                mm.then_inc(sem["psum_ready"], 1)
                if c == 3:
                    slot_spent[slot_of(("in", l, s))] = (sem["psum_ready"], jobs[0])

            def project_rows(l, s, t, who):
                w = slot(("in", l, s)).rearrange("p (k n) -> p k n", k=KT)
                o = open_bank(("in", l, s, t), who)
                for k in range(KT):
                    mm = T.matmul(o[:, :], hT[:, k, t * P:(t + 1) * P], w[:, k, :], start=(k == 0), stop=(k == KT - 1))
                mm.then_inc(sem["psum_ready"], 1)
                if t == 3:
                    slot_spent[slot_of(("in", l, s))] = (sem["psum_ready"], jobs[0])

            units_before = [0]
            rounds = {"norm": 0, "square_used": 0}
            for l in range(DEPTH):
                if stop <= 10 * l + 1:
                    break
                lo = 0 if l == 0 else SEG
                segs = segs_of[l]
                mean_square(("ms", l, 0), 2 * l, 0)
                pe.wait_ge(sem["h_ready"], KT * (2 * l + 1))
                for s, who in ((3, "q_ready"), (4, "k_sig"), (5, "k_sig")):
                    pe.wait_ge(*full(("in", l, s)))
                    for c in range(4):
                        project(l, s, c, who, lo if s == 3 else 0)
                pe.wait_ge(*full(("in", l, 6)))
                for t in range(4):
                    project_rows(l, 6, t, "v_ready")
                if stop <= 10 * l + 2:
                    break

                extra = [(s, c) for s in (0, 1) for c in range(4)]

                def between():
                    if not extra:
                        return
                    s, c = extra.pop(0)
                    if c == 0:
                        pe.wait_ge(*full(("in", l, s)))
                    project(l, s, c, "naqk_ready", lo if s == 0 else 0)

                u = 38 * l
                for hp in range(2):
                    for unit in range(19):
                        pe.wait_ge(sem["fac_ready"], u + 1)
                        f = fac[u % 2]
                        lev, way = (unit - 1) // 2, (unit - 1) % 2
                        if lev < LEVELS:
                            for h in range(2):
                                o = open_bank(("lev", l, u, h), "att_block")
                                for i, sg in enumerate(segs):
                                    for b in range(2):
                                        left = f[:, h * len(segs) + i, b * P:(b + 1) * P]
                                        right = qh[:, 2 * (2 * hp + h) + sg, b * P:(b + 1) * P] if unit == 0 else left
                                        mm = T.matmul(o[:, (2 * i + b) * P:(2 * i + b + 1) * P], left, right,
                                                      start=True, stop=True)
                                mm.then_inc(sem["psum_ready"], 1)
                        elif lev == LEVELS:
                            o = open_bank(("lev", l, u, 0), "att_block")
                            for h in range(2):
                                for i in range(len(segs)):
                                    j = h * len(segs) + i
                                    halves = f[:, j, 0:P], f[:, j, P:SEG]
                                    mm = T.matmul(o[:, j * P:(j + 1) * P], halves[way], halves[1 - way],
                                                  start=True, stop=True)
                            mm.then_inc(sem["psum_ready"], 1)
                        elif way == 1:
                            g = fac[(u - 1) % 2]
                            for h in range(2):
                                o = open_bank(("cross", l, hp, h), "att_block")
                                for sb in range(2):
                                    for n, x in enumerate((g, f)):
                                        mm = T.matmul(o[:, sb * SEG:(sb + 1) * SEG], x[:, 2 * h, sb * P:(sb + 1) * P],
                                                      x[:, 2 * h + 1, :], start=(n == 0), stop=(n == 1))
                                mm.then_inc(sem["psum_ready"], 1)
                        spent[u] = jobs[0]
                        if lev > LEVELS and way == 1:
                            spent[u - 1] = jobs[0]
                        u += 1
                        if unit % 4 == 3:
                            between()
                while extra:
                    between()

                pe.wait_ge(*read_by(("cross", l, 1, 1)))
                for h in range(HG_HEADS):
                    o = open_bank(("o", l, h), "oh_ready")
                    for sg in segs:
                        terms = [(2 * sg + sb, att[:, h, sg, sb, :]) for sb in range(2)]
                        if sg == 1:
                            terms = [(sb, attx[:, h, sb, :]) for sb in range(2)] + terms
                        for n, (t, a) in enumerate(terms):
                            mm = T.matmul(o[:, sg * SEG:(sg + 1) * SEG], vh[:, t, h * P:(h + 1) * P], a,
                                          start=(n == 0), stop=(n == len(terms) - 1))
                    mm.then_inc(sem["psum_ready"], 1)
                if stop <= 10 * l + 3:
                    break

                pe.wait_ge(*full(("in", l, 2)))
                for t in range(4):
                    project_rows(l, 2, t, "nav_ready")
                for n in range(8):
                    buf = (naq, nak)[n // 4]
                    o = open_bank(("rot", l, n), "rope_done")
                    pe.wait_ge(sem["naqk_ready"], 8 * l + n + 1)
                    T.matmul(o[:, 0:SEG], rot, buf[:, n % 4, SEG:TOK], start=True, stop=True)\
                        .then_inc(sem["psum_ready"], 1)
                pe.wait_ge(*full(("in", l, 7)))
                for c in range(4):
                    project(l, 7, c, "hgate_ready", lo)
                pe.wait_ge(sem["rope_done"], 8 * (l + 1))

                tiles = [(h, q) for h in range(NA_HEADS) for sg in segs for q in (2 * sg, 2 * sg + 1)]
                per = len(tiles)
                before = 0 if l == 0 else NA_HEADS * 4
                for n in range(per + 4):
                    if n < per:
                        h, q = tiles[n]
                        r = 64 * (h % 2)
                        nk = SEG if q < 2 else TOK
                        o = open_bank(("S", l, n), "na_z")
                        T.matmul(o[:, 0:nk], naq[r:r + 64, h // 2, q * P:(q + 1) * P], nak[r:r + 64, h // 2, 0:nk],
                                 start=True, stop=True).then_inc(sem["psum_ready"], 1)
                    m = n - 2
                    if 0 <= m < per:
                        h, q = tiles[m]
                        o = open_bank(("TR", l, m), "na_pt")
                        pe.wait_ge(sem["na_pn"], before + m + 1)
                        for k in range(2 if q < 2 else 4):
                            mm = T.transpose(o[:, k * P:(k + 1) * P], probs[(before + m) % 3][:, k * P:(k + 1) * P], ident)
                        mm.then_inc(sem["psum_ready"], 1)
                    m = n - 4
                    if m >= 0 and m % 2 == 1:
                        h, q = tiles[m]
                        r = 64 * (h % 2)
                        o = open_bank(("PV", l, m // 2), "na_o")
                        pe.wait_ge(*read_by(("TR", l, m)))
                        nk = 2 if q < 2 else 4
                        for k in range(nk):
                            mm = T.matmul(o[r:r + 64, 0:SEG], navv[:, k, h * 64:(h + 1) * 64],
                                          pt[(m // 2) % 2][:, k, :], start=(k == 0), stop=(k == nk - 1))
                        mm.then_inc(sem["psum_ready"], 1)
                h, q = tiles[per - 1]
                if stop <= 10 * l + 4:
                    break

                for h in range(HG_HEADS):
                    o = open_bank(("oms", l, h), "hg_std")
                    pe.wait_ge(sem["osq_ready"], 4 * l + h + 1)
                    T.matmul(o[:, lo:TOK], ones, osq[:, h % 2, lo:TOK], start=True, stop=True)\
                        .then_inc(sem["psum_ready"], 1)

                for br, (first, wo, src) in enumerate(((8, "nao", ona), (10, "hgo", oh))):
                    pe.wait_ge(*full((wo, l)))
                    if br == 0:
                        pe.wait_ge(*read_by(("PV", l, per // 2 - 1)))
                    else:
                        pe.wait_ge(sem["og_ready"], 4 * (l + 1))
                    w = slot((wo, l)).rearrange("p (k n) -> p k n", k=4)
                    for d in range(KT):
                        if d % 4 == 0:
                            pe.wait_ge(*full(("in", l, first + d // 4)))
                        project(l, first + d // 4, d % 4, "gate_sig", lo)
                        o = open_bank(("y", l, br, d), "merged_ready")
                        for k in range(4):
                            mm = T.matmul(o[:, lo:TOK], w[:, k, d * P:(d + 1) * P], src[:, k, lo:TOK],
                                          start=(k == 0), stop=(k == 3))
                        mm.then_inc(sem["psum_ready"], 1)
                    slot_spent[slot_of((wo, l))] = (sem["psum_ready"], jobs[0])
                pe.wait_ge(sem["merged_ready"], 16 * (l + 1))
                for d in range(KT):
                    key = ("out", l, d // 4)
                    if d % 4 == 0:
                        pe.wait_ge(*full(key))
                    w = slot(key).rearrange("p (k n) -> p k n", k=KT)
                    o = open_bank(("out", l, d), "x_updated")
                    for k in range(KT):
                        mm = T.matmul(o[:, lo:TOK], w[:, k, (d % 4) * P:(d % 4 + 1) * P], merged[:, k, lo:TOK],
                                      start=(k == 0), stop=(k == KT - 1))
                    mm.then_inc(sem["psum_ready"], 1)
                    if d % 4 == 3:
                        slot_spent[slot_of(key)] = (sem["psum_ready"], jobs[0])
                if stop <= 10 * l + 5:
                    break

                mean_square(("ms", l, 1), 2 * l + 1, lo)
                pe.wait_ge(sem["h_ready"], KT * (2 * l + 2))
                o = open_bank(("route", l), "route_done")
                for t in range(2 * (l > 0), 4):
                    for k in range(KT):
                        mm = T.matmul(o[:, t * N_EXPERTS:(t + 1) * N_EXPERTS], hT[:, k, t * P:(t + 1) * P],
                                      router[:, k, :], start=(k == 0), stop=(k == KT - 1))
                mm.then_inc(sem["psum_ready"], 1)
                for t in range(2 * (l > 0), 4):
                    for half in range(2):
                        o = open_bank(("rows", l, t, half), "hrow_ready")
                        for j in range(4):
                            mm = T.transpose(o[:, j * P:(j + 1) * P], hT[:, 4 * half + j, t * P:(t + 1) * P], ident)
                        mm.then_inc(sem["psum_ready"], 1)
                o = open_bank(("place", l), "place_ready")
                pe.wait_ge(sem["chosen_ready"], l + 1)
                for t in range(2 * (l > 0), 4):
                    for s in range(2 * (l > 0), t + 1):
                        mm = T.matmul(o[:, t * N_EXPERTS:(t + 1) * N_EXPERTS], later if s == t else ones,
                                      chosen[:, s, :], start=(s == 2 * (l > 0)), stop=(s == t))
                for t in range(2 * (l > 0), 4):
                    mm = T.matmul(o[:, 4 * N_EXPERTS:5 * N_EXPERTS], ones, chosen[:, t, :],
                                  start=(t == 2 * (l > 0)), stop=(t == 3))
                mm.then_inc(sem["psum_ready"], 1)

                for b in range(8):
                    pe.wait_ge(*read_by(in_bank[b]))
                tiles = list(range(2 * (l > 0), 4))

                pe.wait_ge(sem["hrow_ready"], (8, 12)[l])
                pe.wait_ge(sem["crowd_ready"], l + 1)
                crowded = pe.value_load(crowd_int[0:1, 0:1])

                def experts(ph):
                    def gather(i, e, half):
                        pe.wait_ge(*total(ph, i, "pick_ready", e, 1))
                        pe.wait_ge(*total(ph, i, "picked_ready", e - 1, half + 1))
                        o = bank[2 + half]
                        for j in range(4):
                            d = 4 * half + j
                            for n, (t, rows) in enumerate([(t, rows) for t in tiles for rows in (hrow_hi, hrow_lo)]):
                                mm = T.matmul(o[:, j * P:(j + 1) * P], rows[:, t, d * P:(d + 1) * P], pick[:, e % 2, t, :],
                                              start=(n == 0), stop=(n == 2 * len(tiles) - 1))
                        mm.then_inc(sem["gathered"], 1)

                    def turn_pick(i, e):
                        pe.wait_ge(*total(ph, i, "spread_ready", e - 1, 1))
                        pe.wait_ge(*total(ph, i, "slot_weight_ready", e - 1, 1))
                        for t in tiles:
                            mm = T.transpose(bank[4][:, t * P:(t + 1) * P], pickw[:, e % 2, t, :], ident)
                        mm.then_inc(sem["pickw_turned"], 1)

                    base = slot_of(("moe", ph, 0, 0))
                    open_phase(pe, "pe")
                    for half in range(2):
                        gather(None, 0, half)
                    turn_pick(None, 0)
                    with pe.Fori(0, phases[ph][1] // 4) as i:
                        for e in range(4):
                            for g, name in enumerate(("gate_done", "up_done")):
                                s = (base + 3 * e + g) % SLOTS
                                pe.wait_ge(slot_full[s], i * 48 + 16 * ((base + 3 * e + g) // SLOTS + 1))
                                if e == 0:
                                    pe.wait_ge(*total(ph, i, "x_added", -4, 6 + g))
                                else:
                                    pe.wait_ge(*total(ph, i, ("silu_ready", "act_ready")[g], e - 1, 1))
                                if g == 0:
                                    pe.wait_ge(*total(ph, i, "picked_ready", e, 2))
                                w = ring[:, s, :].rearrange("p (k n) -> p k n", k=KT)
                                for k in range(KT):
                                    mm = T.matmul(bank[g][:, :], picked[:, k, :], w[:, k, :], start=(k == 0), stop=(k == KT - 1))
                                mm.then_inc(sem[name], 1)
                            gather(i, e + 1, 0)
                            pe.wait_ge(*total(ph, i, "act_ready", e, 1))
                            if e == 0:
                                pe.wait_ge(*total(ph, i, "x_added", -4, 8))
                            else:
                                pe.wait_ge(*total(ph, i, "acts_t_ready", e - 1, 1))
                            for j in range(4):
                                mm = T.transpose(bank[5][:, j * P:(j + 1) * P], acts[:, j * P:(j + 1) * P], ident)
                            mm.then_inc(sem["act_turned"], 1)
                            gather(i, e + 1, 1)
                            turn_pick(i, e + 1)
                            s = (base + 3 * e + 2) % SLOTS
                            pe.wait_ge(slot_full[s], i * 48 + 16 * ((base + 3 * e + 2) // SLOTS + 1))
                            pe.wait_ge(*total(ph, i, "acts_t_ready", e, 1))
                            w = ring[:, s, :].rearrange("p (k n) -> p k n", k=4)
                            for half in range(2):
                                if e == 0:
                                    pe.wait_ge(*total(ph, i, "x_added", -4, 4 + half))
                                else:
                                    pe.wait_ge(*total(ph, i, "y_hi_ready", e - 1, half + 1))
                                    pe.wait_ge(*total(ph, i, "y_lo_ready", e - 1, half + 1))
                                for k in range(4):
                                    mm = T.matmul(bank[6 + half][:, :], acts_t[:, k, :], w[:, k, half * 512:(half + 1) * 512],
                                                  start=(k == 0), stop=(k == 3))
                                mm.then_inc(sem["y_done"], 1)
                        pe.wait_ge(*total(ph, i, "y_hi_ready", 3, 2))
                        pe.wait_ge(*total(ph, i, "y_lo_ready", 3, 2))
                        for d in range(KT):
                            if d >= 5:
                                pe.wait_ge(*total(ph, i, "x_added", 0, d - 4))
                            o = bank[scatter_bank[d]]
                            for n, (e, y) in enumerate([(e, y) for e in range(4) for y in (y_hi, y_lo)]):
                                mm = T.matmul(o[:, lo:TOK], y[:, e, d * P:(d + 1) * P], spread[:, e, lo:TOK],
                                              start=(n == 0), stop=(n == 7))
                            mm.then_inc(sem["scattered"], 1)
                experts(2 * l)
                close_phase(pe, "pe", 2 * l)
                with pe.If(crowded > CAPACITY):
                    experts(2 * l + 1)
                with pe.Else():
                    skip_phase(pe, "pe", 2 * l + 1)
                for ph in (2 * l, 2 * l + 1):
                    for m in range(3 * phases[ph][1]):
                        name, k = (("gate_done", 1), ("up_done", 1), ("y_done", 2))[m % 3]
                        slot_spent[slot_of(("moe", ph, 0, 0)) + m] = total(ph, None, name, m // 3, k)
                last = phases[ph][1] - 1
                for b in range(8):
                    in_bank[b] = ("experts", l, b)
                    name, e, k = ("x_added", last, 2) if b in scatter_bank else \
                        ("picked_ready", last + 1, 2) if b < 4 else ("slot_weight_ready", last + 1, 1)
                    reader["experts", l, b] = (name, total(ph, None, name, e, k)[1])
            if stop > 30:
                mean_square(("ms", 2, 0), 4, SEG)

        @block.sync
        def _(sp):
            sp.dma_start(vec[:], A["vec"]).then_inc(sem["vec_loaded"], 16)
            sp.dma_start(const[:], A["const"]).then_inc(sem["const_loaded"], 16)

            def source(key):
                if key[0] == "ada":
                    return A["w_ada"][key[1], :, key[2] * 512:(key[2] + 1) * 512].rearrange("(k p) n -> p k n", p=P), KT
                if key[0] == "in":
                    return A["w_in"][key[1], :, key[2] * 512:(key[2] + 1) * 512].rearrange("(k p) n -> p k n", p=P), KT
                if key[0] == "out":
                    return A["w_out"][key[1], :, key[2] * 512:(key[2] + 1) * 512].rearrange("(k p) n -> p k n", p=P), KT
                return A["w_na_o" if key[0] == "nao" else "w_hg_o"][key[1]].rearrange("(k p) n -> p k n", p=P), 4

            def fill(n):
                src, k = source(loads[n])
                sp.dma_start(ring[:, n % SLOTS, :].rearrange("p (k n) -> p k n", k=k), src)\
                    .then_inc(slot_full[n % SLOTS], 16)

            for n in range(SLOTS):
                fill(n)
            sp.dma_start(xT[:], A["xT"].rearrange("(k p) n -> p k n", p=P)).then_inc(sem["x_loaded"], 16)
            sp.dma_start(levmask_f[:], A["levmask"]).then_inc(sem["x_loaded"], 16)
            sp.dma_start(router[:], A["w_router"].rearrange("(k p) n -> p k n", p=P)).then_inc(sem["x_loaded"], 16)
            n = SLOTS
            for l in range(DEPTH):
                base = slot_of(("moe", 2 * l, 0, 0))
                while n < base:
                    if n - SLOTS not in slot_spent:
                        break
                    sp.wait_ge(*slot_spent[n - SLOTS])
                    fill(n)
                    n += 1
                if n < base or ("place", l) not in ready:
                    break
                w = (A["w_gate"], A["w_up"], A["w_down"])
                flat = [x.rearrange("l e (k p) n -> (l e) p k n", p=P) for x in w]

                def fill_expert(m, expert):
                    s, k = (base + m) % SLOTS, (KT, KT, 4)[m % 3]
                    src = flat[m % 3][expert] if isinstance(expert, int) else flat[m % 3][expert, :, :, :]
                    sp.dma_start(ring[:, s, :].rearrange("p (k n) -> p k n", k=k), src).then_inc(slot_full[s], 16)

                def fill_spent(ph, i, e, m):
                    name, k = (("gate_done", 1), ("up_done", 1), ("y_done", 2))[(m - SLOTS) % 3]
                    sp.wait_ge(*total(ph, i, name, e + (m - SLOTS) // 3, k))

                for m in range(SLOTS):
                    sp.wait_ge(*slot_spent[base + m - SLOTS])
                    fill_expert(m, l * N_EXPERTS + m // 3)
                with sp.Fori(0, N_EXPERTS // 4 - 1) as i:
                    for m in range(SLOTS, SLOTS + 12):
                        fill_spent(2 * l, i, 0, m)
                        fill_expert(m, i * 4 + (l * N_EXPERTS + m // 3))
                for m in range(SLOTS + 36, 48):
                    fill_spent(2 * l, None, 0, m)
                    fill_expert(m, l * N_EXPERTS + m // 3)
                sp.wait_ge(sem["crowd_ready"], l + 1)
                crowded = sp.value_load(crowd_int[0:1, 0:1])
                with sp.If(crowded > CAPACITY):
                    for e in range(0, phases[2 * l + 1][1], N_EXPERTS):
                        with sp.Fori(0, N_EXPERTS // 4) as i:
                            for m in range(12):
                                fill_spent(2 * l + 1, i, e, m)
                                fill_expert(m, i * 4 + (l * N_EXPERTS + m // 3))
                with sp.Else():
                    for i in range(SLOTS):
                        sp.wait_ge(slot_full[i], 16 * ((base + 48) // SLOTS))
                        sp.sem_inc(slot_full[i], 16 * 3 * phases[2 * l + 1][1] // SLOTS)
                n = base + 48 + 3 * phases[2 * l + 1][1]
            if stop <= 30:
                for i in range(SLOTS):
                    sp.wait_ge(slot_full[i], 16 * sum(1 for m in range(n) if m % SLOTS == i))
                sp.wait_ge(sem["x_loaded"], 48)
            if stop > 30:
                for k in range(KT):
                    sp.wait_ge(sem["h_ready"], KT * 4 + k + 1)
                    sp.dma_start(out[k * P:(k + 1) * P, :], hT[:, k, SEG:TOK]).then_inc(sem["out_stored"], 16)
                sp.wait_ge(sem["out_stored"], 16 * KT)

        @block.scalar
        def _(act):
            chained = [0]

            def link(ins):
                chained[0] += 1
                ins.then_inc(sem["act_chain"], 1)
                act.wait_ge(sem["act_chain"], chained[0])

            act.wait_ge(sem["vec_loaded"], 16)
            S.activation(cond[:].rearrange("p k c -> p (k c)"), vec[:, VEC_COND:VEC_COND + 2 * KT], ACT.Silu)\
                .then_inc(sem["cond_ready"], 1)
            act.wait_ge(sem["lower_ready"], 1)
            S.activation(lowtmp[:, 1:3].rearrange("p l d h -> p (l d h)"),
                         lowtmp[:, 1:3].rearrange("p l d h -> p (l d h)"), ACT.Exp).then_inc(sem["lower_ready"], 1)
            for n in range(DEPTH * 12):
                l, s = n // 12, n % 12
                act.wait_ge(*is_ready(("ada", l, s)))
                if n >= 2:
                    act.wait_ge(*is_ready(("adaT", (n - 2) // 12, (n - 2) % 12)))
                S.activation(adarow[:, n % 2, :], result(("ada", l, s))[0:2, :], ACT.Copy).then_inc(sem["ada_row"], 1)

            def norm(key, count, lo, tail):
                for k in range(KT):
                    if k >= 2:
                        act.wait_ge(sem["square_used"], (KT - 1) * count + k - 1)
                    elif count:
                        act.wait_ge(*is_ready(prev_ms(key)))
                    if count == 0:
                        act.wait_ge(sem["x_loaded"], 48)
                    else:
                        act.wait_ge(*tail(k))
                    S.activation(square[:, k % 2, lo:TOK], xT[:, k, lo:TOK], ACT.Square)\
                        .then_inc(sem["square_ready"], 1)
                act.wait_ge(*is_ready(key))
                act.wait_ge(sem["epsv_ready"], 1)
                if count:
                    act.wait_ge(sem["normed_ready"], KT * count)
                S.activation(rstd[:, lo:TOK], result(key)[:, lo:TOK], ACT.Sqrt, scale=1.0 / D, bias=epsv[:, 0:1])\
                    .then_inc(sem["norm_std"], 1)

            def head_std(l, h, lo):
                act.wait_ge(*is_ready(("oms", l, h)))
                if h >= 2:
                    act.wait_ge(sem["og_ready"], 4 * l + h - 1)
                S.activation(ors[:, h % 2, lo:TOK], result(("oms", l, h))[:, lo:TOK], ACT.Sqrt, scale=1.0 / P,
                             bias=epsv[:, 0:1]).then_inc(sem["hg_std"], 1)

            def prev_ms(key):
                return {("ms", 0, 1): ("ms", 0, 0), ("ms", 1, 0): ("ms", 0, 1), ("ms", 1, 1): ("ms", 1, 0),
                        ("ms", 2, 0): ("ms", 1, 1)}[key]

            for l in range(DEPTH):
                if stop <= 10 * l + 1:
                    break
                lo = 0 if l == 0 else SEG
                segs = segs_of[l]
                norm(("ms", l, 0), 2 * l, 0, lambda k: total(2 * l - 1, None, "x_added", phases[2 * l - 1][1] - 4, k + 1))
                for c in range(4):
                    act.wait_ge(*is_ready(("in", l, 3, c)))
                    S.activation(qh[:, 2 * c + segs[0]:2 * c + 2, :].rearrange("p s t -> p (s t)"),
                                 result(("in", l, 3, c))[:, lo:TOK], ACT.Silu).then_inc(sem["q_ready"], 1)
                for way, k_to in enumerate((kf, kb)):
                    if way == 1:
                        act.wait_ge(sem["log_out"], 2 * l + 1)
                    for c in range(4):
                        key = ("in", l, 4 + way, c)
                        act.wait_ge(*is_ready(key))
                        S.activation(sig[:, c * TOK:(c + 1) * TOK], result(key)[:, :], ACT.Sigmoid)\
                            .then_inc(sem["sig_ready"], 1)
                        S.activation(k_to[:, 2 * c:2 * c + 2, :].rearrange("p s t -> p (s t)"), result(key)[:, :],
                                     ACT.Sigmoid, scale=-1.0).then_inc(sem["k_sig"], 1)
                    act.wait_ge(sem["log_in"], 2 * l + way + 1)
                    S.activation(logs[:], sig[:], ACT.Ln).then_inc(sem["log_out"], 1)
                for t in range(4):
                    act.wait_ge(*is_ready(("in", l, 6, t)))
                    S.activation(vh[:, t, :], result(("in", l, 6, t))[:, :], ACT.Copy).then_inc(sem["v_ready"], 1)
                if stop <= 10 * l + 2:
                    break
                extra = [(s, c) for s in (0, 1) for c in range(4)]

                def between():
                    s, c = extra.pop(0)
                    a = lo if s == 0 else 0
                    act.wait_ge(*is_ready(("in", l, s, c)))
                    S.activation((naq, nak)[s][:, c, a:TOK], result(("in", l, s, c))[:, a:TOK], ACT.Copy)\
                        .then_inc(sem["naqk_ready"], 1)

                d = 36 * l
                u = 38 * l
                for hp in range(2):
                    for unit in range(19):
                        if unit:
                            act.wait_ge(sem["decay_in"], d + 1)
                            na = 4 if (unit - 1) // 2 > LEVELS or l == 0 else 2
                            e = dec[d % 2][:, 0:na, :]
                            S.activation(e, e, ACT.Exp).then_inc(sem["decay_out"], 1)
                            d += 1
                        if unit % 4 == 0 and unit and extra:
                            between()
                        u += 1
                while extra:
                    between()
                for h in range(HG_HEADS):
                    act.wait_ge(*is_ready(("o", l, h)))
                    S.activation(oh[:, h, lo:TOK], result(("o", l, h))[:, lo:TOK], ACT.Copy)\
                        .then_inc(sem["oh_ready"], 1)
                if stop <= 10 * l + 3:
                    break
                for r in range(4):
                    src = A["rel_bias_reversed"]
                    for h in range(NA_HEADS):
                        skew = bass.AP(src.tensor, ((l * NA_HEADS + h) * 15 + 7 - r) * 31 + 15 + 1 - GRID_W,
                                       [[1, GRID_W], [31, 4], [1, GRID_W]])
                        act.dma_start(bias_skew[64 * (r % 2):64 * (r % 2) + 64, h, r // 2, :]
                                      .rearrange("p (a c) -> p a c", a=4), skew).then_inc(sem["bias_loaded"], 16)
                for t in range(4):
                    act.wait_ge(*is_ready(("in", l, 2, t)))
                    S.activation(navv[:, t, :], result(("in", l, 2, t))[:, :], ACT.Copy).then_inc(sem["nav_ready"], 1)
                for c in range(4):
                    act.wait_ge(*is_ready(("in", l, 7, c)))
                    S.activation(hgate[:, c, lo:TOK], result(("in", l, 7, c))[:, lo:TOK], ACT.Silu)\
                        .then_inc(sem["hgate_ready"], 1)
                tiles = [(h, q) for h in range(NA_HEADS) for sg in segs for q in (2 * sg, 2 * sg + 1)]
                per = len(tiles)
                before = 0 if l == 0 else NA_HEADS * 4
                for n in range(per + 2):
                    if n < per:
                        h, q = tiles[n]
                        nk = SEG if q < 2 else TOK
                        act.wait_ge(sem["na_max"], before + n + 1)
                        x = probs[(before + n) % 3]
                        S.activation(x[:, 0:nk], x[:, 0:nk], ACT.Exp, bias=narow[:, (before + n) % 3, 0:1],
                                     accum_out=narow[:, (before + n) % 3, 1:2]).then_inc(sem["na_p"], 1)
                    m = n - 2
                    if m >= 0:
                        h, q = tiles[m]
                        nk = 2 if q < 2 else 4
                        act.wait_ge(*is_ready(("TR", l, m)))
                        if m // 2 >= 2 and m % 2 == 0:
                            act.wait_ge(*is_ready(("PV", l, m // 2 - 2)))
                        S.activation(pt[(m // 2) % 2][:, 0:nk, (q % 2) * P:(q % 2 + 1) * P],
                                     result(("TR", l, m))[:, 0:nk * P].rearrange("p (k q) -> p k q", k=nk), ACT.Copy)\
                            .then_inc(sem["na_pt"], 1)
                if stop <= 10 * l + 4:
                    break
                for h in range(HG_HEADS):
                    if h < 2:
                        act.wait_ge(*is_ready(("PV", l, per // 2 - 1)))
                        act.wait_ge(sem["oh_ready"], 4 * (l + 1))
                    else:
                        act.wait_ge(*is_ready(("oms", l, h - 2)))
                    S.activation(osq[:, h % 2, lo:TOK], oh[:, h, lo:TOK], ACT.Square).then_inc(sem["osq_ready"], 1)
                    if h >= 1:
                        head_std(l, h - 1, lo)
                head_std(l, HG_HEADS - 1, lo)
                for n in range(16):
                    br, d = n // 8, n % 8
                    key = ("in", l, (8, 10)[br] + d // 4, d % 4)
                    act.wait_ge(*is_ready(key))
                    if n >= 2:
                        act.wait_ge(sem["merged_ready"], 16 * l + n - 1)
                    S.activation(gsig[:, n % 2, lo:TOK], result(key)[:, lo:TOK], ACT.Sigmoid)\
                        .then_inc(sem["gate_sig"], 1)
                if stop <= 10 * l + 5:
                    break
                norm(("ms", l, 1), 2 * l + 1, lo, lambda k: (sem["x_updated"], 8 * l + k + 1))
                act.wait_ge(*is_ready(("route", l)))
                S.activation(rt[0][:, 2 * l:4].rearrange("p t g e -> p (t g e)"),
                             result(("route", l))[:, 2 * l * N_EXPERTS:4 * N_EXPERTS], ACT.Sigmoid)\
                    .then_inc(sem["route_done"], 1)
                for t in range(2 * l, 4):
                    for half in range(2):
                        act.wait_ge(*is_ready(("rows", l, t, half)))
                        S.activation(hrow_hi[:, t, half * 512:(half + 1) * 512], result(("rows", l, t, half))[:, :],
                                     ACT.Copy).then_inc(sem["hrow_hi_ready"], 1)
                act.wait_ge(sem["crowd_ready"], l + 1)
                crowded = act.value_load(crowd_int[0:1, 0:1])

                def experts(ph):
                    open_phase(act, "act")

                    def keep_picked(i, e, half):
                        act.wait_ge(*total(ph, i, "gathered", e, half + 1))
                        act.wait_ge(*total(ph, i, "up_done", e - 1, 1))
                        S.activation(picked[:, 4 * half:4 * half + 4, :].rearrange("p k c -> p (k c)"), bank[2 + half][:, :],
                                     ACT.Copy).then_inc(sem["picked_ready"], 1)

                    def slot_weights(i, e):
                        act.wait_ge(*total(ph, i, "pickw_turned", e, 1))
                        act.wait_ge(*total(ph, i, "act_ready", e - 2, 1))
                        act.wait_ge(*total(ph, i, "slot_weight_ready", e - 1, 1))
                        S.activation(unused[:, lo:TOK], bank[4][:, lo:TOK], ACT.Copy, accum_out=slot_weight[:, e % 2:e % 2 + 1])\
                            .then_inc(sem["slot_weight_ready"], 1)

                    for half in range(2):
                        keep_picked(None, 0, half)
                    slot_weights(None, 0)
                    with act.Fori(0, phases[ph][1] // 4) as i:
                        for e in range(4):
                            act.wait_ge(*total(ph, i, "gate_done", e, 1))
                            act.wait_ge(*total(ph, i, "act_ready", e - 1, 1))
                            S.activation(silu[:], bank[0][:, :], ACT.Silu).then_inc(sem["silu_ready"], 1)
                            keep_picked(i, e + 1, 0)
                            act.wait_ge(*total(ph, i, "act_turned", e, 1))
                            act.wait_ge(*total(ph, i, "y_done", e - 1, 2))
                            S.activation(acts_t[:].rearrange("p k c -> p (k c)"), bank[5][:, :], ACT.Copy)\
                                .then_inc(sem["acts_t_ready"], 1)
                            keep_picked(i, e + 1, 1)
                            slot_weights(i, e + 1)
                            for half in range(2):
                                act.wait_ge(*total(ph, i, "y_done", e, half + 1))
                                act.wait_ge(*total(ph, i, "scattered", -1, 2))
                                S.activation(y_hi[:, e, half * 512:(half + 1) * 512], bank[6 + half][:, :], ACT.Copy)\
                                    .then_inc(sem["y_hi_ready"], 1)

                experts(2 * l)
                close_phase(act, "act", 2 * l)
                with act.If(crowded > CAPACITY):
                    experts(2 * l + 1)
                with act.Else():
                    skip_phase(act, "act", 2 * l + 1)
            if stop > 30:
                norm(("ms", 2, 0), 4, SEG, lambda k: total(3, None, "x_added", phases[3][1] - 4, k + 1))

        @block.gpsimd
        def _(pool):
            for l in range(DEPTH):
                if stop <= 10 * l + 3:
                    break
                pool.wait_ge(sem["const_loaded"], 16)
                pool.wait_ge(sem["bias_loaded"], 16 * 32 * (l + 1))
                for h in range(NA_HEADS):
                    b = bias[:, h].rearrange("p q (r c) -> p (q r) c", c=GRID_W)
                    x = bias_skew[:, h].rearrange("p q (r c) -> p (q r) c", c=GRID_W)
                    back = bass.AP(x.tensor, x.offset + GRID_W - 1, [x.ap[0], [GRID_W, 8], [-1, GRID_W]])
                    wide = [P, 8, GRID_W]
                    G.tensor_tensor(b, back, wmul.unsqueeze(1).to_broadcast(wide), ALU.mult).then_inc(sem["pool_chain"], 1)
                    pool.wait_ge(sem["pool_chain"], 8 * l + h + 1)
                    G.tensor_tensor(b, b, wneg.unsqueeze(1).to_broadcast(wide), ALU.add).then_inc(sem["bias_ready"], 1)

        @block.vector
        def _(dve):
            chained = [0]

            def link(ins):
                chained[0] += 1
                ins.then_inc(sem["dve_chain"], 1)
                dve.wait_ge(sem["dve_chain"], chained[0])

            V.memset(epsv[:], EPS).then_inc(sem["epsv_ready"], 1)
            dve.wait_ge(sem["vec_loaded"], 16)
            raw = vec[:, VEC_LOWER:VEC_LOWER + 2 * DEPTH * HG_HEADS].rearrange("p (l d h) -> p l d h", l=DEPTH, d=2)
            link(V.tensor_tensor(lowtmp[:, 0], raw[:, 0], raw[:, 1], ALU.max))
            V.tensor_tensor(lowtmp[:, 1], raw[:, 0], lowtmp[:, 0], ALU.subtract)
            V.tensor_tensor(lowtmp[:, 2], raw[:, 1], lowtmp[:, 0], ALU.subtract).then_inc(sem["lower_ready"], 1)
            dve.wait_ge(sem["lower_ready"], 2)
            link(V.tensor_tensor(lowtmp[:, 3], lowtmp[:, 1], lowtmp[:, 2], ALU.add))
            link(V.reciprocal(lowtmp[:, 3], lowtmp[:, 3]))
            V.tensor_tensor(lowtmp[:, 4], lowtmp[:, 1], lowtmp[:, 3], ALU.mult)
            link(V.tensor_tensor(lowtmp[:, 5], lowtmp[:, 2], lowtmp[:, 3], ALU.mult))
            V.tensor_tensor(lower[:, :, 0], lowtmp[:, 4], lowtmp[:, 4], ALU.subtract)
            link(V.tensor_tensor(lowtmp[:, 6], lowtmp[:, 4], lowtmp[:, 5], ALU.add))
            link(V.tensor_tensor(lower[:, :, 1], lowtmp[:, 6], lowtmp[:, 4], ALU.subtract))
            link(V.tensor_scalar(upper[:], lower[:], -1.0, 1.0, ALU.mult, ALU.add))

            dve.wait_ge(sem["x_loaded"], 48)
            link(V.tensor_copy(levmask[:], levmask_f[:]))

            for n in range(DEPTH * 12):
                l, s = n // 12, n % 12
                dve.wait_ge(*is_ready(("adaT", l, s)))
                b = vec[:, VEC_BADA + 48 * l + 4 * s:VEC_BADA + 48 * l + 4 * s + 4].unsqueeze(2).to_broadcast([P, 4, 2])
                V.tensor_tensor(mod[:, l, 4 * s:4 * s + 4, :], result(("adaT", l, s))[:, 0:8]
                                .rearrange("p (j c) -> p j c", c=2), b, ALU.add).then_inc(sem["ada_mod"], 1)
            dve.wait_ge(sem["ada_mod"], DEPTH * 12)
            for l in range(DEPTH):
                for gain, at_scale, at_g in ((gain1, KT, VEC_N1), (gain2, 4 * KT, VEC_N2)):
                    g = vec[:, at_g + KT * l:at_g + KT * (l + 1)].unsqueeze(2).to_broadcast([P, KT, 2])
                    link(V.scalar_tensor_tensor(gain[:, l], mod[:, l, at_scale:at_scale + KT, :], 1.0, g,
                                                ALU.add, ALU.mult))

            def norm(count, lo, gain, shift):
                dve.wait_ge(sem["norm_std"], count + 1)
                link(V.reciprocal(rstd[:, lo:TOK], rstd[:, lo:TOK]))
                for k in range(KT):
                    V.tensor_tensor(normed[:, k % 2, lo:TOK], xT[:, k, lo:TOK], rstd[:, lo:TOK], ALU.mult)\
                     .then_inc(sem["normed_ready"], 1)
                    dve.wait_ge(sem["normed_ready"], KT * count + k + 1)
                    for sg in range(1 if lo else 0, 2):
                        a = slice(sg * SEG, (sg + 1) * SEG)
                        if shift is None:
                            op = V.tensor_scalar(hT[:, k, a], normed[:, k % 2, a], gain[:, k:k + 1], None, ALU.mult)
                        else:
                            op = V.tensor_scalar(hT[:, k, a], normed[:, k % 2, a], gain[:, k, 1 - sg:2 - sg],
                                                 shift[:, k, 1 - sg:2 - sg], ALU.mult, ALU.add)
                    op.then_inc(sem["h_ready"], 1)

            def add_scaled(key_bank, l, d, at_gate, lo):
                for sg in range(1 if lo else 0, 2):
                    a = slice(sg * SEG, (sg + 1) * SEG)
                    op = V.scalar_tensor_tensor(xT[:, d, a], key_bank[:, a], mod[:, l, at_gate + d, 1 - sg:2 - sg],
                                                xT[:, d, a], ALU.mult, ALU.add)
                return op

            for l in range(DEPTH):
                if stop <= 10 * l + 1:
                    break
                lo = 0 if l == 0 else SEG
                segs = segs_of[l]
                norm(2 * l, 0, gain1[:, l], mod[:, l, 0:KT, :])
                V.memset(onescan[:], 1.0)
                V.memset(pf[:, :, 0:1], 0.0)
                link(V.memset(pb[:, :, 0:1], 0.0))
                for way, (k_to, p_to) in enumerate(((kf, pf), (kb, pb))):
                    for h in range(HG_HEADS):
                        dve.wait_ge(sem["sig_ready"], 8 * l + 4 * way + h + 1)
                        dve.wait_ge(sem["k_sig"], 8 * l + 4 * way + h + 1)
                        up, low = upper[:, way, l, h:h + 1], lower[:, way, l, h:h + 1]
                        kh = k_to[:, 2 * h:2 * h + 2, :].rearrange("p s t -> p (s t)")
                        V.tensor_scalar(kh, kh, up, None, ALU.mult)
                        gh = sig[:, h * TOK:(h + 1) * TOK]
                        last = V.tensor_scalar(gh, gh, up, low, ALU.mult, ALU.add)
                    link(last)
                    V.tensor_scalar(small[:], sig[:], 2.0 ** -40, 2.0 ** 60, ALU.is_lt, ALU.mult)
                    link(V.tensor_scalar(sig[:], sig[:], GATE_FLOOR, None, ALU.max))
                    V.scalar_tensor_tensor(sig[:], small[:], 1.0, sig[:], ALU.add, ALU.mult).then_inc(sem["log_in"], 1)
                    dve.wait_ge(sem["log_out"], 2 * l + way + 1)
                    link(V.scalar_tensor_tensor(logs[:], small[:], -60.0 * float(np.log(2.0)) / 2.0 ** 60, logs[:],
                                                ALU.mult, ALU.add))
                    for hs in range(8):
                        last = V.tensor_tensor_scan(p_to[:, hs, 1:SEG + 1], onescan[:], logs[:, hs * SEG:(hs + 1) * SEG],
                                                    0.0, ALU.mult, ALU.add)
                    link(last)
                if stop <= 10 * l + 2:
                    break

                def rows(hp, all_segs):
                    return slice(4 * hp, 4 * hp + 4) if all_segs else slice(4 * hp + 1, 4 * hp + 4, 2)

                def halves(x, h):
                    y = x.rearrange("p a (n two h) -> p a n two h", two=2, h=h)
                    return y[:, :, :, 0, :], y[:, :, :, 1, :]

                def decays(hp, unit, u, d):
                    if u >= 2:
                        dve.wait_ge(sem["fac_ready"], u - 1)
                    lev, way = (unit - 1) // 2, (unit - 1) % 2
                    p, off = ((pf, 1), (pb, 0))[way]
                    x = dec[d % 2]
                    if lev <= LEVELS:
                        h = 1 << lev
                        r = rows(hp, l == 0)
                        na = 2 * len(segs)
                        left, right = halves(p[:, r, off:off + SEG], h)
                        to_left, to_right = halves(x[:, 0:na, :], h)
                        shape = [P, na, SEG // (2 * h), h]
                        mid = p[:, r, h:SEG:2 * h].unsqueeze(3).to_broadcast(shape)
                        V.tensor_tensor(to_left, mid, left, ALU.subtract)
                        V.tensor_tensor(to_right, right, mid, ALU.subtract).then_inc(sem["decay_in"], 1)
                    else:
                        for sg in range(2):
                            q = p[:, 4 * hp + sg:4 * hp + 4:2, off:off + SEG]
                            to = x[:, sg:4:2, :]
                            if sg == way:
                                end = p[:, 4 * hp + sg:4 * hp + 4:2, SEG:SEG + 1].to_broadcast([P, 2, SEG])
                                op = V.tensor_tensor(to, end, q, ALU.subtract)
                            else:
                                op = V.tensor_copy(to, q)
                        op.then_inc(sem["decay_in"], 1)

                def factors(hp, unit, u, d):
                    lev, way = (unit - 1) // 2, (unit - 1) % 2
                    if u - 2 in spent:
                        dve.wait_ge(sem["psum_ready"], spent[u - 2])
                    y = fac[u % 2]
                    r = rows(hp, l == 0)
                    na = 2 * len(segs)
                    if unit == 0:
                        V.tensor_tensor(y[:, 0:na, :], kf[:, r, :], kb[:, r, :], ALU.add).then_inc(sem["fac_ready"], 1)
                        return
                    dve.wait_ge(sem["decay_out"], d + 1)
                    k = (kf, kb)[way]
                    if lev <= LEVELS:
                        h = 1 << lev
                        e, to = halves(dec[d % 2][:, 0:na, :], h), halves(y[:, 0:na, :], h)
                        src = (halves(k[:, r, :], h)[way], halves(qh[:, r, :], h)[1 - way])
                        V.tensor_tensor(to[way], e[way], src[0], ALU.mult)
                        V.tensor_tensor(to[1 - way], e[1 - way], src[1], ALU.mult).then_inc(sem["fac_ready"], 1)
                    else:
                        x = dec[d % 2]
                        V.tensor_tensor(y[:, 0:4:2, :], x[:, 0:4:2, :], k[:, 4 * hp:4 * hp + 4:2, :], ALU.mult)
                        V.tensor_tensor(y[:, 1:4:2, :], x[:, 1:4:2, :], qh[:, 4 * hp + 1:4 * hp + 4:2, :], ALU.mult)\
                         .then_inc(sem["fac_ready"], 1)

                def diagonal(head):
                    x = att[:, head, segs[0], :, :]
                    dims = [x.ap[0]] + ([[2 * SEG, 2]] if l == 0 else []) + [[SEG + P, 2], [1, P]]
                    return bass.AP(x.tensor, x.offset, dims)

                def collect(hp, unit, u):
                    lev, way = (unit - 1) // 2, (unit - 1) % 2
                    if lev < LEVELS:
                        for h in range(2):
                            dve.wait_ge(*is_ready(("lev", l, u, h)))
                            got = result(("lev", l, u, h))[:, 0:2 * P * len(segs)]
                            if l == 0:
                                got = got.rearrange("p (s b t) -> p s b t", s=2, b=2)
                                shape = [P, 2, 2, P]
                            else:
                                got = got.rearrange("p (b t) -> p b t", b=2)
                                shape = [P, 2, P]
                            if unit == 0:
                                V.tensor_copy(diagonal(2 * hp + h), got).then_inc(sem["att_block"], 1)
                            else:
                                mask = levmask[:, way * LEVELS + lev, :]
                                for _ in range(len(shape) - 2):
                                    mask = mask.unsqueeze(1)
                                dve.wait_ge(*read_by(("lev", l, u - 1, h)))
                                V.copy_predicated(diagonal(2 * hp + h), mask.to_broadcast(shape), got)\
                                 .then_inc(sem["att_block"], 1)
                    elif lev == LEVELS:
                        dve.wait_ge(*is_ready(("lev", l, u, 0)))
                        got = result(("lev", l, u, 0))[:, 0:2 * P * len(segs)]
                        t0 = P * (1 - way)
                        if l == 0:
                            V.tensor_copy(att[:, 2 * hp:2 * hp + 2, :, way, t0:t0 + P],
                                          got.rearrange("p (h s t) -> p h s t", h=2, s=2)).then_inc(sem["att_block"], 1)
                        else:
                            V.tensor_copy(att[:, 2 * hp:2 * hp + 2, 1, way, t0:t0 + P],
                                          got.rearrange("p (h t) -> p h t", h=2)).then_inc(sem["att_block"], 1)
                    elif way == 1:
                        for h in range(2):
                            dve.wait_ge(*is_ready(("cross", l, hp, h)))
                            V.tensor_copy(attx[:, 2 * hp + h].rearrange("p b t -> p (b t)"),
                                          result(("cross", l, hp, h))[:, :]).then_inc(sem["att_block"], 1)

                units = [(hp, unit) for hp in range(2) for unit in range(19)]
                d_in = d_out = 36 * l
                for n in range(-1, len(units) + 1):
                    if n + 1 < len(units) and units[n + 1][1]:
                        decays(*units[n + 1], 38 * l + n + 1, d_in)
                        d_in += 1
                    if 0 <= n < len(units):
                        factors(*units[n], 38 * l + n, d_out)
                        d_out += units[n][1] > 0
                    if n >= 1:
                        collect(*units[n - 1], 38 * l + n - 1)
                if stop <= 10 * l + 3:
                    break

                for n in range(8):
                    dve.wait_ge(*is_ready(("rot", l, n)))
                    if n:
                        dve.wait_ge(sem["rope_done"], 8 * l + n)
                    x = (naq, nak)[n // 4][:, n % 4, SEG:TOK]
                    V.tensor_tensor(roped[:, 0], x, cos, ALU.mult)
                    link(V.tensor_tensor(roped[:, 1], result(("rot", l, n))[:, 0:SEG], sin, ALU.mult))
                    V.tensor_tensor(x, roped[:, 0], roped[:, 1], ALU.add).then_inc(sem["rope_done"], 1)

                tiles = [(h, q) for h in range(NA_HEADS) for sg in segs for q in (2 * sg, 2 * sg + 1)]
                per = len(tiles)
                before = 0 if l == 0 else NA_HEADS * 4
                scale = NA_DIM ** -0.5
                for n in range(per + 5):
                    if n < per:
                        h, q = tiles[n]
                        x = probs[(before + n) % 3]
                        dve.wait_ge(*is_ready(("S", l, n)))
                        if n >= 3:
                            dve.wait_ge(*is_ready(("TR", l, n - 3)))
                        got = result(("S", l, n))
                        op = V.tensor_scalar(x[:, 0:SEG], got[:, 0:SEG], scale, None, ALU.mult)
                        if q >= 2:
                            dve.wait_ge(sem["bias_ready"], 8 * l + h + 1)
                            op = V.scalar_tensor_tensor(x[:, SEG:TOK], got[:, SEG:TOK], scale, bias[:, h, q - 2, :],
                                                        ALU.mult, ALU.add)
                        op.then_inc(sem["na_z"], 1)
                        dve.wait_ge(*read_by(("S", l, n)))
                        V.tensor_reduce(narow[:, (before + n) % 3, 0:1], x[:, 0:SEG if q < 2 else TOK], AX.X, ALU.max,
                                        negate=True).then_inc(sem["na_max"], 1)
                    m = n - 1
                    if 0 <= m < per:
                        h, q = tiles[m]
                        nk = SEG if q < 2 else TOK
                        i = (before + m) % 3
                        dve.wait_ge(sem["na_p"], before + m + 1)
                        link(V.reciprocal(narow[:, i, 2:3], narow[:, i, 1:2]))
                        V.tensor_scalar(probs[i][:, 0:nk], probs[i][:, 0:nk], narow[:, i, 2:3], None, ALU.mult)\
                         .then_inc(sem["na_pn"], 1)
                    m = n - 5
                    if m >= 0 and m % 2 == 1:
                        h, q = tiles[m]
                        r = 64 * (h % 2)
                        sg = q // 2
                        dve.wait_ge(*is_ready(("PV", l, m // 2)))
                        V.tensor_copy(ona[r:r + 64, h // 2, sg * SEG:(sg + 1) * SEG],
                                      result(("PV", l, m // 2))[r:r + 64, 0:SEG]).then_inc(sem["na_o"], 1)
                if stop <= 10 * l + 4:
                    break

                for h in range(HG_HEADS):
                    dve.wait_ge(sem["hg_std"], 4 * l + h + 1)
                    dve.wait_ge(sem["hgate_ready"], 4 * l + h + 1)
                    x, y = oh[:, h, lo:TOK], ors[:, h % 2, lo:TOK]
                    link(V.reciprocal(y, y))
                    link(V.tensor_tensor(x, x, y, ALU.mult))
                    V.scalar_tensor_tensor(x, x, vec[:, VEC_HGAIN + l:VEC_HGAIN + l + 1], hgate[:, h, lo:TOK],
                                           ALU.mult, ALU.mult).then_inc(sem["og_ready"], 1)

                for n in range(16):
                    br, d = n // 8, n % 8
                    dve.wait_ge(sem["gate_sig"], 16 * l + n + 1)
                    dve.wait_ge(*is_ready(("y", l, br, d)))
                    got, gate, to = result(("y", l, br, d))[:, lo:TOK], gsig[:, n % 2, lo:TOK], merged[:, d, lo:TOK]
                    if br == 0:
                        V.tensor_tensor(to, gate, got, ALU.mult).then_inc(sem["merged_ready"], 1)
                    else:
                        link(V.tensor_tensor(gmul[:, n % 2, lo:TOK], gate, got, ALU.mult))
                        V.tensor_tensor(to, to, gmul[:, n % 2, lo:TOK], ALU.add).then_inc(sem["merged_ready"], 1)
                for d in range(KT):
                    dve.wait_ge(*is_ready(("out", l, d)))
                    add_scaled(result(("out", l, d)), l, d, 2 * KT, lo).then_inc(sem["x_updated"], 1)
                if stop <= 10 * l + 5:
                    break
                norm(2 * l + 1, lo, gain2[:, l], mod[:, l, 3 * KT:4 * KT, :])

                t0 = 2 * l
                nt = 4 - t0
                shape = [P, 4 * nt, PER_GROUP]
                idx = vec[:, VEC_GIDX:VEC_GIDX + 4].unsqueeze(1)
                flat = [x[:, t0:4].rearrange("p t g e -> p (t g) e") for x in rt]
                scores, biased, eq, cand, oh1, oh2, sel, m1, m2, mn, gs, ing = flat

                def first_max(x, hot, mx, n):
                    shape = [P, n, 4]
                    link(V.tensor_reduce(mx, x, AX.X, ALU.max))
                    link(V.tensor_tensor(eq[:, 0:n, :], x, mx.to_broadcast(shape), ALU.is_equal))
                    link(V.scalar_tensor_tensor(cand[:, 0:n, :], eq[:, 0:n, :], -8.0, idx.to_broadcast(shape),
                                                ALU.mult, ALU.add))
                    link(V.tensor_reduce(mn[:, 0:n, 0:1], cand[:, 0:n, :], AX.X, ALU.min))
                    link(V.tensor_tensor(hot, cand[:, 0:n, :], mn[:, 0:n, 0:1].to_broadcast(shape), ALU.is_equal))

                dve.wait_ge(sem["route_done"], l + 1)
                rb = vec[:, VEC_RBIAS:VEC_RBIAS + N_EXPERTS].unsqueeze(1).to_broadcast([P, nt, N_EXPERTS])
                link(V.tensor_tensor(biased.rearrange("p (t g) e -> p t (g e)", g=4),
                                     scores.rearrange("p (t g) e -> p t (g e)", g=4), rb, ALU.add))
                first_max(biased, oh1, m1[:, :, 0:1], 4 * nt)
                link(V.scalar_tensor_tensor(biased, oh1, -1e9, biased, ALU.mult, ALU.add))
                first_max(biased, oh2, m2[:, :, 0:1], 4 * nt)
                g4 = gs[:, 0:nt, :]
                link(V.tensor_tensor(g4, m1[:, :, 0].rearrange("p (t g) -> p t g", g=4),
                                     m2[:, :, 0].rearrange("p (t g) -> p t g", g=4), ALU.add))
                first_max(g4, ing[:, 0:nt, :], m1[:, 0:nt, 1:2], nt)
                link(V.tensor_tensor(sel, oh1, oh2, ALU.add))
                link(V.tensor_tensor(sel, sel, ing[:, 0:nt, :].rearrange("p t g -> p (t g)").unsqueeze(2)
                                     .to_broadcast(shape), ALU.mult))
                hot = chosen[:, t0:4].rearrange("p t (g e) -> p (t g) e", e=PER_GROUP)
                V.tensor_copy(hot, sel).then_inc(sem["chosen_ready"], 1)
                link(V.tensor_tensor(sel, sel, scores, ALU.mult))
                wide = [P, nt, N_EXPERTS]
                by_token = sel.rearrange("p (t g) e -> p t (g e)", g=4)
                link(V.tensor_reduce(m2[:, 0:nt, 1:2], by_token, AX.X, ALU.add))
                link(V.reciprocal(m2[:, 0:nt, 2:3], m2[:, 0:nt, 1:2]))
                V.memset(weight[:, :, N_EXPERTS:N_EXPERTS + 1], 0.0)
                V.memset(place[:, :, N_EXPERTS:N_EXPERTS + 1], -1.0)
                link(V.tensor_tensor(weight[:, t0:4, 0:N_EXPERTS], by_token, m2[:, 0:nt, 2:3].to_broadcast(wide), ALU.mult))
                for t in range(t0, 4):
                    for half in range(2):
                        dve.wait_ge(sem["hrow_hi_ready"], 8 * l + 2 * (t - t0) + half + 1)
                        a = slice(half * 512, (half + 1) * 512)
                        V.tensor_tensor(hrow_lo[:, t, a], result(("rows", l, t, half))[:, :], hrow_hi[:, t, a].bitcast(f32),
                                        ALU.subtract).then_inc(sem["hrow_ready"], 1)
                dve.wait_ge(*is_ready(("place", l)))
                pl = place[:, t0:4, 0:N_EXPERTS]
                link(V.scalar_tensor_tensor(pl, result(("place", l))[:, t0 * N_EXPERTS:4 * N_EXPERTS]
                                            .rearrange("p (t e) -> p t e", e=N_EXPERTS), 1.0, chosen[:, t0:4, :],
                                            ALU.add, ALU.mult))
                V.tensor_scalar(pl, pl, -1.0, None, ALU.add).then_inc(sem["place_ready"], 1)
                dve.wait_ge(sem["place_ready"], l + 1)

                link(V.tensor_reduce(crowd[:], result(("place", l))[:, 4 * N_EXPERTS:5 * N_EXPERTS], AX.X, ALU.max))
                V.tensor_copy(crowd_int[:], crowd[:]).then_inc(sem["crowd_ready"], 1)
                dve.wait_ge(sem["crowd_ready"], l + 1)
                crowded = dve.value_load(crowd_int[0:1, 0:1])

                def experts(ph):
                    open_phase(dve, "dve")

                    def make_pick(i, e):
                        dve.wait_ge(*total(ph, i, "pickw_turned", e - 2, 1))
                        at_e = phases[ph][0] + e if i is None else i * 4 + (phases[ph][0] + e)
                        wide = [P, nt, P]
                        hot = pick[:, e % 2, t0:4, :]
                        V.tensor_tensor(hot, iota.unsqueeze(1).to_broadcast(wide),
                                        place[:, t0:4, at_e].unsqueeze(2).to_broadcast(wide), ALU.is_equal)\
                         .then_inc(sem["pick_bare"], 1)
                        dve.wait_ge(*total(ph, i, "pick_bare", e, 1))
                        V.tensor_tensor(pickw[:, e % 2, t0:4, :], hot.bitcast(f32),
                                        weight[:, t0:4, at_e].unsqueeze(2).to_broadcast(wide), ALU.mult)\
                         .then_inc(sem["pick_ready"], 1)

                    make_pick(None, 0)
                    with dve.Fori(0, phases[ph][1] // 4) as i:
                        for e in range(4):
                            make_pick(i, e + 1)
                            dve.wait_ge(*total(ph, i, "pickw_turned", e, 1))
                            dve.wait_ge(*total(ph, i, "scattered", -1, 2))
                            dve.wait_ge(*total(ph, i, "slot_weight_ready", e, 1))
                            V.tensor_scalar(spread[:, e, lo:TOK], bank[4][:, lo:TOK], 0.0, None, ALU.not_equal)\
                             .then_inc(sem["spread_ready"], 1)
                            dve.wait_ge(*total(ph, i, "silu_ready", e, 1))
                            dve.wait_ge(*total(ph, i, "up_done", e, 1))
                            dve.wait_ge(*total(ph, i, "act_turned", e - 1, 1))
                            V.scalar_tensor_tensor(acts[:], bank[1][:, :], slot_weight[:, e % 2:e % 2 + 1], silu[:],
                                                   ALU.mult, ALU.mult).then_inc(sem["act_ready"], 1)
                            for half in range(2):
                                a = slice(half * 512, (half + 1) * 512)
                                dve.wait_ge(*total(ph, i, "y_hi_ready", e, half + 1))
                                V.tensor_tensor(y_lo[:, e, a], bank[6 + half][:, :], y_hi[:, e, a].bitcast(f32),
                                                ALU.subtract).then_inc(sem["y_lo_ready"], 1)
                        for d in range(KT):
                            dve.wait_ge(*total(ph, i, "scattered", 0, d + 1))
                            dve.wait_ge(*total(ph, i, "x_added", -4, d + 1))
                            add_scaled(bank[scatter_bank[d]], l, d, 5 * KT, lo).then_inc(sem["x_added"], 1)

                experts(2 * l)
                close_phase(dve, "dve", 2 * l)
                with dve.If(crowded > CAPACITY):
                    count = phases[2 * l + 1][1]
                    for r in range(count // N_EXPERTS):
                        a = slice(over_at + r * N_EXPERTS, over_at + (r + 1) * N_EXPERTS)
                        V.tensor_scalar(place[:, t0:4, a], pl, -float(CAPACITY * (r + 1)), None, ALU.add)
                        V.tensor_copy(weight[:, t0:4, a], weight[:, t0:4, 0:N_EXPERTS])
                    V.memset(weight[:, :, over_at + count:over_at + count + 1], 0.0)
                    V.memset(place[:, :, over_at + count:over_at + count + 1], -1.0).then_inc(sem["over_ready"], 1)
                    dve.wait_ge(sem["over_ready"], l + 1)
                    experts(2 * l + 1)
                with dve.Else():
                    skip_phase(dve, "dve", 2 * l + 1)
                    dve.sem_inc(sem["over_ready"], 1)
            if stop > 30:
                norm(4, SEG, vec[:, VEC_FINAL:VEC_FINAL + KT], None)


def constants():
    c = np.zeros((P, C_N), np.float32)
    c[:, C_IDENT:C_IDENT + P] = np.eye(P)
    c[:, C_ONES:C_ONES + P] = 1.0
    for i in range(0, P, 2):
        c[i + 1, C_ROT + i] = -1.0
        c[i, C_ROT + i + 1] = 1.0
    t = np.arange(SEG)
    row, col = (t // GRID_W).astype(np.float32), (t % GRID_W).astype(np.float32)
    inv = np.float32(10000.0) ** (-np.arange(0, 32, 2, dtype=np.float32) / np.float32(32))
    ang = np.concatenate([row[:, None] * inv, col[:, None] * inv], axis=-1)
    c[:, C_COS:C_COS + SEG] = np.repeat(np.tile(np.cos(ang).T, (2, 1)), 2, axis=0)
    c[:, C_SIN:C_SIN + SEG] = np.repeat(np.tile(np.sin(ang).T, (2, 1)), 2, axis=0)
    col = np.arange(P)[:, None] % GRID_W
    kc = np.arange(GRID_W)[None, :]
    start = np.clip(col - WIN_COLS // 2, 0, GRID_W - WIN_COLS)
    inside = (kc >= start) & (kc < start + WIN_COLS)
    c[:, C_IOTA:C_IOTA + P] = np.where(np.arange(P) < CAPACITY, np.arange(P), -P * P)
    c[:, C_BEFORE:C_BEFORE + P] = np.triu(np.ones((P, P)), 1)
    c[:, C_WMUL:C_WMUL + GRID_W] = inside
    c[:, C_WNEG:C_WNEG + GRID_W] = np.where(inside, 0.0, MASKED)
    m = np.zeros((P, 2 * LEVELS, P), np.float32)
    s, t = np.arange(P)[:, None], np.arange(P)[None, :]
    for lev in range(LEVELS):
        h = 1 << lev
        same = s // (2 * h) == t // (2 * h)
        m[:, lev] = same & (s % (2 * h) < h) & (t % (2 * h) >= h)
        m[:, LEVELS + lev] = same & (s % (2 * h) >= h) & (t % (2 * h) < h)
    return c, m


def kernel(**inputs):
    import numpy as _np
    import concourse.bacc as _bacc
    from concourse import mybir as _mybir
    from concourse.bass_utils import run_bass_kernel_spmd as _run

    a = {k: _np.asarray(v) for k, v in inputs.items()}

    def cols(x):
        x = x.reshape(*x.shape[:-1], -1, P)
        return _np.moveaxis(x, -1, 0).reshape(P, -1)

    lower = _np.stack([a["hg_lower_fwd"], a["hg_lower_bwd"]], axis=1)
    cond = _np.stack([a["c"][0], a["c_ctx"]], axis=0)
    vec = _np.concatenate([
        cols(a["b_ada"]), cols(a["norm1_g"]), cols(a["norm2_g"]), cols(a["final_g"]), cols(lower),
        _np.ascontiguousarray(a["hg_norm_g"].T),
        _np.moveaxis(cond.reshape(2, KT, P), 2, 0).transpose(0, 2, 1).reshape(P, 2 * KT),
        _np.broadcast_to(a["router_bias"], (P, N_EXPERTS)),
        _np.broadcast_to(_np.arange(4, dtype=_np.float32), (P, 4)),
    ], axis=1)
    assert vec.shape == (P, VEC_N), vec.shape
    const, levmask = constants()
    arrays = {
        "xT": _np.concatenate([a["ctx"][0], a["x"][0]], axis=0).T, "vec": vec, "const": const, "levmask": levmask,
        "rel_bias_reversed": a["na_rel_bias"][..., ::-1],
    }
    for n in ("w_ada", "w_in", "w_na_o", "w_hg_o", "w_out", "w_router", "w_gate", "w_up", "w_down"):
        arrays[n] = a[n]
    arrays = {n: _np.ascontiguousarray(x) for n, x in arrays.items()}
    nc = _bacc.Bacc("TRN2", target_bir_lowering=False, num_devices=1, dynamic_dma_scratch_size=1024)
    aps = {n: nc.dram_tensor(f"in_{n}", x.shape, _mybir.dt.from_np(x.dtype), kind="ExternalInput").ap()
           for n, x in arrays.items()}
    out = nc.dram_tensor("out_yT", (D, SEG), _mybir.dt.float32, kind="ExternalOutput").ap()
    build(nc, aps, out)
    r = _run(nc, [{f"in_{n}": x for n, x in arrays.items()}], core_ids=[0])
    return r.results[0]["out_yT"].T[None]
```

```python
import numpy as np
import concourse.bass as bass
from concourse import mybir
from contextlib import ExitStack

D = 1024
SEG = 256
TOK = 2 * SEG
DEPTH = 2
P = 128
KT = D // P
GRID_W = 64
WIN_COLS = 16
NA_HEADS = 8
NA_DIM = 64
HG_HEADS = 4
EPS = 1e-6
N_EXPERTS = 16
N_GROUPS = 4
PER_GROUP = N_EXPERTS // N_GROUPS
FF = 512
SLOTS = 4
SLOT = 4096
LEVELS = 7
GATE_FLOOR = 1e-30
MASKED = -1e30
CAPACITY = 128

VEC_BADA = 0
VEC_N1 = VEC_BADA + DEPTH * 48
VEC_N2 = VEC_N1 + DEPTH * KT
VEC_FINAL = VEC_N2 + DEPTH * KT
VEC_LOWER = VEC_FINAL + KT
VEC_HGAIN = VEC_LOWER + 2 * DEPTH * HG_HEADS
VEC_COND = VEC_HGAIN + DEPTH
VEC_RBIAS = VEC_COND + 2 * KT
VEC_GIDX = VEC_RBIAS + N_EXPERTS
VEC_N = VEC_GIDX + 4
C_IDENT, C_ONES, C_ROT, C_COS, C_SIN, C_WMUL, C_WNEG, C_IOTA, C_BEFORE = 0, 128, 256, 384, 640, 896, 960, 1024, 1152
C_N = 1280


def build(nc, A, out, stop=99):
    f32, f32r, u8, i32 = mybir.dt.float32, mybir.dt.float32r, mybir.dt.uint8, mybir.dt.int32
    ALU, ACT, AX = mybir.AluOpType, mybir.ActivationFunctionType, mybir.AxisListType
    V, S, G, T = nc.vector, nc.scalar, nc.gpsimd, nc.tensor

    at = [(nc.sbuf_base + 31) // 32 * 32]

    def fixed(name, shape, dtype=f32, offset=None):
        size = int(np.prod(shape[1:])) * (1 if dtype == u8 else 4)
        where = at[0] if offset is None else offset
        if offset is None:
            at[0] += (size + 31) // 32 * 32
        return nc.alloc_sbuf_tensor_at(name, shape, dtype, offset=where)

    xT = fixed("xT", [P, KT, TOK])
    hT_at = at[0]
    hT = fixed("hT", [P, KT, TOK])
    ring_at = at[0]
    ring = fixed("ring", [P, SLOTS, SLOT])
    ring_lo = fixed("ring_lo", [P, SLOTS, SLOT], f32r, offset=ring_at)
    const = fixed("const", [P, C_N])
    levmask = fixed("levmask", [P, 2 * LEVELS, P], u8)
    vec = fixed("vec", [P, VEC_N])
    router = fixed("router", [P, KT, N_EXPERTS])
    cond = fixed("cond", [P, KT, 2])
    mod = fixed("mod", [P, DEPTH, 48, 2])
    gain1 = fixed("gain1", [P, DEPTH, KT, 2])
    gain2 = fixed("gain2", [P, DEPTH, KT, 2])
    lower = fixed("lower", [P, 2, DEPTH, HG_HEADS])
    upper = fixed("upper", [P, 2, DEPTH, HG_HEADS])
    lowtmp = fixed("lowtmp", [P, 8, 2, HG_HEADS])
    over_at = N_EXPERTS
    place = fixed("place", [P, 4, over_at + 3 * N_EXPERTS])
    weight = fixed("weight", [P, 4, over_at + 3 * N_EXPERTS])
    crowd = fixed("crowd", [P, 1])
    crowd_int = fixed("crowd_int", [P, 1], mybir.dt.int32)
    chosen = fixed("chosen", [P, 4, N_EXPERTS])
    slot_weight = fixed("slot_weight", [P, 2])
    epsv = fixed("epsv", [P, 1])
    adarow = fixed("adarow", [2, 2, 512])
    rstd = fixed("rstd", [P, TOK])
    narow = fixed("narow", [P, 3, 4])
    ident = const[:, C_IDENT:C_IDENT + P]
    ones = const[:, C_ONES:C_ONES + P]
    rot = const[:, C_ROT:C_ROT + P]
    cos = const[:, C_COS:C_COS + SEG]
    sin = const[:, C_SIN:C_SIN + SEG]
    wmul = const[:, C_WMUL:C_WMUL + GRID_W]
    iota = const[:, C_IOTA:C_IOTA + P]
    later = const[:, C_BEFORE:C_BEFORE + P]
    wneg = const[:, C_WNEG:C_WNEG + GRID_W]

    A0 = at[0]
    KB = 1024
    qh = fixed("qh", [P, 8, SEG], offset=A0)
    kf = fixed("kf", [P, 8, SEG], offset=A0 + 8 * KB)
    kb = fixed("kb", [P, 8, SEG], offset=A0 + 16 * KB)
    pf = fixed("pf", [P, 8, SEG + 1], offset=A0 + 24 * KB)
    pb = fixed("pb", [P, 8, SEG + 1], offset=A0 + 24 * KB + 8224)
    vh = fixed("vh", [P, 4, 512], offset=A0 + 24 * KB + 2 * 8224)
    B0 = A0 + 32 * KB + 2 * 8224
    att = fixed("att", [P, HG_HEADS, 2, 2, SEG], offset=B0)
    attx = fixed("attx", [P, HG_HEADS, 2, SEG], offset=B0 + 16 * KB)
    dec = [fixed(f"dec{i}", [P, 4, SEG], offset=B0 + 24 * KB + i * 4 * KB) for i in range(2)]
    fac = [fixed(f"fac{i}", [P, 4, SEG], offset=B0 + 32 * KB + i * 4 * KB) for i in range(2)]
    C0 = B0 + 40 * KB
    naq = fixed("naq", [P, 4, TOK], offset=C0)
    nak = fixed("nak", [P, 4, TOK], offset=C0 + 8 * KB)
    roped = fixed("roped", [P, 2, SEG], offset=A0 + 24 * KB + 2 * 8224)
    END = C0 + 16 * KB
    assert END <= nc.sbuf_usable_end, (END, nc.sbuf_usable_end)
    sig = fixed("sig", [P, 8 * SEG], offset=B0 + 24 * KB)
    small = fixed("small", [P, 8 * SEG], offset=B0 + 32 * KB)
    logs = fixed("logs", [P, 8 * SEG], offset=B0)
    onescan = fixed("onescan", [P, SEG], offset=B0 + 8 * KB)
    oh = fixed("oh", [P, HG_HEADS, TOK], offset=A0 + 8 * KB)
    hgate = fixed("hgate", [P, HG_HEADS, TOK], offset=A0 + 16 * KB)
    navv = fixed("navv", [P, 4, 512], offset=A0)
    ona = fixed("ona", [P, 4, TOK], offset=A0 + 24 * KB)
    pt = [fixed(f"pt{i}", [P, 4, SEG], offset=A0 + 32 * KB + 4 * KB * i) for i in range(2)]
    bias = fixed("bias", [P, NA_HEADS, 2, 4 * GRID_W], offset=B0 + 24 * KB)
    levmask_f = fixed("levmask_f", [P, 2 * LEVELS, P], offset=A0)
    bias_skew = fixed("bias_skew", [P, NA_HEADS, 2, 4 * GRID_W], offset=B0)
    probs = [fixed(f"probs{i}", [P, TOK], offset=B0 + 16 * KB + 2 * KB * i) for i in range(3)]
    square = fixed("square", [P, 2, TOK], offset=C0 + 8 * KB)
    normed = fixed("normed", [P, 2, TOK], offset=C0 + 12 * KB)
    osq = fixed("osq", [P, 2, TOK], offset=C0)
    ors = fixed("ors", [P, 2, TOK], offset=C0 + 4 * KB)
    merged = fixed("merged", [P, KT, TOK], offset=B0)
    gsig = fixed("gsig", [P, 2, TOK], offset=C0 + 8 * KB)
    gmul = fixed("gmul", [P, 2, TOK], offset=C0 + 12 * KB)
    hrow_hi = fixed("hrow_hi", [P, 4, D], f32r, offset=A0)
    hrow_lo = fixed("hrow_lo", [P, 4, D], f32r, offset=A0 + 16 * KB)
    y_hi = fixed("y_hi", [P, 2, D], f32r, offset=A0 + 32 * KB)
    y_lo = fixed("y_lo", [P, 2, D], f32r, offset=A0 + 40 * KB)
    w_hi = [fixed("w_hi0", [P, SLOT], f32r, offset=hT_at), fixed("w_hi1", [P, SLOT], f32r, offset=A0 + 48 * KB)]
    spread = fixed("spread", [P, 4, TOK], f32r, offset=A0 + 64 * KB)
    picked_rows = fixed("picked_rows", [P, D], offset=A0 + 72 * KB)
    picked_hi = fixed("picked_hi", [P, KT, P], f32r, offset=A0 + 76 * KB)
    picked_lo = fixed("picked_lo", [P, KT, P], f32r, offset=A0 + 80 * KB)
    pick = fixed("pick", [P, 2, 4, P], f32r, offset=A0 + 84 * KB)
    pickw = fixed("pickw", [P, 2, 4, P], offset=A0 + 88 * KB)
    silu = fixed("silu", [P, FF], offset=A0 + 92 * KB)
    acts = fixed("acts", [P, FF], offset=A0 + 94 * KB)
    acts_hi = fixed("acts_hi", [P, 4, P], f32r, offset=A0 + 96 * KB)
    acts_lo = fixed("acts_lo", [P, 4, P], f32r, offset=A0 + 98 * KB)
    unused = fixed("unused", [P, TOK], offset=A0 + 100 * KB)
    rt = [fixed(f"rt{i}", [P, 4, N_GROUPS, PER_GROUP], offset=A0 + 92 * KB + 256 * i) for i in range(12)]
    scores_t = fixed("scores_t", [N_EXPERTS, TOK], offset=A0 + 100 * KB)
    assert A0 + 102 * KB <= END

    names = """const_loaded vec_loaded x_loaded bias_loaded out_stored psum_ready cond_ready ada_row ada_mod
        epsv_ready gains_ready lower_ready square_ready square_used norm_std rstd_ready normed_ready h_ready q_ready
        sig_ready k_sig gates_ready log_in log_out v_ready naqk_ready rope_done sums_ready decay_in decay_out fac_ready
        att_block oh_ready osq_ready hg_std og_ready hgate_ready nav_ready bias_ready na_z na_max na_p na_pn
        na_pt na_o gate_sig merged_ready x_updated route_done scores_ready chosen_ready place_ready crowd_ready over_ready
        hrow_hi_ready hrow_ready gathered pickw_turned gate_done up_done act_turned rows_turned y_done scattered
        pick_bare pick_ready spread_ready act_ready acts_lo_ready picked_lo_ready y_lo_ready x_added own_lo_ready
        rows_ready picked_hi_ready slot_weight_ready silu_ready acts_hi_ready y_hi_ready w_hi_ready w_lo_ready
        dve_chain act_chain pool_chain pool_ready""".split()
    with ExitStack() as ctx:
        sem = {n: ctx.enter_context(nc.semaphore(n)) for n in names}
        slot_full = [ctx.enter_context(nc.semaphore(f"slot_full{i}")) for i in range(SLOTS)]
        bank = [ctx.enter_context(nc.psum_tensor(f"bank{i}", [P, 512], f32)) for i in range(8)]
        block = ctx.enter_context(nc.Block())

        loads = []

        def slot_of(key):
            return loads.index(key)

        for l in range(DEPTH):
            loads += [("ada", l, s) for s in range(12)]
        for l in range(DEPTH):
            loads += [("in", l, s) for s in (3, 4, 5, 6, 0, 1, 2, 7)]
            loads += [("in", l, 8), ("nao", l), ("in", l, 9), ("hgo", l), ("in", l, 10), ("in", l, 11)]
            loads += [("out", l, 0), ("out", l, 1)]
            assert len(loads) % SLOTS == 0
            for ph, n in ((2 * l, N_EXPERTS), (2 * l + 1, 3 * N_EXPERTS if l == 0 else N_EXPERTS)):
                loads += [("moe", ph, e, k) for e in range(n) for k in range(3)]

        def slot(key):
            return ring[:, slot_of(key) % SLOTS, :]

        def full(key):
            n = slot_of(key)
            return slot_full[n % SLOTS], 16 * (n // SLOTS + 1)

        ready, reader, last_use, spent = {}, {}, {}, {}
        in_bank = [None] * 8
        counts = {}
        slot_spent = {}
        jobs = [0]

        def read_by(key):
            return sem[reader[key][0]], reader[key][1]

        def is_ready(key):
            return sem["psum_ready"], ready[key][1]

        def result(key):
            return bank[ready[key][0]]

        scatter_bank = (1, 5, 6, 7, 1, 5, 6, 7)
        segs_of = {0: (0, 1), 1: (1,)}

        phases = []
        for l in range(DEPTH):
            rounds_left = (len(segs_of[l]) * SEG + CAPACITY - 1) // CAPACITY - 1
            phases += [(0, N_EXPERTS), (over_at, N_EXPERTS * rounds_left)]
        signals = {"gathered": 2, "pickw_turned": 1, "gate_done": 1, "up_done": 1, "act_turned": 1,
                   "rows_turned": 2, "y_done": 2, "scattered": 4,
                   "pick_bare": 1, "pick_ready": 1, "spread_ready": 1, "act_ready": 1, "acts_lo_ready": 1,
                   "picked_lo_ready": 2, "y_lo_ready": 2, "x_added": 4, "own_lo_ready": 3,
                   "rows_ready": 2, "picked_hi_ready": 2, "slot_weight_ready": 1, "silu_ready": 1,
                   "acts_hi_ready": 1, "y_hi_ready": 2, "w_hi_ready": 3, "w_lo_ready": 3}
        signalled_by = {
            "pe": ("gathered", "pickw_turned", "gate_done", "up_done", "act_turned", "rows_turned", "y_done", "scattered"),
            "dve": ("pick_bare", "pick_ready", "spread_ready", "act_ready", "acts_lo_ready", "picked_lo_ready",
                    "y_lo_ready", "x_added", "own_lo_ready"),
            "act": ("rows_ready", "picked_hi_ready", "slot_weight_ready", "silu_ready", "acts_hi_ready", "y_hi_ready",
                    "w_hi_ready"),
            "pool": ("w_lo_ready",)}

        def worth(ph, name):
            return signals[name] * (phases[ph][1] + 4)

        def total(ph, i, name, e, k):
            per = signals[name]
            static = sum(worth(p, name) for p in range(ph)) + 4 * per + per * e + k
            return sem[name], (static if i is None else i * (4 * per) + static)

        def by_fours(engine, ph, body):
            count = phases[ph][1]
            with engine.Fori(0, count // 4 - 1) as i:
                for e in range(4):
                    body(i, e, False)
            for e in range(count - 4, count):
                body(None, e, e == count - 1)

        gpsimd_part = (SLOT * 3 // 4, SLOT // 2, SLOT // 2)

        def open_phase(engine, who):
            for name in signalled_by[who]:
                engine.sem_inc(sem[name], 4 * signals[name])

        def close_phase(engine, who, ph):
            for name in signalled_by[who]:
                engine.wait_ge(*total(ph, None, name, phases[ph][1] - 1, signals[name]))

        def skip_phase(engine, who, ph):
            for name in signalled_by[who]:
                engine.sem_inc(sem[name], worth(ph, name))

        def rows(hp, all_segs):
            return slice(4 * hp, 4 * hp + 4) if all_segs else slice(4 * hp + 1, 4 * hp + 4, 2)

        def halves(x, h):
            y = x.rearrange("p a (n two h) -> p a n two h", two=2, h=h)
            return y[:, :, :, 0, :], y[:, :, :, 1, :]

        @block.tensor
        def _(pe):
            def open_bank(key, who):
                b = jobs[0] % 8
                jobs[0] += 1
                if in_bank[b] is not None:
                    pe.wait_ge(*read_by(in_bank[b]))
                in_bank[b] = key
                counts[who] = counts.get(who, 0) + 1
                ready[key] = (b, jobs[0])
                reader[key] = (who, counts[who])
                return bank[b]

            pe.wait_ge(sem["const_loaded"], 16)
            pe.wait_ge(sem["cond_ready"], 1)

            def ada_rows(l, s):
                pe.wait_ge(*full(("ada", l, s)))
                w = slot(("ada", l, s)).rearrange("p (k n) -> p k n", k=KT)
                o = open_bank(("ada", l, s), "ada_row")
                for k in range(KT):
                    mm = T.matmul(o[0:2, :], cond[:, k, :], w[:, k, :], start=(k == 0), stop=(k == KT - 1))
                mm.then_inc(sem["psum_ready"], 1)
                slot_spent[slot_of(("ada", l, s))] = (sem["psum_ready"], jobs[0])

            def ada_turn(l, s):
                o = open_bank(("adaT", l, s), "ada_mod")
                pe.wait_ge(*read_by(("ada", l, s)))
                n = (l * 12 + s) % 2
                for j in range(4):
                    mm = T.transpose(o[:, 2 * j:2 * j + 2], adarow[:, n, j * P:(j + 1) * P], ident[0:2, 0:2])
                mm.then_inc(sem["psum_ready"], 1)

            for n in range(DEPTH * 12 + 1):
                if n < DEPTH * 12:
                    ada_rows(n // 12, n % 12)
                if n:
                    ada_turn((n - 1) // 12, (n - 1) % 12)

            def mean_square(key, count, lo):
                o = open_bank(key, "norm_std")
                for k in range(KT):
                    pe.wait_ge(sem["square_ready"], count * KT + k + 1)
                    mm = T.matmul(o[:, lo:TOK], ones, square[:, k % 2, lo:TOK], start=(k == 0), stop=(k == KT - 1))
                    if k < KT - 1:
                        mm.then_inc(sem["square_used"], 1)
                mm.then_inc(sem["psum_ready"], 1)

            def project(l, s, c, who, lo):
                w = slot(("in", l, s)).rearrange("p (k n) -> p k n", k=KT)
                o = open_bank(("in", l, s, c), who)
                for k in range(KT):
                    if c == 0 and s == 3:
                        pe.wait_ge(sem["h_ready"], KT * 2 * l + k + 1)
                    mm = T.matmul(o[:, lo:TOK], w[:, k, c * P:(c + 1) * P], hT[:, k, lo:TOK],
                                  start=(k == 0), stop=(k == KT - 1))
                mm.then_inc(sem["psum_ready"], 1)
                if c == 3:
                    slot_spent[slot_of(("in", l, s))] = (sem["psum_ready"], jobs[0])

            def project_rows(l, s, t, who):
                w = slot(("in", l, s)).rearrange("p (k n) -> p k n", k=KT)
                o = open_bank(("in", l, s, t), who)
                for k in range(KT):
                    mm = T.matmul(o[:, :], hT[:, k, t * P:(t + 1) * P], w[:, k, :], start=(k == 0), stop=(k == KT - 1))
                mm.then_inc(sem["psum_ready"], 1)
                if t == 3:
                    slot_spent[slot_of(("in", l, s))] = (sem["psum_ready"], jobs[0])

            units_before = [0]
            rounds = {"norm": 0, "square_used": 0}
            for l in range(DEPTH):
                if stop <= 10 * l + 1:
                    break
                lo = 0 if l == 0 else SEG
                segs = segs_of[l]
                mean_square(("ms", l, 0), 2 * l, 0)
                for s, who in ((3, "q_ready"), (4, "k_sig"), (5, "k_sig")):
                    pe.wait_ge(*full(("in", l, s)))
                    for c in range(4):
                        project(l, s, c, who, lo if s == 3 else 0)
                pe.wait_ge(*full(("in", l, 6)))
                for t in range(4):
                    project_rows(l, 6, t, "v_ready")
                if stop <= 10 * l + 2:
                    break

                extra = [(s, c) for s in (0, 1) for c in range(4)]

                def between():
                    if not extra:
                        return
                    s, c = extra.pop(0)
                    if c == 0:
                        pe.wait_ge(*full(("in", l, s)))
                    project(l, s, c, "naqk_ready", lo if s == 0 else 0)

                u = 38 * l
                for hp in range(2):
                    for unit in range(19):
                        pe.wait_ge(sem["fac_ready"], u + 1)
                        f = fac[u % 2]
                        lev, way = (unit - 1) // 2, (unit - 1) % 2
                        if lev < LEVELS:
                            for h in range(2):
                                o = open_bank(("lev", l, u, h), "att_block")
                                for i, sg in enumerate(segs):
                                    for b in range(2):
                                        left = f[:, h * len(segs) + i, b * P:(b + 1) * P]
                                        right = qh[:, 2 * (2 * hp + h) + sg, b * P:(b + 1) * P] if unit == 0 else left
                                        mm = T.matmul(o[:, (2 * i + b) * P:(2 * i + b + 1) * P], left, right,
                                                      start=True, stop=True)
                                mm.then_inc(sem["psum_ready"], 1)
                        elif lev == LEVELS:
                            o = open_bank(("lev", l, u, 0), "att_block")
                            for h in range(2):
                                for i in range(len(segs)):
                                    j = h * len(segs) + i
                                    halves = f[:, j, 0:P], f[:, j, P:SEG]
                                    mm = T.matmul(o[:, j * P:(j + 1) * P], halves[way], halves[1 - way],
                                                  start=True, stop=True)
                            mm.then_inc(sem["psum_ready"], 1)
                        elif way == 1:
                            g = fac[(u - 1) % 2]
                            for h in range(2):
                                o = open_bank(("cross", l, hp, h), "att_block")
                                for sb in range(2):
                                    for n, x in enumerate((g, f)):
                                        mm = T.matmul(o[:, sb * SEG:(sb + 1) * SEG], x[:, 2 * h, sb * P:(sb + 1) * P],
                                                      x[:, 2 * h + 1, :], start=(n == 0), stop=(n == 1))
                                mm.then_inc(sem["psum_ready"], 1)
                        spent[u] = jobs[0]
                        if lev > LEVELS and way == 1:
                            spent[u - 1] = jobs[0]
                        u += 1
                        if unit % 4 == 3:
                            between()
                while extra:
                    between()

                pe.wait_ge(*read_by(("cross", l, 1, 1)))
                for h in range(HG_HEADS):
                    o = open_bank(("o", l, h), "oh_ready")
                    for sg in segs:
                        terms = [(2 * sg + sb, att[:, h, sg, sb, :]) for sb in range(2)]
                        if sg == 1:
                            terms = [(sb, attx[:, h, sb, :]) for sb in range(2)] + terms
                        for n, (t, a) in enumerate(terms):
                            mm = T.matmul(o[:, sg * SEG:(sg + 1) * SEG], vh[:, t, h * P:(h + 1) * P], a,
                                          start=(n == 0), stop=(n == len(terms) - 1))
                    mm.then_inc(sem["psum_ready"], 1)
                if stop <= 10 * l + 3:
                    break

                pe.wait_ge(*full(("in", l, 2)))
                for t in range(4):
                    project_rows(l, 2, t, "nav_ready")
                for n in range(8):
                    buf = (naq, nak)[n // 4]
                    o = open_bank(("rot", l, n), "rope_done")
                    pe.wait_ge(sem["naqk_ready"], 8 * l + n + 1)
                    T.matmul(o[:, 0:SEG], rot, buf[:, n % 4, SEG:TOK], start=True, stop=True)\
                        .then_inc(sem["psum_ready"], 1)
                pe.wait_ge(*full(("in", l, 7)))
                for c in range(4):
                    project(l, 7, c, "hgate_ready", lo)
                pe.wait_ge(sem["rope_done"], 8 * (l + 1))

                tiles = [(h, q) for h in range(NA_HEADS) for sg in segs for q in (2 * sg, 2 * sg + 1)]
                per = len(tiles)
                before = 0 if l == 0 else NA_HEADS * 4
                for n in range(per + 4):
                    if n < per:
                        h, q = tiles[n]
                        r = 64 * (h % 2)
                        nk = SEG if q < 2 else TOK
                        o = open_bank(("S", l, n), "na_z")
                        T.matmul(o[:, 0:nk], naq[r:r + 64, h // 2, q * P:(q + 1) * P], nak[r:r + 64, h // 2, 0:nk],
                                 start=True, stop=True).then_inc(sem["psum_ready"], 1)
                    m = n - 2
                    if 0 <= m < per:
                        h, q = tiles[m]
                        o = open_bank(("TR", l, m), "na_pt")
                        pe.wait_ge(sem["na_pn"], before + m + 1)
                        for k in range(2 if q < 2 else 4):
                            mm = T.transpose(o[:, k * P:(k + 1) * P], probs[(before + m) % 3][:, k * P:(k + 1) * P], ident)
                        mm.then_inc(sem["psum_ready"], 1)
                    m = n - 4
                    if m >= 0 and m % 2 == 1:
                        h, q = tiles[m]
                        r = 64 * (h % 2)
                        o = open_bank(("PV", l, m // 2), "na_o")
                        pe.wait_ge(*read_by(("TR", l, m)))
                        nk = 2 if q < 2 else 4
                        for k in range(nk):
                            mm = T.matmul(o[r:r + 64, 0:SEG], navv[:, k, h * 64:(h + 1) * 64],
                                          pt[(m // 2) % 2][:, k, :], start=(k == 0), stop=(k == nk - 1))
                        mm.then_inc(sem["psum_ready"], 1)
                h, q = tiles[per - 1]
                if stop <= 10 * l + 4:
                    break

                for h in range(HG_HEADS):
                    o = open_bank(("oms", l, h), "hg_std")
                    pe.wait_ge(sem["osq_ready"], 4 * l + h + 1)
                    T.matmul(o[:, lo:TOK], ones, osq[:, h % 2, lo:TOK], start=True, stop=True)\
                        .then_inc(sem["psum_ready"], 1)

                for br, (first, wo, src) in enumerate(((8, "nao", ona), (10, "hgo", oh))):
                    pe.wait_ge(*full((wo, l)))
                    if br == 0:
                        pe.wait_ge(*read_by(("PV", l, per // 2 - 1)))
                    else:
                        pe.wait_ge(sem["og_ready"], 4 * (l + 1))
                    w = slot((wo, l)).rearrange("p (k n) -> p k n", k=4)
                    for d in range(KT):
                        if d % 4 == 0:
                            pe.wait_ge(*full(("in", l, first + d // 4)))
                        project(l, first + d // 4, d % 4, "gate_sig", lo)
                        o = open_bank(("y", l, br, d), "merged_ready")
                        for k in range(4):
                            mm = T.matmul(o[:, lo:TOK], w[:, k, d * P:(d + 1) * P], src[:, k, lo:TOK],
                                          start=(k == 0), stop=(k == 3))
                        mm.then_inc(sem["psum_ready"], 1)
                    slot_spent[slot_of((wo, l))] = (sem["psum_ready"], jobs[0])
                pe.wait_ge(sem["merged_ready"], 16 * (l + 1))
                for d in range(KT):
                    key = ("out", l, d // 4)
                    if d % 4 == 0:
                        pe.wait_ge(*full(key))
                    w = slot(key).rearrange("p (k n) -> p k n", k=KT)
                    o = open_bank(("out", l, d), "x_updated")
                    for k in range(KT):
                        mm = T.matmul(o[:, lo:TOK], w[:, k, (d % 4) * P:(d % 4 + 1) * P], merged[:, k, lo:TOK],
                                      start=(k == 0), stop=(k == KT - 1))
                    mm.then_inc(sem["psum_ready"], 1)
                    if d % 4 == 3:
                        slot_spent[slot_of(key)] = (sem["psum_ready"], jobs[0])
                if stop <= 10 * l + 5:
                    break

                mean_square(("ms", l, 1), 2 * l + 1, lo)
                o = open_bank(("route", l), "route_done")
                for k in range(KT):
                    pe.wait_ge(sem["h_ready"], KT * (2 * l + 1) + k + 1)
                    mm = T.matmul(o[0:N_EXPERTS, lo:TOK], router[:, k, :], hT[:, k, lo:TOK],
                                  start=(k == 0), stop=(k == KT - 1))
                mm.then_inc(sem["psum_ready"], 1)
                for t in range(2 * (l > 0), 4):
                    for half in range(2):
                        o = open_bank(("rows", l, t, half), "hrow_ready")
                        for j in range(4):
                            mm = T.transpose(o[:, j * P:(j + 1) * P], hT[:, 4 * half + j, t * P:(t + 1) * P], ident)
                        mm.then_inc(sem["psum_ready"], 1)
                    if t == 2 * (l > 0):
                        pe.wait_ge(*read_by(("route", l)))
                        o = open_bank(("scores", l), "scores_ready")
                        for x in range(2 * (l > 0), 4):
                            mm = T.transpose(o[:, x * N_EXPERTS:(x + 1) * N_EXPERTS], scores_t[:, x * P:(x + 1) * P],
                                             ident[0:N_EXPERTS, 0:N_EXPERTS])
                        mm.then_inc(sem["psum_ready"], 1)
                o = open_bank(("place", l), "place_ready")
                pe.wait_ge(sem["chosen_ready"], l + 1)
                for t in range(2 * (l > 0), 4):
                    for s in range(2 * (l > 0), t + 1):
                        mm = T.matmul(o[:, t * N_EXPERTS:(t + 1) * N_EXPERTS], later if s == t else ones,
                                      chosen[:, s, :], start=(s == 2 * (l > 0)), stop=(s == t))
                for t in range(2 * (l > 0), 4):
                    mm = T.matmul(o[:, 4 * N_EXPERTS:5 * N_EXPERTS], ones, chosen[:, t, :],
                                  start=(t == 2 * (l > 0)), stop=(t == 3))
                mm.then_inc(sem["psum_ready"], 1)

                for b in range(8):
                    pe.wait_ge(*read_by(in_bank[b]))
                tiles = list(range(2 * (l > 0), 4))

                pe.wait_ge(sem["hrow_ready"], (8, 12)[l])

                def experts(ph):
                    def gather(i, e, half):
                        pe.wait_ge(*total(ph, i, "pick_ready", e, 1))
                        pe.wait_ge(*total(ph, i, "picked_lo_ready", e - 1, half + 1))
                        for n, (t, rows) in enumerate([(t, rows) for t in tiles for rows in (hrow_hi, hrow_lo)]):
                            mm = T.matmul(bank[2 + half][:, :], pick[:, e % 2, t, :],
                                          rows[:, t, half * 512:(half + 1) * 512],
                                          start=(n == 0), stop=(n == 2 * len(tiles) - 1))
                        mm.then_inc(sem["gathered"], 1)

                    def turn_pick(i, e):
                        pe.wait_ge(*total(ph, i, "spread_ready", e - 1, 1))
                        for t in tiles:
                            mm = T.transpose(bank[4][:, t * P:(t + 1) * P], pickw[:, e % 2, t, :], ident)
                        mm.then_inc(sem["pickw_turned"], 1)

                    def turn_rows(i, e):
                        for half in range(2):
                            pe.wait_ge(*total(ph, i, "rows_ready", e, half + 1))
                            for j in range(4):
                                d = 4 * half + j
                                mm = T.transpose(bank[2 + half][:, j * P:(j + 1) * P], picked_rows[:, d * P:(d + 1) * P],
                                                 ident)
                            mm.then_inc(sem["rows_turned"], 1)

                    def down(i, e, last):
                        hi = w_hi[(3 * e + 2) % 2][:].rearrange("p (k n) -> p k n", k=4)
                        low = ring_lo[:, (base + 3 * e + 2) % SLOTS, :].rearrange("p (k n) -> p k n", k=4)
                        pe.wait_ge(*total(ph, i, "w_hi_ready", e, 3))
                        pe.wait_ge(*total(ph, i, "acts_hi_ready", e, 1))
                        for half in range(2):
                            if e % 2 == 0:
                                pe.wait_ge(*total(ph, i, "x_added", e - 2, 7 + half))
                            else:
                                pe.wait_ge(*total(ph, i, "y_lo_ready", e - 1, half + 1))
                            for k in range(4):
                                T.matmul(bank[6 + half][:, :], acts_hi[:, k, :], hi[:, k, half * 512:(half + 1) * 512],
                                         start=(k == 0), stop=False)
                        pe.wait_ge(*total(ph, i, "acts_lo_ready", e, 1))
                        for half in range(2):
                            for k in range(4):
                                T.matmul(bank[6 + half][:, :], acts_lo[:, k, :], hi[:, k, half * 512:(half + 1) * 512],
                                         start=False, stop=False)
                        if not last:
                            turn_rows(i, e + 1)
                        pe.wait_ge(*total(ph, i, "w_lo_ready", e, 3))
                        pe.wait_ge(*total(ph, i, "own_lo_ready", e, 3))
                        for half in range(2):
                            for k in range(4):
                                mm = T.matmul(bank[6 + half][:, :], acts_hi[:, k, :],
                                              low[:, k, half * 512:(half + 1) * 512], start=False, stop=(k == 3))
                            mm.then_inc(sem["y_done"], 1)

                    def into_hidden(i, e, g):
                        if g == 1 and e % 2 == 0:
                            pe.wait_ge(*total(ph, i, "x_added", e - 2, 5))
                        else:
                            pe.wait_ge(*total(ph, i, ("silu_ready", "act_ready")[g], e - 1, 1))
                        hi = w_hi[(3 * e + g) % 2][:].rearrange("p (k n) -> p k n", k=KT)
                        low = ring_lo[:, (base + 3 * e + g) % SLOTS, :].rearrange("p (k n) -> p k n", k=KT)
                        pe.wait_ge(*total(ph, i, "w_hi_ready", e, g + 1))
                        for k in range(KT):
                            if g == 0 and k % 4 == 0:
                                pe.wait_ge(*total(ph, i, "picked_hi_ready", e, k // 4 + 1))
                            T.matmul(bank[g][:, :], picked_hi[:, k, :], hi[:, k, :], start=(k == 0), stop=False)
                        for k in range(KT):
                            if g == 0 and k % 4 == 0:
                                pe.wait_ge(*total(ph, i, "picked_lo_ready", e, k // 4 + 1))
                            T.matmul(bank[g][:, :], picked_lo[:, k, :], hi[:, k, :], start=False, stop=False)
                        pe.wait_ge(*total(ph, i, "w_lo_ready", e, g + 1))
                        pe.wait_ge(*total(ph, i, "own_lo_ready", e, g + 1))
                        for k in range(KT):
                            mm = T.matmul(bank[g][:, :], picked_hi[:, k, :], low[:, k, :], start=False,
                                          stop=(k == KT - 1))
                        mm.then_inc(sem[("gate_done", "up_done")[g]], 1)

                    def expert(i, e, last):
                        into_hidden(i, e, 1)
                        if not last:
                            gather(i, e + 1, 0)
                        pe.wait_ge(*total(ph, i, "act_ready", e, 1))
                        if e % 2 == 0:
                            pe.wait_ge(*total(ph, i, "x_added", e - 2, 6))
                        else:
                            pe.wait_ge(*total(ph, i, "acts_lo_ready", e - 1, 1))
                        for j in range(4):
                            mm = T.transpose(bank[5][:, j * P:(j + 1) * P], acts[:, j * P:(j + 1) * P], ident)
                        mm.then_inc(sem["act_turned"], 1)
                        if not last:
                            gather(i, e + 1, 1)
                            turn_pick(i, e + 1)
                        down(i, e, last)
                        if not last:
                            into_hidden(i, e + 1, 0)
                        if e % 2 == 0:
                            return
                        pe.wait_ge(*total(ph, i, "y_lo_ready", e, 2))
                        for d in range(KT):
                            if d >= 4:
                                pe.wait_ge(*total(ph, i, "x_added", e - 1, d - 3))
                            o = bank[scatter_bank[d]]
                            for n, (x, y) in enumerate([(x, y) for x in (e - 1, e) for y in (y_hi, y_lo)]):
                                mm = T.matmul(o[:, lo:TOK], y[:, x % 2, d * P:(d + 1) * P], spread[:, x % 4, lo:TOK],
                                              start=(n == 0), stop=(n == 3))
                            mm.then_inc(sem["scattered"], 1)

                    base = slot_of(("moe", ph, 0, 0))
                    open_phase(pe, "pe")
                    gather(None, 0, 0)
                    gather(None, 0, 1)
                    turn_pick(None, 0)
                    turn_rows(None, 0)
                    into_hidden(None, 0, 0)
                    by_fours(pe, ph, expert)

                experts(2 * l)
                close_phase(pe, "pe", 2 * l)
                pe.wait_ge(sem["crowd_ready"], l + 1)
                crowded = pe.value_load(crowd_int[0:1, 0:1])
                with pe.If(crowded > CAPACITY):
                    experts(2 * l + 1)
                with pe.Else():
                    skip_phase(pe, "pe", 2 * l + 1)
                for ph in (2 * l, 2 * l + 1):
                    for m in range(3 * phases[ph][1]):
                        name, k = (("gate_done", 1), ("up_done", 1), ("y_done", 2))[m % 3]
                        slot_spent[slot_of(("moe", ph, 0, 0)) + m] = total(ph, None, name, m // 3, k)
                last = phases[ph][1] - 1
                for b in range(8):
                    in_bank[b] = ("experts", l, b)
                    name, e, k = ("x_added", last, 4) if b in scatter_bank else ("silu_ready", last, 1) if b == 0 else \
                        ("picked_lo_ready", last, 2) if b < 4 else ("spread_ready", last, 1)
                    reader["experts", l, b] = (name, total(ph, None, name, e, k)[1])
            if stop > 30:
                mean_square(("ms", 2, 0), 4, SEG)

        @block.sync
        def _(sp):
            sp.dma_start(vec[:], A["vec"]).then_inc(sem["vec_loaded"], 16)
            sp.dma_start(const[:], A["const"]).then_inc(sem["const_loaded"], 16)

            def source(key):
                if key[0] == "ada":
                    return A["w_ada"][key[1], :, key[2] * 512:(key[2] + 1) * 512].rearrange("(k p) n -> p k n", p=P), KT
                if key[0] == "in":
                    return A["w_in"][key[1], :, key[2] * 512:(key[2] + 1) * 512].rearrange("(k p) n -> p k n", p=P), KT
                if key[0] == "out":
                    return A["w_out"][key[1], :, key[2] * 512:(key[2] + 1) * 512].rearrange("(k p) n -> p k n", p=P), KT
                return A["w_na_o" if key[0] == "nao" else "w_hg_o"][key[1]].rearrange("(k p) n -> p k n", p=P), 4

            def fill(n):
                src, k = source(loads[n])
                sp.dma_start(ring[:, n % SLOTS, :].rearrange("p (k n) -> p k n", k=k), src)\
                    .then_inc(slot_full[n % SLOTS], 16)

            for n in range(SLOTS):
                fill(n)
            sp.dma_start(xT[:], A["xT"].rearrange("(k p) n -> p k n", p=P)).then_inc(sem["x_loaded"], 16)
            sp.dma_start(levmask_f[:], A["levmask"]).then_inc(sem["x_loaded"], 16)
            sp.dma_start(router[:], A["w_router"].rearrange("(k p) n -> p k n", p=P)).then_inc(sem["x_loaded"], 16)
            n = SLOTS
            for l in range(DEPTH):
                base = slot_of(("moe", 2 * l, 0, 0))
                while n < base:
                    if n - SLOTS not in slot_spent:
                        break
                    sp.wait_ge(*slot_spent[n - SLOTS])
                    fill(n)
                    n += 1
                if n < base or ("place", l) not in ready:
                    break
                w = (A["w_gate"], A["w_up"], A["w_down"])
                flat = [x.rearrange("l e (k p) n -> (l e) p k n", p=P) for x in w]

                def fill_expert(m, expert):
                    s, k = (base + m) % SLOTS, (KT, KT, 4)[m % 3]
                    src = flat[m % 3][expert] if isinstance(expert, int) else flat[m % 3][expert, :, :, :]
                    sp.dma_start(ring[:, s, :].rearrange("p (k n) -> p k n", k=k), src).then_inc(slot_full[s], 16)

                def fill_spent(ph, i, e, m):
                    name, k = (("gate_done", 1), ("up_done", 1), ("y_done", 2))[(m - SLOTS) % 3]
                    sp.wait_ge(*total(ph, i, name, e + (m - SLOTS) // 3, k))

                for m in range(SLOTS):
                    sp.wait_ge(*slot_spent[base + m - SLOTS])
                    fill_expert(m, l * N_EXPERTS + m // 3)
                with sp.Fori(0, N_EXPERTS // 4 - 1) as i:
                    for m in range(SLOTS, SLOTS + 12):
                        fill_spent(2 * l, i, 0, m)
                        fill_expert(m, i * 4 + (l * N_EXPERTS + m // 3))
                for m in range(SLOTS + 36, 48):
                    fill_spent(2 * l, None, 0, m)
                    fill_expert(m, l * N_EXPERTS + m // 3)
                sp.wait_ge(sem["crowd_ready"], l + 1)
                crowded = sp.value_load(crowd_int[0:1, 0:1])
                with sp.If(crowded > CAPACITY):
                    for e in range(0, phases[2 * l + 1][1], N_EXPERTS):
                        with sp.Fori(0, N_EXPERTS // 4) as i:
                            for m in range(12):
                                fill_spent(2 * l + 1, i, e, m)
                                fill_expert(m, i * 4 + (l * N_EXPERTS + m // 3))
                with sp.Else():
                    for i in range(SLOTS):
                        sp.wait_ge(slot_full[i], 16 * ((base + 48) // SLOTS))
                        sp.sem_inc(slot_full[i], 16 * 3 * phases[2 * l + 1][1] // SLOTS)
                n = base + 48 + 3 * phases[2 * l + 1][1]
            if stop <= 30:
                for i in range(SLOTS):
                    sp.wait_ge(slot_full[i], 16 * sum(1 for m in range(n) if m % SLOTS == i))
                sp.wait_ge(sem["x_loaded"], 48)
            if stop > 30:
                for k in range(KT):
                    sp.wait_ge(sem["h_ready"], KT * 4 + k + 1)
                    sp.dma_start(out[k * P:(k + 1) * P, :], hT[:, k, SEG:TOK]).then_inc(sem["out_stored"], 16)
                sp.wait_ge(sem["out_stored"], 16 * KT)

        @block.scalar
        def _(act):
            chained = [0]

            def link(ins):
                chained[0] += 1
                ins.then_inc(sem["act_chain"], 1)
                act.wait_ge(sem["act_chain"], chained[0])

            act.wait_ge(sem["vec_loaded"], 16)
            S.activation(cond[:].rearrange("p k c -> p (k c)"), vec[:, VEC_COND:VEC_COND + 2 * KT], ACT.Silu)\
                .then_inc(sem["cond_ready"], 1)
            act.wait_ge(sem["lower_ready"], 1)
            S.activation(lowtmp[:, 1:3].rearrange("p l d h -> p (l d h)"),
                         lowtmp[:, 1:3].rearrange("p l d h -> p (l d h)"), ACT.Exp).then_inc(sem["lower_ready"], 1)
            for n in range(DEPTH * 12):
                l, s = n // 12, n % 12
                act.wait_ge(*is_ready(("ada", l, s)))
                if n >= 2:
                    act.wait_ge(*is_ready(("adaT", (n - 2) // 12, (n - 2) % 12)))
                S.activation(adarow[:, n % 2, :], result(("ada", l, s))[0:2, :], ACT.Copy).then_inc(sem["ada_row"], 1)

            def norm(key, count, lo, tail):
                for k in range(KT):
                    if k >= 2:
                        act.wait_ge(sem["square_used"], (KT - 1) * count + k - 1)
                    elif count:
                        act.wait_ge(*is_ready(prev_ms(key)))
                    if count == 0:
                        act.wait_ge(sem["x_loaded"], 48)
                    else:
                        act.wait_ge(*tail(k))
                    S.activation(square[:, k % 2, lo:TOK], xT[:, k, lo:TOK], ACT.Square)\
                        .then_inc(sem["square_ready"], 1)
                act.wait_ge(*is_ready(key))
                act.wait_ge(sem["epsv_ready"], 1)
                if count:
                    act.wait_ge(sem["normed_ready"], KT * count)
                S.activation(rstd[:, lo:TOK], result(key)[:, lo:TOK], ACT.Sqrt, scale=1.0 / D, bias=epsv[:, 0:1])\
                    .then_inc(sem["norm_std"], 1)

            def head_std(l, h, lo):
                act.wait_ge(*is_ready(("oms", l, h)))
                if h >= 2:
                    act.wait_ge(sem["og_ready"], 4 * l + h - 1)
                S.activation(ors[:, h % 2, lo:TOK], result(("oms", l, h))[:, lo:TOK], ACT.Sqrt, scale=1.0 / P,
                             bias=epsv[:, 0:1]).then_inc(sem["hg_std"], 1)

            def prev_ms(key):
                return {("ms", 0, 1): ("ms", 0, 0), ("ms", 1, 0): ("ms", 0, 1), ("ms", 1, 1): ("ms", 1, 0),
                        ("ms", 2, 0): ("ms", 1, 1)}[key]

            for l in range(DEPTH):
                if stop <= 10 * l + 1:
                    break
                lo = 0 if l == 0 else SEG
                segs = segs_of[l]
                norm(("ms", l, 0), 2 * l, 0, lambda k: total(2 * l - 1, None, "x_added", phases[2 * l - 1][1] - 2, k + 1))
                for c in range(4):
                    act.wait_ge(*is_ready(("in", l, 3, c)))
                    S.activation(qh[:, 2 * c + segs[0]:2 * c + 2, :].rearrange("p s t -> p (s t)"),
                                 result(("in", l, 3, c))[:, lo:TOK], ACT.Silu).then_inc(sem["q_ready"], 1)
                for way, k_to in enumerate((kf, kb)):
                    if way == 1:
                        act.wait_ge(sem["log_out"], 2 * l + 1)
                    for c in range(4):
                        key = ("in", l, 4 + way, c)
                        act.wait_ge(*is_ready(key))
                        S.activation(sig[:, c * TOK:(c + 1) * TOK], result(key)[:, :], ACT.Sigmoid)\
                            .then_inc(sem["sig_ready"], 1)
                        S.activation(k_to[:, 2 * c:2 * c + 2, :].rearrange("p s t -> p (s t)"), result(key)[:, :],
                                     ACT.Sigmoid, scale=-1.0).then_inc(sem["k_sig"], 1)
                    act.wait_ge(sem["log_in"], 2 * l + way + 1)
                    S.activation(logs[:], sig[:], ACT.Ln).then_inc(sem["log_out"], 1)
                for t in range(4):
                    act.wait_ge(*is_ready(("in", l, 6, t)))
                    S.activation(vh[:, t, :], result(("in", l, 6, t))[:, :], ACT.Copy).then_inc(sem["v_ready"], 1)
                if stop <= 10 * l + 2:
                    break
                extra = [(s, c) for s in (0, 1) for c in range(4)]

                def between():
                    s, c = extra.pop(0)
                    a = lo if s == 0 else 0
                    act.wait_ge(*is_ready(("in", l, s, c)))
                    S.activation((naq, nak)[s][:, c, a:TOK], result(("in", l, s, c))[:, a:TOK], ACT.Copy)\
                        .then_inc(sem["naqk_ready"], 1)

                d = 36 * l
                u = 38 * l
                for hp in range(2):
                    for unit in range(19):
                        if unit:
                            act.wait_ge(sem["decay_in"], d + 1)
                            na = 4 if (unit - 1) // 2 > LEVELS or l == 0 else 2
                            e = dec[d % 2][:, 0:na, :]
                            S.activation(e, e, ACT.Exp).then_inc(sem["decay_out"], 1)
                            d += 1
                        if unit % 4 == 0 and unit and extra:
                            between()
                        u += 1
                while extra:
                    between()
                for h in range(HG_HEADS):
                    act.wait_ge(*is_ready(("o", l, h)))
                    S.activation(oh[:, h, lo:TOK], result(("o", l, h))[:, lo:TOK], ACT.Copy)\
                        .then_inc(sem["oh_ready"], 1)
                if stop <= 10 * l + 3:
                    break
                for r in range(4):
                    src = A["rel_bias_reversed"]
                    for h in range(NA_HEADS):
                        skew = bass.AP(src.tensor, ((l * NA_HEADS + h) * 15 + 7 - r) * 31 + 15 + 1 - GRID_W,
                                       [[1, GRID_W], [31, 4], [1, GRID_W]])
                        act.dma_start(bias_skew[64 * (r % 2):64 * (r % 2) + 64, h, r // 2, :]
                                      .rearrange("p (a c) -> p a c", a=4), skew).then_inc(sem["bias_loaded"], 16)
                for t in range(4):
                    act.wait_ge(*is_ready(("in", l, 2, t)))
                    S.activation(navv[:, t, :], result(("in", l, 2, t))[:, :], ACT.Copy).then_inc(sem["nav_ready"], 1)
                for c in range(4):
                    act.wait_ge(*is_ready(("in", l, 7, c)))
                    S.activation(hgate[:, c, lo:TOK], result(("in", l, 7, c))[:, lo:TOK], ACT.Silu)\
                        .then_inc(sem["hgate_ready"], 1)
                tiles = [(h, q) for h in range(NA_HEADS) for sg in segs for q in (2 * sg, 2 * sg + 1)]
                per = len(tiles)
                before = 0 if l == 0 else NA_HEADS * 4
                for n in range(per + 2):
                    if n < per:
                        h, q = tiles[n]
                        nk = SEG if q < 2 else TOK
                        act.wait_ge(sem["na_max"], before + n + 1)
                        x = probs[(before + n) % 3]
                        S.activation(x[:, 0:nk], x[:, 0:nk], ACT.Exp, bias=narow[:, (before + n) % 3, 0:1],
                                     accum_out=narow[:, (before + n) % 3, 1:2]).then_inc(sem["na_p"], 1)
                    m = n - 2
                    if m >= 0:
                        h, q = tiles[m]
                        nk = 2 if q < 2 else 4
                        act.wait_ge(*is_ready(("TR", l, m)))
                        if m // 2 >= 2 and m % 2 == 0:
                            act.wait_ge(*is_ready(("PV", l, m // 2 - 2)))
                        S.activation(pt[(m // 2) % 2][:, 0:nk, (q % 2) * P:(q % 2 + 1) * P],
                                     result(("TR", l, m))[:, 0:nk * P].rearrange("p (k q) -> p k q", k=nk), ACT.Copy)\
                            .then_inc(sem["na_pt"], 1)
                if stop <= 10 * l + 4:
                    break
                for h in range(HG_HEADS):
                    if h < 2:
                        act.wait_ge(*is_ready(("PV", l, per // 2 - 1)))
                        act.wait_ge(sem["oh_ready"], 4 * (l + 1))
                    else:
                        act.wait_ge(*is_ready(("oms", l, h - 2)))
                    S.activation(osq[:, h % 2, lo:TOK], oh[:, h, lo:TOK], ACT.Square).then_inc(sem["osq_ready"], 1)
                    if h >= 1:
                        head_std(l, h - 1, lo)
                head_std(l, HG_HEADS - 1, lo)
                for n in range(16):
                    br, d = n // 8, n % 8
                    key = ("in", l, (8, 10)[br] + d // 4, d % 4)
                    act.wait_ge(*is_ready(key))
                    if n >= 2:
                        act.wait_ge(sem["merged_ready"], 16 * l + n - 1)
                    S.activation(gsig[:, n % 2, lo:TOK], result(key)[:, lo:TOK], ACT.Sigmoid)\
                        .then_inc(sem["gate_sig"], 1)
                if stop <= 10 * l + 5:
                    break
                norm(("ms", l, 1), 2 * l + 1, lo, lambda k: (sem["x_updated"], 8 * l + k + 1))
                act.wait_ge(*is_ready(("route", l)))
                S.activation(scores_t[:, lo:TOK], result(("route", l))[0:N_EXPERTS, lo:TOK], ACT.Sigmoid)\
                    .then_inc(sem["route_done"], 1)
                for t in range(2 * l, 4):
                    for half in range(2):
                        act.wait_ge(*is_ready(("rows", l, t, half)))
                        S.activation(hrow_hi[:, t, half * 512:(half + 1) * 512], result(("rows", l, t, half))[:, :],
                                     ACT.Copy).then_inc(sem["hrow_hi_ready"], 1)

                def experts(ph):
                    base = slot_of(("moe", ph, 0, 0))

                    def split_high(i, e, g):
                        m = 3 * e + g
                        s = (base + m) % SLOTS
                        full_at = 16 * ((base + m) // SLOTS + 1)
                        act.wait_ge(slot_full[s], full_at if i is None else i * 48 + full_at)
                        name, k = (("gate_done", 1), ("up_done", 1), ("y_done", 2))[(m - 2) % 3]
                        act.wait_ge(*total(ph, i, name, (m - 2) // 3, k))
                        S.activation(w_hi[m % 2][:], ring[:, s, :], ACT.Copy).then_inc(sem["w_hi_ready"], 1)

                    def keep_rows(i, e):
                        for half in range(2):
                            act.wait_ge(*total(ph, i, "gathered", e, half + 1))
                            act.wait_ge(*total(ph, i, "rows_turned", e - 1, half + 1))
                            S.activation(picked_rows[:, half * 512:(half + 1) * 512], bank[2 + half][:, :], ACT.Copy)\
                                .then_inc(sem["rows_ready"], 1)

                    def slot_weights(i, e):
                        act.wait_ge(*total(ph, i, "pickw_turned", e, 1))
                        act.wait_ge(*total(ph, i, "act_ready", e - 2, 1))
                        act.wait_ge(*total(ph, i, "slot_weight_ready", e - 1, 1))
                        S.activation(unused[:, lo:TOK], bank[4][:, lo:TOK], ACT.Copy,
                                     accum_out=slot_weight[:, e % 2:e % 2 + 1]).then_inc(sem["slot_weight_ready"], 1)

                    def keep_picked(i, e):
                        act.wait_ge(*total(ph, i, "up_done", e - 1, 1))
                        for half in range(2):
                            act.wait_ge(*total(ph, i, "rows_turned", e, half + 1))
                            S.activation(picked_hi[:, 4 * half:4 * half + 4, :].rearrange("p k c -> p (k c)"),
                                         bank[2 + half][:, :], ACT.Copy).then_inc(sem["picked_hi_ready"], 1)

                    def expert(i, e, last):
                        act.wait_ge(*total(ph, i, "gate_done", e, 1))
                        act.wait_ge(*total(ph, i, "act_ready", e - 1, 1))
                        S.activation(silu[:], bank[0][:, :], ACT.Silu).then_inc(sem["silu_ready"], 1)
                        split_high(i, e, 2)
                        act.wait_ge(*total(ph, i, "act_turned", e, 1))
                        act.wait_ge(*total(ph, i, "y_done", e - 1, 2))
                        S.activation(acts_hi[:].rearrange("p k c -> p (k c)"), bank[5][:, :], ACT.Copy)\
                            .then_inc(sem["acts_hi_ready"], 1)
                        if not last:
                            split_high(i, e + 1, 0)
                            keep_rows(i, e + 1)
                            slot_weights(i, e + 1)
                            keep_picked(i, e + 1)
                        act.wait_ge(*total(ph, i, "scattered", e - 2 - e % 2, 8))
                        for half in range(2):
                            act.wait_ge(*total(ph, i, "y_done", e, half + 1))
                            S.activation(y_hi[:, e % 2, half * 512:(half + 1) * 512], bank[6 + half][:, :], ACT.Copy)\
                                .then_inc(sem["y_hi_ready"], 1)
                        if not last:
                            split_high(i, e + 1, 1)

                    open_phase(act, "act")
                    split_high(None, 0, 0)
                    keep_rows(None, 0)
                    keep_picked(None, 0)
                    split_high(None, 0, 1)
                    slot_weights(None, 0)
                    by_fours(act, ph, expert)

                experts(2 * l)
                close_phase(act, "act", 2 * l)
                act.wait_ge(sem["crowd_ready"], l + 1)
                crowded = act.value_load(crowd_int[0:1, 0:1])
                with act.If(crowded > CAPACITY):
                    experts(2 * l + 1)
                with act.Else():
                    skip_phase(act, "act", 2 * l + 1)
            if stop > 30:
                norm(("ms", 2, 0), 4, SEG, lambda k: total(3, None, "x_added", phases[3][1] - 2, k + 1))

        @block.gpsimd
        def _(pool):
            for l in range(DEPTH):
                if stop <= 10 * l + 2:
                    break
                segs = segs_of[l]

                def decays(hp, unit, u, d):
                    if u >= 2:
                        pool.wait_ge(sem["fac_ready"], u - 1)
                    lev, way = (unit - 1) // 2, (unit - 1) % 2
                    p, off = ((pf, 1), (pb, 0))[way]
                    x = dec[d % 2]
                    if lev <= LEVELS:
                        h = 1 << lev
                        r = rows(hp, l == 0)
                        na = 2 * len(segs)
                        left, right = halves(p[:, r, off:off + SEG], h)
                        to_left, to_right = halves(x[:, 0:na, :], h)
                        shape = [P, na, SEG // (2 * h), h]
                        mid = p[:, r, h:SEG:2 * h].unsqueeze(3).to_broadcast(shape)
                        G.tensor_tensor(to_left, mid, left, ALU.subtract)
                        G.tensor_tensor(to_right, right, mid, ALU.subtract).then_inc(sem["decay_in"], 1)
                    else:
                        for sg in range(2):
                            q = p[:, 4 * hp + sg:4 * hp + 4:2, off:off + SEG]
                            to = x[:, sg:4:2, :]
                            if sg == way:
                                end = p[:, 4 * hp + sg:4 * hp + 4:2, SEG:SEG + 1].to_broadcast([P, 2, SEG])
                                op = G.tensor_tensor(to, end, q, ALU.subtract)
                            else:
                                op = G.tensor_copy(to, q)
                        op.then_inc(sem["decay_in"], 1)

                pool.wait_ge(sem["sums_ready"], l + 1)
                d = 36 * l
                for n, (hp, unit) in enumerate([(hp, unit) for hp in range(2) for unit in range(19)]):
                    if unit:
                        decays(hp, unit, 38 * l + n, d)
                        d += 1
                if stop <= 10 * l + 3:
                    break
                pool.wait_ge(sem["const_loaded"], 16)
                pool.wait_ge(sem["bias_loaded"], 16 * 32 * (l + 1))
                for h in range(NA_HEADS):
                    b = bias[:, h].rearrange("p q (r c) -> p (q r) c", c=GRID_W)
                    x = bias_skew[:, h].rearrange("p q (r c) -> p (q r) c", c=GRID_W)
                    back = bass.AP(x.tensor, x.offset + GRID_W - 1, [x.ap[0], [GRID_W, 8], [-1, GRID_W]])
                    wide = [P, 8, GRID_W]
                    G.tensor_tensor(b, back, wmul.unsqueeze(1).to_broadcast(wide), ALU.mult).then_inc(sem["pool_chain"], 1)
                    pool.wait_ge(sem["pool_chain"], 8 * l + h + 1)
                    G.tensor_tensor(b, b, wneg.unsqueeze(1).to_broadcast(wide), ALU.add).then_inc(sem["bias_ready"], 1)
                if stop <= 10 * l + 5:
                    break

                def experts(ph):
                    base = slot_of(("moe", ph, 0, 0))

                    def split_low(i, e, g):
                        s = (base + 3 * e + g) % SLOTS
                        a = slice(0, gpsimd_part[g])
                        pool.wait_ge(*total(ph, i, "w_hi_ready", e, g + 1))
                        G.tensor_tensor(ring_lo[:, s, a], ring[:, s, a], w_hi[(3 * e + g) % 2][:, a].bitcast(f32),
                                        ALU.subtract).then_inc(sem["w_lo_ready"], 1)

                    def expert(i, e, last):
                        split_low(i, e, 2)
                        if not last:
                            split_low(i, e + 1, 0)
                            split_low(i, e + 1, 1)

                    open_phase(pool, "pool")
                    split_low(None, 0, 0)
                    split_low(None, 0, 1)
                    by_fours(pool, ph, expert)

                experts(2 * l)
                close_phase(pool, "pool", 2 * l)
                pool.wait_ge(sem["crowd_ready"], l + 1)
                crowded = pool.value_load(crowd_int[0:1, 0:1])
                with pool.If(crowded > CAPACITY):
                    experts(2 * l + 1)
                with pool.Else():
                    skip_phase(pool, "pool", 2 * l + 1)

        @block.vector
        def _(dve):
            chained = [0]

            def link(ins):
                chained[0] += 1
                ins.then_inc(sem["dve_chain"], 1)
                dve.wait_ge(sem["dve_chain"], chained[0])

            V.memset(epsv[:], EPS).then_inc(sem["epsv_ready"], 1)
            dve.wait_ge(sem["vec_loaded"], 16)
            raw = vec[:, VEC_LOWER:VEC_LOWER + 2 * DEPTH * HG_HEADS].rearrange("p (l d h) -> p l d h", l=DEPTH, d=2)
            link(V.tensor_tensor(lowtmp[:, 0], raw[:, 0], raw[:, 1], ALU.max))
            V.tensor_tensor(lowtmp[:, 1], raw[:, 0], lowtmp[:, 0], ALU.subtract)
            V.tensor_tensor(lowtmp[:, 2], raw[:, 1], lowtmp[:, 0], ALU.subtract).then_inc(sem["lower_ready"], 1)
            dve.wait_ge(sem["lower_ready"], 2)
            link(V.tensor_tensor(lowtmp[:, 3], lowtmp[:, 1], lowtmp[:, 2], ALU.add))
            link(V.reciprocal(lowtmp[:, 3], lowtmp[:, 3]))
            V.tensor_tensor(lowtmp[:, 4], lowtmp[:, 1], lowtmp[:, 3], ALU.mult)
            link(V.tensor_tensor(lowtmp[:, 5], lowtmp[:, 2], lowtmp[:, 3], ALU.mult))
            V.tensor_tensor(lower[:, :, 0], lowtmp[:, 4], lowtmp[:, 4], ALU.subtract)
            link(V.tensor_tensor(lowtmp[:, 6], lowtmp[:, 4], lowtmp[:, 5], ALU.add))
            link(V.tensor_tensor(lower[:, :, 1], lowtmp[:, 6], lowtmp[:, 4], ALU.subtract))
            link(V.tensor_scalar(upper[:], lower[:], -1.0, 1.0, ALU.mult, ALU.add))

            dve.wait_ge(sem["x_loaded"], 48)
            link(V.tensor_copy(levmask[:], levmask_f[:]))

            for n in range(DEPTH * 12):
                l, s = n // 12, n % 12
                dve.wait_ge(*is_ready(("adaT", l, s)))
                b = vec[:, VEC_BADA + 48 * l + 4 * s:VEC_BADA + 48 * l + 4 * s + 4].unsqueeze(2).to_broadcast([P, 4, 2])
                V.tensor_tensor(mod[:, l, 4 * s:4 * s + 4, :], result(("adaT", l, s))[:, 0:8]
                                .rearrange("p (j c) -> p j c", c=2), b, ALU.add).then_inc(sem["ada_mod"], 1)
            dve.wait_ge(sem["ada_mod"], DEPTH * 12)
            for l in range(DEPTH):
                for gain, at_scale, at_g in ((gain1, KT, VEC_N1), (gain2, 4 * KT, VEC_N2)):
                    g = vec[:, at_g + KT * l:at_g + KT * (l + 1)].unsqueeze(2).to_broadcast([P, KT, 2])
                    link(V.scalar_tensor_tensor(gain[:, l], mod[:, l, at_scale:at_scale + KT, :], 1.0, g,
                                                ALU.add, ALU.mult))

            def norm(count, lo, gain, shift):
                dve.wait_ge(sem["norm_std"], count + 1)
                link(V.reciprocal(rstd[:, lo:TOK], rstd[:, lo:TOK]))
                for k in range(KT):
                    V.tensor_tensor(normed[:, k % 2, lo:TOK], xT[:, k, lo:TOK], rstd[:, lo:TOK], ALU.mult)\
                     .then_inc(sem["normed_ready"], 1)
                    dve.wait_ge(sem["normed_ready"], KT * count + k + 1)
                    for sg in range(1 if lo else 0, 2):
                        a = slice(sg * SEG, (sg + 1) * SEG)
                        if shift is None:
                            op = V.tensor_scalar(hT[:, k, a], normed[:, k % 2, a], gain[:, k:k + 1], None, ALU.mult)
                        else:
                            op = V.tensor_scalar(hT[:, k, a], normed[:, k % 2, a], gain[:, k, 1 - sg:2 - sg],
                                                 shift[:, k, 1 - sg:2 - sg], ALU.mult, ALU.add)
                    op.then_inc(sem["h_ready"], 1)

            def add_scaled(key_bank, l, d, at_gate, lo):
                for sg in range(1 if lo else 0, 2):
                    a = slice(sg * SEG, (sg + 1) * SEG)
                    op = V.scalar_tensor_tensor(xT[:, d, a], key_bank[:, a], mod[:, l, at_gate + d, 1 - sg:2 - sg],
                                                xT[:, d, a], ALU.mult, ALU.add)
                return op

            for l in range(DEPTH):
                if stop <= 10 * l + 1:
                    break
                lo = 0 if l == 0 else SEG
                segs = segs_of[l]
                norm(2 * l, 0, gain1[:, l], mod[:, l, 0:KT, :])
                V.memset(onescan[:], 1.0)
                V.memset(pf[:, :, 0:1], 0.0)
                link(V.memset(pb[:, :, 0:1], 0.0))
                for way, (k_to, p_to) in enumerate(((kf, pf), (kb, pb))):
                    for h in range(HG_HEADS):
                        dve.wait_ge(sem["sig_ready"], 8 * l + 4 * way + h + 1)
                        dve.wait_ge(sem["k_sig"], 8 * l + 4 * way + h + 1)
                        up, low = upper[:, way, l, h:h + 1], lower[:, way, l, h:h + 1]
                        kh = k_to[:, 2 * h:2 * h + 2, :].rearrange("p s t -> p (s t)")
                        V.tensor_scalar(kh, kh, up, None, ALU.mult)
                        gh = sig[:, h * TOK:(h + 1) * TOK]
                        last = V.tensor_scalar(gh, gh, up, low, ALU.mult, ALU.add)
                    link(last)
                    V.tensor_scalar(small[:], sig[:], 2.0 ** -40, 2.0 ** 60, ALU.is_lt, ALU.mult)
                    link(V.tensor_scalar(sig[:], sig[:], GATE_FLOOR, None, ALU.max))
                    V.scalar_tensor_tensor(sig[:], small[:], 1.0, sig[:], ALU.add, ALU.mult).then_inc(sem["log_in"], 1)
                    dve.wait_ge(sem["log_out"], 2 * l + way + 1)
                    link(V.scalar_tensor_tensor(logs[:], small[:], -60.0 * float(np.log(2.0)) / 2.0 ** 60, logs[:],
                                                ALU.mult, ALU.add))
                    for hs in range(8):
                        last = V.tensor_tensor_scan(p_to[:, hs, 1:SEG + 1], onescan[:], logs[:, hs * SEG:(hs + 1) * SEG],
                                                    0.0, ALU.mult, ALU.add)
                    if way == 1:
                        last.then_inc(sem["sums_ready"], 1)
                    else:
                        link(last)
                if stop <= 10 * l + 2:
                    break

                def factors(hp, unit, u, d):
                    lev, way = (unit - 1) // 2, (unit - 1) % 2
                    if u - 2 in spent:
                        dve.wait_ge(sem["psum_ready"], spent[u - 2])
                    y = fac[u % 2]
                    r = rows(hp, l == 0)
                    na = 2 * len(segs)
                    if unit == 0:
                        V.tensor_tensor(y[:, 0:na, :], kf[:, r, :], kb[:, r, :], ALU.add).then_inc(sem["fac_ready"], 1)
                        return
                    dve.wait_ge(sem["decay_out"], d + 1)
                    k = (kf, kb)[way]
                    if lev <= LEVELS:
                        h = 1 << lev
                        e, to = halves(dec[d % 2][:, 0:na, :], h), halves(y[:, 0:na, :], h)
                        src = (halves(k[:, r, :], h)[way], halves(qh[:, r, :], h)[1 - way])
                        V.tensor_tensor(to[way], e[way], src[0], ALU.mult)
                        V.tensor_tensor(to[1 - way], e[1 - way], src[1], ALU.mult).then_inc(sem["fac_ready"], 1)
                    else:
                        x = dec[d % 2]
                        V.tensor_tensor(y[:, 0:4:2, :], x[:, 0:4:2, :], k[:, 4 * hp:4 * hp + 4:2, :], ALU.mult)
                        V.tensor_tensor(y[:, 1:4:2, :], x[:, 1:4:2, :], qh[:, 4 * hp + 1:4 * hp + 4:2, :], ALU.mult)\
                         .then_inc(sem["fac_ready"], 1)

                def diagonal(head):
                    x = att[:, head, segs[0], :, :]
                    dims = [x.ap[0]] + ([[2 * SEG, 2]] if l == 0 else []) + [[SEG + P, 2], [1, P]]
                    return bass.AP(x.tensor, x.offset, dims)

                def collect(hp, unit, u):
                    lev, way = (unit - 1) // 2, (unit - 1) % 2
                    if lev < LEVELS:
                        for h in range(2):
                            dve.wait_ge(*is_ready(("lev", l, u, h)))
                            got = result(("lev", l, u, h))[:, 0:2 * P * len(segs)]
                            if l == 0:
                                got = got.rearrange("p (s b t) -> p s b t", s=2, b=2)
                                shape = [P, 2, 2, P]
                            else:
                                got = got.rearrange("p (b t) -> p b t", b=2)
                                shape = [P, 2, P]
                            if unit == 0:
                                V.tensor_copy(diagonal(2 * hp + h), got).then_inc(sem["att_block"], 1)
                            else:
                                mask = levmask[:, way * LEVELS + lev, :]
                                for _ in range(len(shape) - 2):
                                    mask = mask.unsqueeze(1)
                                dve.wait_ge(*read_by(("lev", l, u - 1, h)))
                                V.copy_predicated(diagonal(2 * hp + h), mask.to_broadcast(shape), got)\
                                 .then_inc(sem["att_block"], 1)
                    elif lev == LEVELS:
                        dve.wait_ge(*is_ready(("lev", l, u, 0)))
                        got = result(("lev", l, u, 0))[:, 0:2 * P * len(segs)]
                        t0 = P * (1 - way)
                        if l == 0:
                            V.tensor_copy(att[:, 2 * hp:2 * hp + 2, :, way, t0:t0 + P],
                                          got.rearrange("p (h s t) -> p h s t", h=2, s=2)).then_inc(sem["att_block"], 1)
                        else:
                            V.tensor_copy(att[:, 2 * hp:2 * hp + 2, 1, way, t0:t0 + P],
                                          got.rearrange("p (h t) -> p h t", h=2)).then_inc(sem["att_block"], 1)
                    elif way == 1:
                        for h in range(2):
                            dve.wait_ge(*is_ready(("cross", l, hp, h)))
                            V.tensor_copy(attx[:, 2 * hp + h].rearrange("p b t -> p (b t)"),
                                          result(("cross", l, hp, h))[:, :]).then_inc(sem["att_block"], 1)

                units = [(hp, unit) for hp in range(2) for unit in range(19)]
                d_out = 36 * l
                for n in range(len(units) + 1):
                    if n < len(units):
                        factors(*units[n], 38 * l + n, d_out)
                        d_out += units[n][1] > 0
                    if n >= 1:
                        collect(*units[n - 1], 38 * l + n - 1)
                if stop <= 10 * l + 3:
                    break

                for n in range(8):
                    dve.wait_ge(*is_ready(("rot", l, n)))
                    if n:
                        dve.wait_ge(sem["rope_done"], 8 * l + n)
                    x = (naq, nak)[n // 4][:, n % 4, SEG:TOK]
                    V.tensor_tensor(roped[:, 0], x, cos, ALU.mult)
                    link(V.tensor_tensor(roped[:, 1], result(("rot", l, n))[:, 0:SEG], sin, ALU.mult))
                    V.tensor_tensor(x, roped[:, 0], roped[:, 1], ALU.add).then_inc(sem["rope_done"], 1)

                tiles = [(h, q) for h in range(NA_HEADS) for sg in segs for q in (2 * sg, 2 * sg + 1)]
                per = len(tiles)
                before = 0 if l == 0 else NA_HEADS * 4
                scale = NA_DIM ** -0.5
                for n in range(per + 5):
                    if n < per:
                        h, q = tiles[n]
                        x = probs[(before + n) % 3]
                        dve.wait_ge(*is_ready(("S", l, n)))
                        if n >= 3:
                            dve.wait_ge(*is_ready(("TR", l, n - 3)))
                        got = result(("S", l, n))
                        op = V.tensor_scalar(x[:, 0:SEG], got[:, 0:SEG], scale, None, ALU.mult)
                        if q >= 2:
                            dve.wait_ge(sem["bias_ready"], 8 * l + h + 1)
                            op = V.scalar_tensor_tensor(x[:, SEG:TOK], got[:, SEG:TOK], scale, bias[:, h, q - 2, :],
                                                        ALU.mult, ALU.add)
                        op.then_inc(sem["na_z"], 1)
                        dve.wait_ge(*read_by(("S", l, n)))
                        V.tensor_reduce(narow[:, (before + n) % 3, 0:1], x[:, 0:SEG if q < 2 else TOK], AX.X, ALU.max,
                                        negate=True).then_inc(sem["na_max"], 1)
                    m = n - 1
                    if 0 <= m < per:
                        h, q = tiles[m]
                        nk = SEG if q < 2 else TOK
                        i = (before + m) % 3
                        dve.wait_ge(sem["na_p"], before + m + 1)
                        link(V.reciprocal(narow[:, i, 2:3], narow[:, i, 1:2]))
                        V.tensor_scalar(probs[i][:, 0:nk], probs[i][:, 0:nk], narow[:, i, 2:3], None, ALU.mult)\
                         .then_inc(sem["na_pn"], 1)
                    m = n - 5
                    if m >= 0 and m % 2 == 1:
                        h, q = tiles[m]
                        r = 64 * (h % 2)
                        sg = q // 2
                        dve.wait_ge(*is_ready(("PV", l, m // 2)))
                        V.tensor_copy(ona[r:r + 64, h // 2, sg * SEG:(sg + 1) * SEG],
                                      result(("PV", l, m // 2))[r:r + 64, 0:SEG]).then_inc(sem["na_o"], 1)
                if stop <= 10 * l + 4:
                    break

                for h in range(HG_HEADS):
                    dve.wait_ge(sem["hg_std"], 4 * l + h + 1)
                    dve.wait_ge(sem["hgate_ready"], 4 * l + h + 1)
                    x, y = oh[:, h, lo:TOK], ors[:, h % 2, lo:TOK]
                    link(V.reciprocal(y, y))
                    link(V.tensor_tensor(x, x, y, ALU.mult))
                    V.scalar_tensor_tensor(x, x, vec[:, VEC_HGAIN + l:VEC_HGAIN + l + 1], hgate[:, h, lo:TOK],
                                           ALU.mult, ALU.mult).then_inc(sem["og_ready"], 1)

                for n in range(16):
                    br, d = n // 8, n % 8
                    dve.wait_ge(sem["gate_sig"], 16 * l + n + 1)
                    dve.wait_ge(*is_ready(("y", l, br, d)))
                    got, gate, to = result(("y", l, br, d))[:, lo:TOK], gsig[:, n % 2, lo:TOK], merged[:, d, lo:TOK]
                    if br == 0:
                        V.tensor_tensor(to, gate, got, ALU.mult).then_inc(sem["merged_ready"], 1)
                    else:
                        link(V.tensor_tensor(gmul[:, n % 2, lo:TOK], gate, got, ALU.mult))
                        V.tensor_tensor(to, to, gmul[:, n % 2, lo:TOK], ALU.add).then_inc(sem["merged_ready"], 1)
                for d in range(KT):
                    dve.wait_ge(*is_ready(("out", l, d)))
                    add_scaled(result(("out", l, d)), l, d, 2 * KT, lo).then_inc(sem["x_updated"], 1)
                if stop <= 10 * l + 5:
                    break
                norm(2 * l + 1, lo, gain2[:, l], mod[:, l, 3 * KT:4 * KT, :])

                t0 = 2 * l
                nt = 4 - t0
                shape = [P, 4 * nt, PER_GROUP]
                idx = vec[:, VEC_GIDX:VEC_GIDX + 4].unsqueeze(1)
                flat = [x[:, t0:4].rearrange("p t g e -> p (t g) e") for x in rt]
                scores, biased, eq, cand, oh1, oh2, sel, m1, m2, mn, gs, ing = flat

                def first_max(x, hot, mx, n):
                    shape = [P, n, 4]
                    link(V.tensor_reduce(mx, x, AX.X, ALU.max))
                    link(V.tensor_tensor(eq[:, 0:n, :], x, mx.to_broadcast(shape), ALU.is_equal))
                    link(V.scalar_tensor_tensor(cand[:, 0:n, :], eq[:, 0:n, :], -8.0, idx.to_broadcast(shape),
                                                ALU.mult, ALU.add))
                    link(V.tensor_reduce(mn[:, 0:n, 0:1], cand[:, 0:n, :], AX.X, ALU.min))
                    link(V.tensor_tensor(hot, cand[:, 0:n, :], mn[:, 0:n, 0:1].to_broadcast(shape), ALU.is_equal))

                dve.wait_ge(*is_ready(("scores", l)))
                V.tensor_copy(rt[0][:, t0:4].rearrange("p t g e -> p (t g e)"),
                              result(("scores", l))[:, t0 * N_EXPERTS:4 * N_EXPERTS]).then_inc(sem["scores_ready"], 1)
                dve.wait_ge(sem["scores_ready"], l + 1)
                rb = vec[:, VEC_RBIAS:VEC_RBIAS + N_EXPERTS].unsqueeze(1).to_broadcast([P, nt, N_EXPERTS])
                link(V.tensor_tensor(biased.rearrange("p (t g) e -> p t (g e)", g=4),
                                     scores.rearrange("p (t g) e -> p t (g e)", g=4), rb, ALU.add))
                first_max(biased, oh1, m1[:, :, 0:1], 4 * nt)
                link(V.scalar_tensor_tensor(biased, oh1, -1e9, biased, ALU.mult, ALU.add))
                first_max(biased, oh2, m2[:, :, 0:1], 4 * nt)
                g4 = gs[:, 0:nt, :]
                link(V.tensor_tensor(g4, m1[:, :, 0].rearrange("p (t g) -> p t g", g=4),
                                     m2[:, :, 0].rearrange("p (t g) -> p t g", g=4), ALU.add))
                first_max(g4, ing[:, 0:nt, :], m1[:, 0:nt, 1:2], nt)
                link(V.tensor_tensor(sel, oh1, oh2, ALU.add))
                link(V.tensor_tensor(sel, sel, ing[:, 0:nt, :].rearrange("p t g -> p (t g)").unsqueeze(2)
                                     .to_broadcast(shape), ALU.mult))
                hot = chosen[:, t0:4].rearrange("p t (g e) -> p (t g) e", e=PER_GROUP)
                V.tensor_copy(hot, sel).then_inc(sem["chosen_ready"], 1)
                link(V.tensor_tensor(sel, sel, scores, ALU.mult))
                wide = [P, nt, N_EXPERTS]
                by_token = sel.rearrange("p (t g) e -> p t (g e)", g=4)
                link(V.tensor_reduce(m2[:, 0:nt, 1:2], by_token, AX.X, ALU.add))
                link(V.reciprocal(m2[:, 0:nt, 2:3], m2[:, 0:nt, 1:2]))
                link(V.tensor_tensor(weight[:, t0:4, 0:N_EXPERTS], by_token, m2[:, 0:nt, 2:3].to_broadcast(wide), ALU.mult))
                for t in range(t0, 4):
                    for half in range(2):
                        dve.wait_ge(sem["hrow_hi_ready"], 8 * l + 2 * (t - t0) + half + 1)
                        a = slice(half * 512, (half + 1) * 512)
                        V.tensor_tensor(hrow_lo[:, t, a], result(("rows", l, t, half))[:, :], hrow_hi[:, t, a].bitcast(f32),
                                        ALU.subtract).then_inc(sem["hrow_ready"], 1)
                dve.wait_ge(*is_ready(("place", l)))
                pl = place[:, t0:4, 0:N_EXPERTS]
                link(V.scalar_tensor_tensor(pl, result(("place", l))[:, t0 * N_EXPERTS:4 * N_EXPERTS]
                                            .rearrange("p (t e) -> p t e", e=N_EXPERTS), 1.0, chosen[:, t0:4, :],
                                            ALU.add, ALU.mult))
                V.tensor_scalar(pl, pl, -1.0, None, ALU.add).then_inc(sem["place_ready"], 1)
                dve.wait_ge(sem["place_ready"], l + 1)

                link(V.tensor_reduce(crowd[:], result(("place", l))[:, 4 * N_EXPERTS:5 * N_EXPERTS], AX.X, ALU.max))
                V.tensor_copy(crowd_int[:], crowd[:]).then_inc(sem["crowd_ready"], 1)
                dve.wait_ge(sem["crowd_ready"], l + 1)

                def experts(ph):
                    base = slot_of(("moe", ph, 0, 0))

                    def make_pick(i, e):
                        dve.wait_ge(*total(ph, i, "pickw_turned", e - 2, 1))
                        at_e = phases[ph][0] + e if i is None else i * 4 + (phases[ph][0] + e)
                        wide = [P, nt, P]
                        hot = pick[:, e % 2, t0:4, :]
                        V.tensor_tensor(hot, iota.unsqueeze(1).to_broadcast(wide),
                                        place[:, t0:4, at_e].unsqueeze(2).to_broadcast(wide), ALU.is_equal)\
                         .then_inc(sem["pick_bare"], 1)
                        dve.wait_ge(*total(ph, i, "pick_bare", e, 1))
                        V.tensor_tensor(pickw[:, e % 2, t0:4, :], hot.bitcast(f32),
                                        weight[:, t0:4, at_e].unsqueeze(2).to_broadcast(wide), ALU.mult)\
                         .then_inc(sem["pick_ready"], 1)

                    def keep_picked(i, e):
                        for half in range(2):
                            a = slice(4 * half, 4 * half + 4)
                            dve.wait_ge(*total(ph, i, "picked_hi_ready", e, half + 1))
                            V.tensor_tensor(picked_lo[:, a, :].rearrange("p k c -> p (k c)"), bank[2 + half][:, :],
                                            picked_hi[:, a, :].rearrange("p k c -> p (k c)").bitcast(f32),
                                            ALU.subtract).then_inc(sem["picked_lo_ready"], 1)

                    def split_low(i, e, g):
                        s = (base + 3 * e + g) % SLOTS
                        a = slice(gpsimd_part[g], SLOT)
                        dve.wait_ge(*total(ph, i, "w_hi_ready", e, g + 1))
                        V.tensor_tensor(ring_lo[:, s, a], ring[:, s, a], w_hi[(3 * e + g) % 2][:, a].bitcast(f32),
                                        ALU.subtract).then_inc(sem["own_lo_ready"], 1)

                    def expert(i, e, last):
                        if not last:
                            make_pick(i, e + 1)
                        dve.wait_ge(*total(ph, i, "slot_weight_ready", e, 1))
                        dve.wait_ge(*total(ph, i, "scattered", e - 4 - e % 2, 8))
                        V.tensor_scalar(spread[:, e % 4, lo:TOK], bank[4][:, lo:TOK], 0.0, None, ALU.not_equal)\
                         .then_inc(sem["spread_ready"], 1)
                        dve.wait_ge(*total(ph, i, "silu_ready", e, 1))
                        dve.wait_ge(*total(ph, i, "up_done", e, 1))
                        dve.wait_ge(*total(ph, i, "act_turned", e - 1, 1))
                        V.scalar_tensor_tensor(acts[:], bank[1][:, :], slot_weight[:, e % 2:e % 2 + 1], silu[:],
                                               ALU.mult, ALU.mult).then_inc(sem["act_ready"], 1)
                        split_low(i, e, 2)
                        dve.wait_ge(*total(ph, i, "acts_hi_ready", e, 1))
                        V.tensor_tensor(acts_lo[:].rearrange("p k c -> p (k c)"), bank[5][:, :],
                                        acts_hi[:].rearrange("p k c -> p (k c)").bitcast(f32),
                                        ALU.subtract).then_inc(sem["acts_lo_ready"], 1)
                        if not last:
                            split_low(i, e + 1, 0)
                            keep_picked(i, e + 1)
                        for half in range(2):
                            a = slice(half * 512, (half + 1) * 512)
                            dve.wait_ge(*total(ph, i, "y_hi_ready", e, half + 1))
                            V.tensor_tensor(y_lo[:, e % 2, a], bank[6 + half][:, :], y_hi[:, e % 2, a].bitcast(f32),
                                            ALU.subtract).then_inc(sem["y_lo_ready"], 1)
                        for d in range(KT if e % 2 else 0):
                            dve.wait_ge(*total(ph, i, "scattered", e - 1, d + 1))
                            dve.wait_ge(*total(ph, i, "x_added", e - 3, d + 1))
                            add_scaled(bank[scatter_bank[d]], l, d, 5 * KT, lo).then_inc(sem["x_added"], 1)
                        if not last:
                            split_low(i, e + 1, 1)

                    open_phase(dve, "dve")
                    make_pick(None, 0)
                    split_low(None, 0, 0)
                    keep_picked(None, 0)
                    split_low(None, 0, 1)
                    by_fours(dve, ph, expert)

                experts(2 * l)
                close_phase(dve, "dve", 2 * l)
                crowded = dve.value_load(crowd_int[0:1, 0:1])
                with dve.If(crowded > CAPACITY):
                    count = phases[2 * l + 1][1]
                    for r in range(count // N_EXPERTS):
                        a = slice(over_at + r * N_EXPERTS, over_at + (r + 1) * N_EXPERTS)
                        V.tensor_scalar(place[:, t0:4, a], pl, -float(CAPACITY * (r + 1)), None, ALU.add)
                        op = V.tensor_copy(weight[:, t0:4, a], weight[:, t0:4, 0:N_EXPERTS])
                    op.then_inc(sem["over_ready"], 1)
                    dve.wait_ge(sem["over_ready"], l + 1)
                    experts(2 * l + 1)
                with dve.Else():
                    skip_phase(dve, "dve", 2 * l + 1)
                    dve.sem_inc(sem["over_ready"], 1)
            if stop > 30:
                norm(4, SEG, vec[:, VEC_FINAL:VEC_FINAL + KT], None)


def constants():
    c = np.zeros((P, C_N), np.float32)
    c[:, C_IDENT:C_IDENT + P] = np.eye(P)
    c[:, C_ONES:C_ONES + P] = 1.0
    for i in range(0, P, 2):
        c[i + 1, C_ROT + i] = -1.0
        c[i, C_ROT + i + 1] = 1.0
    t = np.arange(SEG)
    row, col = (t // GRID_W).astype(np.float32), (t % GRID_W).astype(np.float32)
    inv = np.float32(10000.0) ** (-np.arange(0, 32, 2, dtype=np.float32) / np.float32(32))
    ang = np.concatenate([row[:, None] * inv, col[:, None] * inv], axis=-1)
    c[:, C_COS:C_COS + SEG] = np.repeat(np.tile(np.cos(ang).T, (2, 1)), 2, axis=0)
    c[:, C_SIN:C_SIN + SEG] = np.repeat(np.tile(np.sin(ang).T, (2, 1)), 2, axis=0)
    col = np.arange(P)[:, None] % GRID_W
    kc = np.arange(GRID_W)[None, :]
    start = np.clip(col - WIN_COLS // 2, 0, GRID_W - WIN_COLS)
    inside = (kc >= start) & (kc < start + WIN_COLS)
    c[:, C_IOTA:C_IOTA + P] = np.where(np.arange(P) < CAPACITY, np.arange(P), -P * P)
    c[:, C_BEFORE:C_BEFORE + P] = np.triu(np.ones((P, P)), 1)
    c[:, C_WMUL:C_WMUL + GRID_W] = inside
    c[:, C_WNEG:C_WNEG + GRID_W] = np.where(inside, 0.0, MASKED)
    m = np.zeros((P, 2 * LEVELS, P), np.float32)
    s, t = np.arange(P)[:, None], np.arange(P)[None, :]
    for lev in range(LEVELS):
        h = 1 << lev
        same = s // (2 * h) == t // (2 * h)
        m[:, lev] = same & (s % (2 * h) < h) & (t % (2 * h) >= h)
        m[:, LEVELS + lev] = same & (s % (2 * h) >= h) & (t % (2 * h) < h)
    return c, m


def kernel(**inputs):
    import numpy as _np
    import concourse.bacc as _bacc
    from concourse import mybir as _mybir
    from concourse.bass_utils import run_bass_kernel_spmd as _run

    a = {k: _np.asarray(v) for k, v in inputs.items()}

    def cols(x):
        x = x.reshape(*x.shape[:-1], -1, P)
        return _np.moveaxis(x, -1, 0).reshape(P, -1)

    lower = _np.stack([a["hg_lower_fwd"], a["hg_lower_bwd"]], axis=1)
    cond = _np.stack([a["c"][0], a["c_ctx"]], axis=0)
    vec = _np.concatenate([
        cols(a["b_ada"]), cols(a["norm1_g"]), cols(a["norm2_g"]), cols(a["final_g"]), cols(lower),
        _np.ascontiguousarray(a["hg_norm_g"].T),
        _np.moveaxis(cond.reshape(2, KT, P), 2, 0).transpose(0, 2, 1).reshape(P, 2 * KT),
        _np.broadcast_to(a["router_bias"], (P, N_EXPERTS)),
        _np.broadcast_to(_np.arange(4, dtype=_np.float32), (P, 4)),
    ], axis=1)
    assert vec.shape == (P, VEC_N), vec.shape
    const, levmask = constants()
    arrays = {
        "xT": _np.concatenate([a["ctx"][0], a["x"][0]], axis=0).T, "vec": vec, "const": const, "levmask": levmask,
        "rel_bias_reversed": a["na_rel_bias"][..., ::-1],
    }
    for n in ("w_ada", "w_in", "w_na_o", "w_hg_o", "w_out", "w_router", "w_gate", "w_up", "w_down"):
        arrays[n] = a[n]
    arrays = {n: _np.ascontiguousarray(x) for n, x in arrays.items()}
    nc = _bacc.Bacc("TRN2", target_bir_lowering=False, num_devices=1, dynamic_dma_scratch_size=1024)
    aps = {n: nc.dram_tensor(f"in_{n}", x.shape, _mybir.dt.from_np(x.dtype), kind="ExternalInput").ap()
           for n, x in arrays.items()}
    out = nc.dram_tensor("out_yT", (D, SEG), _mybir.dt.float32, kind="ExternalOutput").ap()
    build(nc, aps, out)
    r = _run(nc, [{f"in_{n}": x for n, x in arrays.items()}], core_ids=[0])
    return r.results[0]["out_yT"].T[None]
```
